# Optimizing a Trainium2 kernel written in Bass

```python
import math
import jax, jax.numpy as jnp
from jax import lax
import numpy as np

D_MODEL = 1024
BATCH = 1
SEQ = 512
DEPTH = 1

GRID_W = 64
CTX_LEN = 256
MLA_HEADS = 8
QK_NOPE = 64
QK_ROPE = 32
QK_DIM = QK_NOPE + QK_ROPE
V_DIM = 64
Q_LORA = 384
KV_LORA = 256
ROPE_THETA = 10000.0
Q_BLOCK = 128
F_GROUPS = 4
F_GROUP_DIM = 128
D_F = F_GROUPS * F_GROUP_DIM
OFF_Q = 0
OFF_KV = OFF_Q + Q_LORA
OFF_KPE = OFF_KV + KV_LORA
OFF_F = OFF_KPE + QK_ROPE
OFF_GA = OFF_F + D_F
OFF_GB = OFF_GA + D_MODEL
N_IN = OFF_GB + D_MODEL
N_EXPERTS = 16
D_EXPERT = 512
CAPACITY_FACTOR = 2
EPS = 1e-6


def _rms(x, g):
    xf = x.astype(jnp.float32)
    y = xf * lax.rsqrt(jnp.mean(xf * xf, axis=-1, keepdims=True) + EPS)
    return (y * g.astype(jnp.float32)).astype(x.dtype)

def _modulate(h, shift, scale):
    return h * (1.0 + scale) + shift

def _axial_tables(pos_row, pos_col, dtype):
    half = QK_ROPE // 2
    n_freq = half // 2
    inv_freq = 1.0 / (ROPE_THETA ** (jnp.arange(n_freq, dtype=jnp.float32) / n_freq))

    def tab(pos):
        ang = pos.astype(jnp.float32)[:, None] * inv_freq[None, :]
        ang = jnp.concatenate([ang, ang], axis=-1)[None, :, None, :]
        return jnp.cos(ang).astype(dtype), jnp.sin(ang).astype(dtype)

    cr, sr = tab(pos_row)
    cc, scol = tab(pos_col)
    return cr, sr, cc, scol

def _rope_axis(x, cos, sin):
    x1, x2 = jnp.split(x, 2, axis=-1)
    return x * cos + jnp.concatenate([-x2, x1], axis=-1) * sin

def _rope_2d(x, tabs):
    cr, sr, cc, scol = tabs
    xr, xc = jnp.split(x, 2, axis=-1)
    return jnp.concatenate([_rope_axis(xr, cr, sr), _rope_axis(xc, cc, scol)], axis=-1)

def _mla_qkv(p, q_a_g, kv_a_g, w_q_up, w_kv_up, q_g, k_g, tabs):
    B, T, _ = p.shape
    cq = _rms(p[..., OFF_Q:OFF_KV], q_a_g)
    ckv = _rms(p[..., OFF_KV:OFF_KPE], kv_a_g)
    k_pe = p[..., OFF_KPE:OFF_F]
    q = (cq @ w_q_up).reshape(B, T, MLA_HEADS, QK_DIM)
    kv = (ckv @ w_kv_up).reshape(B, T, MLA_HEADS, QK_NOPE + V_DIM)
    k_nope, v = kv[..., :QK_NOPE], kv[..., QK_NOPE:]
    k = jnp.concatenate([k_nope, jnp.broadcast_to(k_pe[:, :, None, :], (B, T, MLA_HEADS, QK_ROPE))], axis=-1)
    q = _rms(q, q_g)
    k = _rms(k, k_g)
    if tabs is not None:
        q = jnp.concatenate([q[..., :QK_NOPE], _rope_2d(q[..., QK_NOPE:], tabs)], axis=-1)
        k = jnp.concatenate([k[..., :QK_NOPE], _rope_2d(k[..., QK_NOPE:], tabs)], axis=-1)
    return q, k, v

def _attend_dense(q, k, v):
    s = jnp.einsum('bqhd,bkhd->bhqk', q, k, preferred_element_type=jnp.float32) * (QK_DIM ** -0.5)
    pr = jax.nn.softmax(s, axis=-1).astype(v.dtype)
    return jnp.einsum('bhqk,bkhd->bqhd', pr, v)

def _attend_latent(q, k_lat, v_lat, k_ctx, v_ctx):
    B, T, H, _ = q.shape
    k_all = jnp.concatenate([k_lat, k_ctx], axis=1)
    v_all = jnp.concatenate([v_lat, v_ctx], axis=1)
    nb = T // Q_BLOCK
    qb = jnp.moveaxis(q.reshape(B, nb, Q_BLOCK, H, QK_DIM), 1, 0)
    o = lax.map(lambda qi: _attend_dense(qi, k_all, v_all), qb)
    return jnp.moveaxis(o, 0, 1).reshape(B, T, H * V_DIM)

def _fourier(f):
    B, T, _ = f.shape
    fg = f.reshape(B, T, F_GROUPS, F_GROUP_DIM).astype(jnp.float32)
    y = jnp.fft.fft2(fg, axes=(1, 3), norm="ortho").real
    return y.reshape(B, T, D_F).astype(f.dtype)

def _expert_choice(h, w_r, w_g, w_u, w_d):
    B, T, D = h.shape
    cap = (CAPACITY_FACTOR * T) // N_EXPERTS
    logits = jnp.einsum('btd,de->bte', h, w_r, preferred_element_type=jnp.float32)
    aff = jax.nn.softmax(logits, axis=-1)
    gate, idx = lax.top_k(jnp.swapaxes(aff, 1, 2), cap)
    xe = jax.vmap(lambda hb, ib: hb[ib])(h, idx)
    a = jnp.einsum('becd,edf->becf', xe, w_g)
    u = jnp.einsum('becd,edf->becf', xe, w_u)
    ye = jnp.einsum('becf,efd->becd', jax.nn.silu(a) * u, w_d) * gate[..., None].astype(h.dtype)
    return jax.vmap(lambda yb, ib: jnp.zeros((T, D), yb.dtype).at[ib.reshape(-1)].add(yb.reshape(-1, D)))(ye, idx)

def _merge(p, attn_o, four_o, w_o_attn, w_fourier, w_out):
    ga = jax.nn.sigmoid(p[..., OFF_GA:OFF_GB])
    gb = jax.nn.sigmoid(p[..., OFF_GB:N_IN])
    return (ga * (attn_o @ w_o_attn) + gb * (four_o @ w_fourier)) @ w_out

def first_inputs(seed: int = 0) -> dict:
    key = jax.random.key(seed)
    ks = jax.random.split(key, 24)
    L, D = DEPTH, D_MODEL

    def nrm(k, shape, fan_in, mult=1.0):
        return jax.random.normal(k, shape, jnp.float32) * (mult * fan_in ** -0.5)

    def gain(k, shape):
        return 1.0 + 0.02 * jax.random.normal(k, shape, jnp.float32)

    return {
        "x": jax.random.normal(ks[0], (BATCH, SEQ, D), jnp.float32),
        "c": jax.random.normal(ks[1], (BATCH, D), jnp.float32),
        "ctx": jax.random.normal(ks[2], (BATCH, CTX_LEN, D), jnp.float32),
        "c_ctx": 0.5 * jax.random.normal(ks[3], (D,), jnp.float32),
        "w_mod": nrm(ks[4], (L, D, 6 * D), D, 0.5),
        "b_mod": 0.02 * jax.random.normal(ks[5], (L, 6 * D), jnp.float32),
        "norm1_g": gain(ks[6], (L, D)),
        "w_in": nrm(ks[7], (L, D, N_IN), D),
        "q_a_norm_g": gain(ks[8], (L, Q_LORA)),
        "kv_a_norm_g": gain(ks[9], (L, KV_LORA)),
        "w_q_up": nrm(ks[10], (L, Q_LORA, MLA_HEADS * QK_DIM), Q_LORA),
        "w_kv_up": nrm(ks[11], (L, KV_LORA, MLA_HEADS * (QK_NOPE + V_DIM)), KV_LORA),
        "q_norm_g": gain(ks[12], (L, QK_DIM)),
        "k_norm_g": gain(ks[13], (L, QK_DIM)),
        "w_o_attn": nrm(ks[14], (L, MLA_HEADS * V_DIM, D), MLA_HEADS * V_DIM),
        "w_fourier": nrm(ks[15], (L, D_F, D), D_F),
        "w_out": nrm(ks[16], (L, D, D), D),
        "norm2_g": gain(ks[17], (L, D)),
        "w_router": nrm(ks[18], (L, D, N_EXPERTS), D),
        "w_e_gate": nrm(ks[19], (L, N_EXPERTS, D, D_EXPERT), D),
        "w_e_up": nrm(ks[20], (L, N_EXPERTS, D, D_EXPERT), D),
        "w_e_down": nrm(ks[21], (L, N_EXPERTS, D_EXPERT, D), D_EXPERT),
    }

def first_block(x, c, ctx, c_ctx, w_mod, b_mod, norm1_g, w_in, q_a_norm_g, kv_a_norm_g,
              w_q_up, w_kv_up, q_norm_g, k_norm_g, w_o_attn, w_fourier, w_out, norm2_g,
              w_router, w_e_gate, w_e_up, w_e_down):
    T = x.shape[1]
    rows = T // GRID_W
    pos_row = jnp.repeat(jnp.arange(rows, dtype=jnp.int32), GRID_W)
    pos_col = jnp.tile(jnp.arange(GRID_W, dtype=jnp.int32), rows)
    tabs = _axial_tables(pos_row, pos_col, x.dtype)
    s_lat = jax.nn.silu(c)
    s_ctx = jax.nn.silu(c_ctx)

    for l in range(DEPTH):
        last = l == DEPTH - 1
        mod_l = (s_lat @ w_mod[l] + b_mod[l])[:, None, :]
        mod_c = s_ctx @ w_mod[l] + b_mod[l]
        sh1, sc1, g1, sh2, sc2, g2 = jnp.split(mod_l, 6, axis=-1)
        csh1, csc1, cg1, csh2, csc2, cg2 = jnp.split(mod_c, 6, axis=-1)

        h = _modulate(_rms(x, norm1_g[l]), sh1, sc1)
        hc = _modulate(_rms(ctx, norm1_g[l]), csh1, csc1)
        p = h @ w_in[l]
        pc = hc @ w_in[l]
        mla_w = (q_a_norm_g[l], kv_a_norm_g[l], w_q_up[l], w_kv_up[l], q_norm_g[l], k_norm_g[l])
        q, k, v = _mla_qkv(p, *mla_w, tabs)
        qc, kc, vc = _mla_qkv(pc, *mla_w, None)
        attn_lat = _attend_latent(q, k, v, kc, vc)
        four_lat = _fourier(p[..., OFF_F:OFF_GA])
        x = x + g1 * _merge(p, attn_lat, four_lat, w_o_attn[l], w_fourier[l], w_out[l])

        if not last:
            B = ctx.shape[0]
            attn_ctx = _attend_dense(qc, kc, vc).reshape(B, CTX_LEN, MLA_HEADS * V_DIM)
            four_ctx = _fourier(pc[..., OFF_F:OFF_GA])
            ctx = ctx + cg1 * _merge(pc, attn_ctx, four_ctx, w_o_attn[l], w_fourier[l], w_out[l])

        moe_w = (w_router[l], w_e_gate[l], w_e_up[l], w_e_down[l])
        h2 = _modulate(_rms(x, norm2_g[l]), sh2, sc2)
        x = x + g2 * _expert_choice(h2, *moe_w)
        if not last:
            hc2 = _modulate(_rms(ctx, norm2_g[l]), csh2, csc2)
            ctx = ctx + cg2 * _expert_choice(hc2, *moe_w)
    return x


LRU_HEADS = 16
LRU_HEAD_DIM = 64
D_LRU = LRU_HEADS * LRU_HEAD_DIM
SC_GROUPS = 8
SC_GROUP_DIM = 64
D_SC = SC_GROUPS * SC_GROUP_DIM
D_MIX = D_LRU + D_SC
D_IN = 2 * D_LRU + 3 * D_SC
LRU_CONV_WIDTH = 4
SC_CONV_WIDTH = 3
RG_C = 8.0
D_FF = 3 * D_MODEL
FFN_CONV_WIDTH = 3


def rms_norm(x, g):
    xf = x.astype(jnp.float32)
    y = xf * lax.rsqrt(jnp.mean(xf * xf, axis=-1, keepdims=True) + EPS)
    return (y * g.astype(jnp.float32)).astype(x.dtype)

def causal_dwconv(x, w):
    k_width = w.shape[0]
    s = x.shape[1]
    xp = jnp.pad(x, ((0, 0), (k_width - 1, 0), (0, 0)))
    y = xp[:, 0:s] * w[0]
    for k in range(1, k_width):
        y = y + xp[:, k:k + s] * w[k]
    return y

def rg_lru(x, wa, ba, wx, bx, lam):
    bsz, s, c = x.shape
    xh = x.reshape(bsz, s, LRU_HEADS, LRU_HEAD_DIM)
    r = jax.nn.sigmoid(jnp.einsum('bshi,hij->bshj', xh, wa).reshape(bsz, s, c) + ba)
    i = jax.nn.sigmoid(jnp.einsum('bshi,hij->bshj', xh, wx).reshape(bsz, s, c) + bx)
    log_a = -RG_C * r.astype(jnp.float32) * jax.nn.softplus(-lam.astype(jnp.float32))
    a = jnp.exp(log_a)
    mult = jnp.sqrt(-jnp.expm1(2.0 * log_a))
    b = mult * (i * x).astype(jnp.float32)

    def combine(left, right):
        a1, b1 = left
        a2, b2 = right
        return a1 * a2, a2 * b1 + b2

    _, h = lax.associative_scan(combine, (a, b), axis=1)
    return h.astype(x.dtype)

def second_inputs(seed: int = 0) -> dict:
    key = jax.random.key(seed)
    ks = jax.random.split(key, 20)
    f32 = jnp.float32
    res_scale = (2.0 * DEPTH) ** -0.5
    x = jax.random.normal(ks[0], (BATCH, SEQ, D_MODEL), f32)
    norm1_g = 1.0 + 0.02 * jax.random.normal(ks[1], (DEPTH, D_MODEL), f32)
    w_in = jax.random.normal(ks[2], (DEPTH, D_MODEL, D_IN), f32) * D_MODEL ** -0.5
    lru_conv_w = jax.random.normal(ks[3], (DEPTH, LRU_CONV_WIDTH, D_LRU), f32) * LRU_CONV_WIDTH ** -0.5
    lru_conv_b = 0.02 * jax.random.normal(ks[4], (DEPTH, D_LRU), f32)
    lru_wa = jax.random.normal(ks[5], (DEPTH, LRU_HEADS, LRU_HEAD_DIM, LRU_HEAD_DIM), f32) * LRU_HEAD_DIM ** -0.5
    lru_ba = 0.02 * jax.random.normal(ks[6], (DEPTH, D_LRU), f32)
    lru_wx = jax.random.normal(ks[7], (DEPTH, LRU_HEADS, LRU_HEAD_DIM, LRU_HEAD_DIM), f32) * LRU_HEAD_DIM ** -0.5
    lru_bx = 0.02 * jax.random.normal(ks[8], (DEPTH, D_LRU), f32)
    u = jax.random.uniform(ks[9], (DEPTH, D_LRU), f32, minval=0.9, maxval=0.999)
    a0 = u ** (1.0 / RG_C)
    lru_lambda = jnp.log(a0) - jnp.log1p(-a0)
    sc_conv_w = jax.random.normal(ks[10], (DEPTH, SC_CONV_WIDTH, D_SC), f32) * SC_CONV_WIDTH ** -0.5
    w_out = jax.random.normal(ks[11], (DEPTH, D_MIX, D_MODEL), f32) * D_MIX ** -0.5 * res_scale
    norm2_g = 1.0 + 0.02 * jax.random.normal(ks[12], (DEPTH, D_MODEL), f32)
    w_up = jax.random.normal(ks[13], (DEPTH, D_MODEL, 2 * D_FF), f32) * D_MODEL ** -0.5
    ffn_conv_w = jax.random.normal(ks[14], (DEPTH, FFN_CONV_WIDTH, 2 * D_FF), f32) * FFN_CONV_WIDTH ** -0.5
    w_down = jax.random.normal(ks[15], (DEPTH, D_FF, D_MODEL), f32) * D_FF ** -0.5 * res_scale
    final_g = 1.0 + 0.02 * jax.random.normal(ks[16], (D_MODEL,), f32)
    return {"x": x, "norm1_g": norm1_g, "w_in": w_in, "lru_conv_w": lru_conv_w,
            "lru_conv_b": lru_conv_b, "lru_wa": lru_wa, "lru_ba": lru_ba, "lru_wx": lru_wx,
            "lru_bx": lru_bx, "lru_lambda": lru_lambda, "sc_conv_w": sc_conv_w, "w_out": w_out,
            "norm2_g": norm2_g, "w_up": w_up, "ffn_conv_w": ffn_conv_w, "w_down": w_down,
            "final_g": final_g}

def second_block(x, norm1_g, w_in, lru_conv_w, lru_conv_b, lru_wa, lru_ba, lru_wx, lru_bx,
              lru_lambda, sc_conv_w, w_out, norm2_g, w_up, ffn_conv_w, w_down, final_g):
    splits = [D_LRU, 2 * D_LRU, 2 * D_LRU + D_SC, 2 * D_LRU + 2 * D_SC]
    for l in range(DEPTH):
        h = rms_norm(x, norm1_g[l])
        z = jnp.einsum('bsd,de->bse', h, w_in[l])
        lru_x, lru_gate, sc_b, sc_c, sc_x = jnp.split(z, splits, axis=-1)
        lru_x = causal_dwconv(lru_x, lru_conv_w[l]) + lru_conv_b[l]
        y_lru = rg_lru(lru_x, lru_wa[l], lru_ba[l], lru_wx[l], lru_bx[l], lru_lambda[l]) \
            * jax.nn.gelu(lru_gate)
        y_sc = sc_b * causal_dwconv(sc_c * sc_x, sc_conv_w[l])
        y_mix = jnp.concatenate([y_lru, y_sc], axis=-1)
        x = x + jnp.einsum('bse,ed->bsd', y_mix, w_out[l])
        h = rms_norm(x, norm2_g[l])
        u = causal_dwconv(jnp.einsum('bsd,df->bsf', h, w_up[l]), ffn_conv_w[l])
        gate, up = jnp.split(u, 2, axis=-1)
        x = x + jnp.einsum('bsf,fd->bsd', jax.nn.gelu(gate) * up, w_down[l])
    return rms_norm(x, final_g)


def setup_inputs(seed=0):
    out = dict(first_inputs(seed))
    for name, value in second_inputs(seed + 1).items():
        if name != "x":
            out[name + "_2"] = value
    return out


def reference(
    x, c, ctx, c_ctx, w_mod, b_mod, norm1_g, w_in, q_a_norm_g, kv_a_norm_g, w_q_up, w_kv_up,
    q_norm_g, k_norm_g, w_o_attn, w_fourier, w_out, norm2_g, w_router, w_e_gate, w_e_up,
    w_e_down, norm1_g_2, w_in_2, lru_conv_w_2, lru_conv_b_2, lru_wa_2, lru_ba_2, lru_wx_2,
    lru_bx_2, lru_lambda_2, sc_conv_w_2, w_out_2, norm2_g_2, w_up_2, ffn_conv_w_2, w_down_2,
    final_g_2,
):
    x = first_block(
        x, c, ctx, c_ctx, w_mod, b_mod, norm1_g, w_in, q_a_norm_g, kv_a_norm_g, w_q_up, w_kv_up,
        q_norm_g, k_norm_g, w_o_attn, w_fourier, w_out, norm2_g, w_router, w_e_gate, w_e_up,
        w_e_down,
    )
    return second_block(
        x, norm1_g_2, w_in_2, lru_conv_w_2, lru_conv_b_2, lru_wa_2, lru_ba_2, lru_wx_2,
        lru_bx_2, lru_lambda_2, sc_conv_w_2, w_out_2, norm2_g_2, w_up_2, ffn_conv_w_2, w_down_2,
        final_g_2,
    )


_drawn_inputs = setup_inputs


def setup_inputs(seed=0):
    import zlib

    import numpy as np

    out = dict(_drawn_inputs(seed))
    spreads = {}
    factors = {'ctx': 5.746,
     'c_ctx': 4.001,
     'b_mod': 3.425,
     'norm1_g': 8.0,
     'q_a_norm_g': 8.0,
     'kv_a_norm_g': 8.0,
     'w_q_up': 3.367,
     'q_norm_g': 8.0,
     'k_norm_g': 8.0,
     'norm2_g': 7.982,
     'norm1_g_2': 3.651,
     'lru_ba_2': 64.0,
     'lru_bx_2': 64.0,
     'norm2_g_2': 22.408,
     'final_g_2': 7.484,
     'lru_conv_b_2': 8.0}
    for name, (base, spread) in spreads.items():
        noise = np.random.default_rng([zlib.crc32(name.encode()), seed]).standard_normal(out[name].shape)
        drawn = base * np.exp(spread * noise) if base else spread * noise
        out[name] = __import__('jax').numpy.asarray(drawn.astype(out[name].dtype))
    for name, factor in factors.items():
        out[name] = (out[name] * factor).astype(out[name].dtype)
    return out
```

```python
import concourse.bass as bass
from concourse import mybir
from contextlib import ExitStack

F32 = mybir.dt.float32
F32R = mybir.dt.float32r
ALU = mybir.AluOpType
ACT = mybir.ActivationFunctionType
AX = mybir.AxisListType

P = 128
T = 512
TC = 256
TK = T + TC
D = 1024
KD = D // P
EPS = 1e-6
H = 8
QK = 96
NOPE = 64
ROPE = 32
VD = 64
QL = 384 // P
KL = 256 // P
NF = 512 // P
TT = T // P
KT = TK // P
NE = 16
CAP = 2 * T // NE
FE = 512 // P
PAIRS = NE // 2
LRU = 8
SC = 4
FF = 3072 // P
QUARTERS = 4
FQ = FF // QUARTERS

CH = 2048
NRAW = 4
NHL = 3
SECTIONS = [("mod_a", 8, False), ("s1", 20, True), ("mod_b", 16, False), ("wo", 2, True), ("w_out", 4, True),
            ("experts", 96, False), ("w_in_2", 14, True), ("w_out_2", 6, True), ("ffn", 36, True)]
B = 128
S1_QKV, S1_KPE, S1_F, S1_DFT = 0, 40 * B, 44 * B, 80 * B
S1_GA, S1_GB, S1_V, S1_HEADS = 112 * B, 176 * B, 17 * CH, 18 * CH
HEAD_W = QL * QK + KL * NOPE
assert 4 * HEAD_W <= CH

COLS = {}
_n = 0
for _name, _w in [("norm1_g", 8), ("b_mod", 48), ("q_a_norm_g", QL), ("kv_a_norm_g", KL), ("q_norm_g", 1),
                  ("k_norm_g", 1), ("norm2_g", 8), ("cond", 16), ("norm1_g_2", 8), ("lru_conv_w_2", 32),
                  ("lru_conv_b_2", 8), ("lru_ba_2", 8), ("lru_bx_2", 8), ("lru_lambda_2", 8),
                  ("sc_conv_w_2", 12), ("norm2_g_2", 8), ("ffn_conv_w_2", 144), ("final_g_2", 8), ("slot", 1)]:
    COLS[_name] = _n
    _n += _w
NCOLS = _n


class Order:

    def __init__(self):
        self.at = {}

    def add(self, *name):
        assert name not in self.at, name
        self.at[name] = len(self.at)

    def __getitem__(self, name):
        return self.at[name if isinstance(name, tuple) else (name,)]

    def __len__(self):
        return len(self.at)


class Plan:

    def __init__(self):
        self.tiles = Order()
        self.bank, self.freed, self.prev = [], [], []
        self.counts = {"act": 0, "dve": 0}
        self.last_user = {}
        self.owner = {}
        self.nb = 6
        self.start = 0

    def phase(self, nb):
        self.nb, self.start = nb, len(self.tiles)

    def add(self, *name, by="dve", raw=(), split=()):
        t = len(self.tiles)
        self.tiles.add(*name)
        b = (t - self.start) % self.nb
        self.bank.append(b)
        if isinstance(by, str):
            self.counts[by] += 1
            by = (by, self.counts[by])
        self.freed.append(by)
        self.prev.append(self.owner.get(b))
        self.owner[b] = t
        for c in raw:
            self.last_user["raw", c] = t
        for c in split:
            self.last_user["split", c] = t

    def freed_count(self, t):
        return self.freed[t][1]


def section_start(name, split_only):
    n = 0
    for s, k, split in SECTIONS:
        if s == name:
            return n
        if split or not split_only:
            n += k


def raw_chunks():
    out, ns, nr = [], 0, 0
    for _, k, split in SECTIONS:
        for _ in range(k):
            out.append((split, ns if split else nr))
            ns, nr = ns + split, nr + (not split)
    return out


CHUNKS = raw_chunks()
RAW_OF_SPLIT = [n for n, (s, _) in enumerate(CHUNKS) if s]
SPLIT0 = {s: section_start(s, True) for s, _, sp in SECTIONS if sp}
RAW0 = {s: section_start(s, False) for s, _, sp in SECTIONS}


def blocks(base, first, count, width=B):
    return range(base + first // CH, base + (first + count * width - 1) // CH + 1)


def split_steps():
    o = Order()
    for j in range(KD):
        o.add("h", j)
    for j in range(KD):
        o.add("hc", j)
    o.add("f", 0)
    o.add("f", 1)
    for j in range(QL):
        o.add("cq", j)
    for j in range(KL):
        o.add("ckv", j)
    o.add("f", 2)
    o.add("f", 3)
    for g in range(NF + 1):
        if g < NF:
            o.add("f_ch", g, 0)
            o.add("f_ch", g, 1)
        if g >= 1:
            o.add("four", g - 1)
    for h in range(H):
        o.add("q", h)
        o.add("k", h)
    for j in range(4):
        o.add("attn", j)
    for j in range(KD):
        o.add("m", j)
    for t in range(TT):
        o.add("h2_tok", t, 0)
        o.add("h2_tok", t, 1)
    for e in range(NE):
        o.add("ye", e, 0)
        o.add("ye", e, 1)
    for j in range(KD):
        o.add("g", j)
    for j in range(SC):
        o.add("y_sc", j)
    for j in range(LRU):
        o.add("y_lru", j)
    for j in range(KD):
        o.add("g2", j)
    for q in range(QUARTERS):
        for i in range(FQ):
            o.add("ff", q, i)
    return o


SPLITS = split_steps()

PRE_Q = 2 * KD + QL + KL
PRE_SC = PRE_Q + 2 * H + 2 * KD
PRE_FF = PRE_SC + SC + LRU + KD


def make_plan():
    p = Plan()
    s1 = SPLIT0["s1"]
    p.add("ssq_x", by="act")
    p.add("ssq_ctx", by="act")
    for g in range(4):
        p.add("mod", g, raw=(2 * g, 2 * g + 1))
    for j in range(QL):
        p.add("cq", j, split=blocks(s1, S1_QKV + j * 8 * B, 8))
    for j in range(KL):
        p.add("ckv", j, 0)
        p.add("ckv", j, 1, split=blocks(s1, S1_QKV + (QL + j) * 8 * B, 8))
    p.add("kpe", 0)
    p.add("kpe", 1, split=blocks(s1, S1_KPE, 2))
    p.add("f", 0, by=("lo_done", SPLITS["f", 0] + 1), split=blocks(s1, S1_F, 8))
    p.add("f", 1, by=("lo_done", SPLITS["f", 1] + 1), split=blocks(s1, S1_F + 8 * B, 8))
    p.add("ssq_cq", by="act")
    p.add("ssq_ckv", 0, by="act")
    p.add("ssq_ckv", 1, by="act")
    p.add("f", 2, by=("lo_done", SPLITS["f", 2] + 1), split=blocks(s1, S1_F + 16 * B, 8))
    p.add("f", 3, by=("lo_done", SPLITS["f", 3] + 1), split=blocks(s1, S1_F + 24 * B, 12))
    p.add("rot_k")
    for g in range(NF + 1):
        if g < NF:
            p.add("f_ch", g, 0, by=("lo_done", SPLITS["f_ch", g, 0] + 1))
            p.add("f_ch", g, 1, by=("lo_done", SPLITS["f_ch", g, 1] + 1))
        if g >= 1:
            p.add("four", g - 1, by=("lo_done", SPLITS["four", g - 1] + 1), split=blocks(s1, S1_DFT, 32))
    for j in range(KD):
        p.add("ga", j, by="act", split=blocks(s1, S1_GA + j * 8 * B, 8))
    for j in range(KD):
        p.add("gb", j, by="act", split=blocks(s1, S1_GB + j * 12 * B, 8))
        p.add("four_o", j, by=("resid_done", j + 1), split=blocks(s1, S1_GB + j * 12 * B + 8 * B, 4))
    for t in range(KT):
        p.add("v", t, by="act", split=blocks(s1, S1_V, 8))

    def prep_a(h):
        c = (s1 + (S1_HEADS + (h // 4) * CH) // CH,)
        p.add("uq", h, by=("qk_raw", 2 * h + 1), split=c)
        p.add("uk", h, 0, by=("qk_raw", 2 * h + 2), split=c)
        p.add("uk", h, 1, by=("qk_raw", 2 * h + 2), split=c)

    def prep_b(h):
        p.add("ssq_q", h, by="act")
        p.add("ssq_k", h, 0, by="act")
        p.add("ssq_k", h, 1, by="act")
        p.add("rot_q", h)

    prep_a(0)
    prep_b(0)
    for h in range(H):
        for q in range(TT):
            for s in range(2):
                p.add("mx", h, q, s)
        if h + 1 < H:
            prep_a(h + 1)
        p.add("mx_row", h, by="act")
        for k in range(KT):
            p.add("sT", h, k, by="act")
        if h + 1 < H:
            prep_b(h + 1)
        p.add("mod", 4 + h, raw=(8 + 2 * h, 9 + 2 * h))
    for j in range(KD):
        p.add("attn_o", j, split=blocks(SPLIT0["wo"], j * 4 * B, 4))
    for j in range(KD):
        p.add("merged", j, by=("resid_done", KD + j + 1), split=blocks(SPLIT0["w_out"], j * 8 * B, 8))
    p.add("logits", by=("logit_max", 1))
    p.add("aff_t")
    for t in range(TT):
        p.add("h2_tok", t, 0, by=("lo_done", SPLITS["h2_tok", t, 0] + 1))
        p.add("h2_tok", t, 1, by=("lo_done", SPLITS["h2_tok", t, 1] + 1))
    p.add("slots_tok")
    p.add("gates")
    for i in range(KD):
        p.add("xe", i, 0, by="act")
        p.add("xe", i, 1, by="act")
    for i in range(PAIRS):
        p.add("onehot", i)
    e0 = 8 + 16
    p.phase(6)
    p.add("gu", 0, by=("act_done", 1), raw=range(e0, e0 + 4))
    for e in range(NE):
        at = e0 + 4 + 6 * e
        if e + 1 < NE:
            p.add("gu", e + 1, by=("act_done", e + 2), raw=range(at, at + 4))
            at += 4
        p.add("ye", e, 0, by=("lo_done", SPLITS["ye", e, 0] + 1), raw=(at,))
        p.add("ye", e, 1, by=("lo_done", SPLITS["ye", e, 1] + 1), raw=(at + 1,))
    for j in range(KD):
        p.add("combine", j, by=("resid_done", 2 * KD + j + 1))
    w = SPLIT0["w_in_2"]
    for j in range(LRU):
        p.add("lru_x", j, by=("conv_done", j + 1), split=blocks(w, j * 8 * B, 8))
        if j >= 1:
            p.add("lru_r", j - 1, by="act")
            p.add("lru_i", j - 1, by="act")
    for j in range(SC):
        p.add("sc_c", j, by="act", split=blocks(w, (LRU + 3 * j) * 8 * B, 8))
        if j == 0:
            p.add("lru_r", LRU - 1, by="act")
            p.add("lru_i", LRU - 1, by="act")
        p.add("sc_x", j, split=blocks(w, (LRU + 3 * j + 1) * 8 * B, 8))
        p.add("sc_b", j, by=("pre_done", PRE_SC + j + 1), split=blocks(w, (LRU + 3 * j + 2) * 8 * B, 8))
    for j in range(LRU):
        p.add("lru_gate", j, by="act", split=blocks(w, (LRU + 3 * SC + j) * 8 * B, 8))
    for j in range(KD):
        p.add("mix_o", j, by=("resid_done", 3 * KD + j + 1), split=blocks(SPLIT0["w_out_2"], j * 12 * B, 12))
    w = SPLIT0["ffn"]
    p.phase(5)
    for q in range(QUARTERS):
        for i in range(FQ):
            p.add("ff_g", q, i, by=("accg_done", q * FQ + i + 1), split=blocks(w, (q * 144 + i * 16) * B, 8))
            p.add("ff_u", q, i, by=("accu_done", q * FQ + i + 1), split=blocks(w, (q * 144 + i * 16 + 8) * B, 8))
        for j in range(KD):
            p.add("ff_o", q, j, by=("resid_done", (4 + q) * KD + j + 1), split=blocks(w, (q * 144 + 96 + j * 6) * B, 6))
    return p


PLAN = make_plan()
TILE = PLAN.tiles
LAST = PLAN.last_user


NSPLIT = len(RAW_OF_SPLIT)


def split_due(c):
    n = RAW_OF_SPLIT[c] - NRAW
    due = [LAST["split", c - NHL] + 1] if c >= NHL else [0]
    due += [LAST["raw", k] + 1 for sp, k in CHUNKS[:max(n + 1, 0)] if not sp]
    if c >= SPLIT0["w_in_2"]:
        due.append(TILE["combine", KD - 1] + 1)
    return max(due)


SPLIT_DUE = [split_due(c) for c in range(NSPLIT)]
FFN0 = TILE["ff_g", 0, 0]
FFN_TILES = 2 * FQ + KD
FFN_CHUNKS = 9


def build(nc, stream, cols_d, x_d, ctx_d, router_d, wab_d, rope_d, rot_d, dftc_d, ident_d, iota_d, pick_d, out):
    with ExitStack() as ctx:
        base = 16512

        def at(name, kb, shape, dt=F32):
            return nc.alloc_sbuf_tensor_at(name, shape, dt, offset=base + int(kb * 1024))

        def sem(name):
            return ctx.enter_context(nc.semaphore(name))

        raw = at("raw", 0, [P, NRAW, CH])
        w_hi = at("w_hi", 32, [P, NHL, CH], F32R)
        w_lo = at("w_lo", 56, [P, NHL, CH], F32R)
        R = 80
        x1 = at("x1", R + 96, [P, KD, T])
        cols = at("cols", R + 122.75, [P, NCOLS])
        mod = at("mod", R + 124.25, [P, 48, 2])
        ones = at("ones", R + 124.75, [P, P])
        ident = at("ident", R + 125.25, [P, P])
        router = at("router", R + 125.75, [P, KD, NE])
        iota = at("iota", R + 126.25, [P, CAP])
        small = at("small", R + 126.5, [P, 256])
        assert base + (R + 127.5) * 1024 <= 229368 and NCOLS * 4 <= 1536

        def cut(off, n):
            return small[:, off:off + n]
        a1, a1c, a2 = cut(0, 8), cut(8, 8), cut(16, 8)
        eps, csil = cut(24, 1), cut(32, 16)
        nba, nbx, nc8, c8 = cut(48, 8), cut(56, 8), cut(64, 8), cut(72, 8)
        sp_z, sp_s, sp_s2, sp_p = cut(80, 8), cut(88, 8), cut(96, 8), cut(104, 8)
        mx2, mxq, gcol = cut(112, 8), cut(120, 4), cut(128, 8)
        h_hi = at("h_hi", R + 0, [P, KD, T], F32R)
        h_lo = at("h_lo", R + 16, [P, KD, T], F32R)
        hc_hi = at("hc_hi", R + 32, [P, KD, TC], F32R)
        hc_lo = at("hc_lo", R + 40, [P, KD, TC], F32R)
        x0 = at("x0", R + 48, [P, KD, T])
        c0 = at("c0", R + 64, [P, KD, TC])
        sq_x0 = at("sq_x0", R + 72, [P, KD, T])
        sq_c0 = at("sq_c0", R + 88, [P, KD, TC])
        pre = at("pre", R + 96, [P, 2, T])
        rstd_x0 = at("rstd_x0", R + 112, [P, T])
        rstd_c0 = at("rstd_c0", R + 114, [P, TC])
        cqg = at("cqg", R + 48, [P, QL, T])
        ckvg = at("ckvg", R + 54, [P, KL, TK])
        sq_q = at("sq_cq", R + 60, [P, QL, T])
        sq_kv = at("sq_ckv", R + 66, [P, KL, TK])
        rstd_cq = at("rstd_cq", R + 72, [P, T])
        rstd_ckv = at("rstd_ckv", R + 74, [P, TK])
        cq_hi = at("cq_hi", R + 80, [P, QL, T], F32R)
        cq_lo = at("cq_lo", R + 86, [P, QL, T], F32R)
        ckv_hi = at("ckv_hi", R + 92, [P, KL, TK], F32R)
        ckv_lo = at("ckv_lo", R + 98, [P, KL, TK], F32R)
        f_hi = at("f_hi", R + 32, [P, NF, T], F32R)
        f_lo = at("f_lo", R + 40, [P, NF, T], F32R)
        fc_hi = at("fc_hi", R + 48, [P, 2, 2, 2, 256], F32R)
        fc_lo = at("fc_lo", R + 56, [P, 2, 2, 2, 256], F32R)
        ga = at("ga", R + 48, [P, KD, T])
        gbf = at("gbf", R + 64, [P, KD, T])
        kraw = at("kraw", R + 104, [QK, TK])
        sqk = at("sqk", R + 107, [QK, TK])
        sqq = at("sqq", R + 110, [QK, T])
        rk = at("rk", R + 112, [QK, TK])
        rope_cs = at("rope_cs", R + 115, [QK, 2, T])
        dftc = at("dftc", R + 119, [P, 256])
        dftc_hi = at("dftc_hi", R + 120, [P, 256], F32R)
        dftc_lo = at("dftc_lo", R + 121, [P, 256], F32R)
        rotm = at("rotm", R + 122, [QK, QK])
        sg = [at("sg0", R + 110, [P, T]), at("sg1", R + 112, [P, T])]
        v = at("v", R + 0, [P, KT, H // 2, 3, VD])
        q_hi = at("q_hi", R + 18, [QK + 1, T], F32R)
        q_lo = at("q_lo", R + 20, [QK + 1, T], F32R)
        k_hi = at("k_hi", R + 22, [QK + 1, TK], F32R)
        k_lo = at("k_lo", R + 25, [QK + 1, TK], F32R)
        probs = at("probs", R + 28, [P, 3, T])
        att = at("att", R + 34, [P, 4, T])
        tmp_a = at("tmp_a", R + 42, [P, T])
        rs = at("rs", R + 44, [P, T])
        qg = at("qg", R + 46, [QK, T])
        rq = at("rq", R + 119, [QK, T])
        att_hi = at("att_hi", R + 80, [P, 4, T], F32R)
        att_lo = at("att_lo", R + 88, [P, 4, T], F32R)
        m_hi = at("m_hi", R + 0, [P, KD, T], F32R)
        m_lo = at("m_lo", R + 16, [P, KD, T], F32R)
        m_tmp = at("m_tmp", R + 42, [P, 2, T])
        sq = at("sq", R + 48, [P, 2, T])
        rstd = at("rstd", R + 120, [P, T])
        h2 = at("h2", R + 80, [P, KD, T])
        h2t_hi = at("h2t_hi", R + 0, [P, TT, D], F32R)
        h2t_lo = at("h2t_lo", R + 16, [P, TT, D], F32R)
        pick_tok = at("pick_tok", R + 32, [P, TT, NE * CAP], F32R)
        xe = at("xe", R + 48, [P, KD, NE * CAP])
        place = at("place", R + 80, [P, PAIRS, T], F32R)
        aff_t = at("aff_t", R + 112, [NE, T])
        work = at("work", R + 114, [NE, T])
        chosen = at("chosen", R + 116, [NE, T])
        slots = at("slots", R + 118, [NE, T])
        pick = at("pick", R + 112, [NE, PAIRS * P])
        aff = at("aff", R + 120, [P, TT, NE])
        aff_m = at("aff_m", R + 120.25, [P, TT])
        aff_s = at("aff_s", R + 120.5, [P, TT])
        slots_tok = at("slots_tok", R + 120.75, [P, TT, NE])
        top8 = at("top8", R + 121, [NE, 8])
        ones_row = at("ones_row", R + 40, [NE, T])
        gate_s = at("gate_s", R + 112, [P, 2, FE * CAP])
        act_e = at("act_e", R + 114, [P, 2, FE * CAP])
        ye_hi = at("ye_hi", R + 0, [P, PAIRS, D], F32R)
        ye_lo = at("ye_lo", 32, [P, PAIRS, D], F32R)
        lru_a = at("lru_a", R + 32, [P, LRU, T])
        lru_v = at("lru_v", R + 48, [P, LRU, T])
        lru_b = at("lru_b", R + 64, [P, LRU, T])
        g_pre = at("g_pre", R + 80, [P, 2, T])
        conv_u = at("conv_u", R + 84, [P, 2, T])
        e_r = at("e_r", R + 88, [P, T])
        e_i = at("e_i", R + 90, [P, T])
        a_sq = at("a_sq", R + 92, [P, T])
        a_th = at("a_th", R + 94, [P, T])
        wab = at("wab", R + 112, [P, 2, LRU, P])
        ysc_hi = at("ysc_hi", R + 80, [P, SC, T], F32R)
        ysc_lo = at("ysc_lo", R + 88, [P, SC, T], F32R)
        sc_c = at("sc_c", R + 112, [P, T])
        sc_cx = at("sc_cx", R + 114, [P, T])
        sc_acc = at("sc_acc", R + 116, [P, T])
        sc_y = at("sc_y", R + 118, [P, T])
        gl = at("gl", R + 112, [P, 2, T])
        y_pre = at("y_pre", R + 116, [P, 2, T])
        ylru_hi = at("ylru_hi", R + 32, [P, LRU, T], F32R)
        ylru_lo = at("ylru_lo", R + 64, [P, LRU, T], F32R)
        ff_hi = at("ff_hi", R + 32, [P, FQ, T], F32R)
        ff_lo = at("ff_lo", R + 44, [P, FQ, T], F32R)
        acc_g = at("acc_g", R + 56, [P, 2, T])
        acc_u = at("acc_u", R + 60, [P, 2, T])
        ff_gl = at("ff_gl", R + 64, [P, 2, T])
        ff_pre = at("ff_pre", R + 68, [P, 2, T])
        sq_last = at("sq_last", R + 72, [P, 2, T])
        y_out = at("y_out", R + 0, [P, KD, T])

        psum = nc.alloc_psum_tensor("psum", [P, 8, T], F32)

        raw_full = [sem(f"raw_full{i}") for i in range(NRAW)]
        w_hi_done = sem("w_hi_done")
        w_lo_done = sem("w_lo_done")
        tile_full = sem("tile_full")
        freed_act = sem("freed_act")
        freed_dve = sem("freed_dve")
        hi_done = sem("hi_done")
        lo_done = sem("lo_done")
        consts_in = sem("consts_in")
        x_in = sem("x_in")
        x_again = sem("x_again")
        wab_in = sem("wab_in")
        pick_in = sem("pick_in")
        silu_done = sem("silu_done")
        sq_done = sem("sq_done")
        sum_full = sem("sum_full")
        sq_summed = sem("sq_summed")
        std_done = sem("std_done")
        pre_done = sem("pre_done")
        act_seq = sem("act_seq")
        dve_seq = sem("dve_seq")
        ones_done = sem("ones_done")
        qk_raw = sem("qk_raw")
        mx_done = sem("mx_done")
        o_full = sem("o_full")
        o_freed = sem("o_freed")
        gate_done = sem("gate_done")
        v_done = sem("v_done")
        resid_done = sem("resid_done")
        h2_done = sem("h2_done")
        logit_max = sem("logit_max")
        aff_exp = sem("aff_exp")
        aff_done = sem("aff_done")
        slots_done = sem("slots_done")
        picks_done = sem("picks_done")
        silu_e = sem("silu_e")
        act_done = sem("act_done")
        conv_done = sem("conv_done")
        eri_done = sem("eri_done")
        ri_done = sem("ri_done")
        av_done = sem("av_done")
        v_ready = sem("v_ready")
        mult_done = sem("mult_done")
        glu_done = sem("glu_done")
        acc_done = sem("acc_done")
        accg_done = sem("accg_done")
        accu_done = sem("accu_done")
        sp_done = sem("sp_done")
        y_done = sem("y_done")
        out_done = sem("out_done")
        z_done = sem("z_done")

        freeing = {"act": freed_act, "dve": freed_dve, "lo_done": lo_done, "resid_done": resid_done,
                   "qk_raw": qk_raw, "logit_max": logit_max, "act_done": act_done, "conv_done": conv_done,
                   "pre_done": pre_done, "accg_done": accg_done, "accu_done": accu_done}

        block = ctx.enter_context(nc.Block())

        def col(name, j=0, n=1):
            return cols[:, COLS[name] + j:COLS[name] + j + n]

        def bank(*name):
            return psum[:, PLAN.bank[TILE[name]], :]

        def full(eng, *name, plus=0):
            eng.wait_ge(tile_full, TILE[name] + 1 + plus)

        @block.sync
        def _(sp):
            sp.dma_start(cols[:], cols_d).then_inc(consts_in, 16)
            sp.dma_start(x0[:], x_d).then_inc(x_in, 16)
            sp.dma_start(c0[:], ctx_d).then_inc(x_in, 16)
            sp.dma_start(ident[:], ident_d).then_inc(consts_in, 16)
            sp.dma_start(iota[:], iota_d).then_inc(consts_in, 16)
            sp.dma_start(router[:], router_d).then_inc(consts_in, 16)
            sp.dma_start(dftc[:], dftc_d).then_inc(consts_in, 16)
            sp.dma_start(rotm[:], rot_d).then_inc(consts_in, 16)
            sp.dma_start(rope_cs[NOPE:QK, :, :], rope_d).then_inc(consts_in, 16)

            def load(n, slot):
                sp.dma_start(raw[:, slot, :], stream[bass.ds(n, 1), :, :].rearrange("a p c -> p (a c)")
                             if not isinstance(n, int) else stream[n, :, :]).then_inc(raw_full[slot], 16)

            for n in range(NRAW):
                load(n, n)
            n = NRAW
            while n < len(CHUNKS):
                split, k = CHUNKS[n - NRAW]
                run = n
                while run < len(CHUNKS) and CHUNKS[run - NRAW][0] == split:
                    run += 1
                loops = (run - n) // NRAW if split else 0
                if loops >= 2:
                    with sp.Fori(0, loops) as i:
                        for s in range(NRAW):
                            sp.wait_ge(w_lo_done, i * NRAW + k + s + 1)
                            load(i * NRAW + (n + s), (n + s) % NRAW)
                    n += loops * NRAW
                    continue
                for m in range(n, run):
                    _, k = CHUNKS[m - NRAW]
                    if split:
                        sp.wait_ge(w_lo_done, k + 1)
                    else:
                        sp.wait_ge(tile_full, LAST["raw", k] + 1)
                    load(m, m % NRAW)
                n = run
            sp.wait_ge(out_done, 16 * KD)

        @block.gpsimd
        def _(pool):
            nc.gpsimd.memset(ones[:], 1.0).then_inc(ones_done, 1)

            def lo(c, slot, raw_slot):
                pool.wait_ge(w_hi_done, c + 1)
                nc.gpsimd.tensor_tensor(w_lo[:, slot, :], raw[:, raw_slot, :], w_hi[:, slot, :].bitcast(F32),
                                        ALU.subtract).then_inc(w_lo_done, 1)

            PERIOD = NRAW * NHL
            c = 0
            while c < NSPLIT:
                run = c
                while run < NSPLIT and RAW_OF_SPLIT[run] - run == RAW_OF_SPLIT[c] - c:
                    run += 1
                loops = (run - c) // PERIOD
                if loops >= 2:
                    with pool.Fori(0, loops) as i:
                        for s in range(PERIOD):
                            lo(i * PERIOD + (c + s), (c + s) % NHL, RAW_OF_SPLIT[c + s] % NRAW)
                    c += loops * PERIOD
                for s in range(c, run):
                    lo(s, s % NHL, RAW_OF_SPLIT[s] % NRAW)
                c = run

        @block.tensor
        def _(pe):
            mm = nc.tensor.matmul
            seen = [0]

            def open_tile(*name):
                t = TILE[name]
                prev = PLAN.prev[t]
                if prev is not None:
                    pe.wait_ge(freeing[PLAN.freed[prev][0]], PLAN.freed_count(prev))
                return psum[:, PLAN.bank[t], :]

            def weights(base, off, width):
                c, o = base + off // CH, off % CH
                assert o + width <= CH
                if c + 1 > seen[0]:
                    pe.wait_ge(w_lo_done, c + 1)
                    seen[0] = c + 1
                return w_hi[:, c % NHL, o:o + width], w_lo[:, c % NHL, o:o + width]

            def mm3(o, w, x, start, stop):
                mm(o, w[0], x[0], start=start, stop=False)
                mm(o, w[0], x[1], start=False, stop=False)
                return mm(o, w[1], x[0], start=False, stop=stop)

            def done(ins):
                ins.then_inc(tile_full, 1)

            def project(o, base, off, width, ks, x_of):
                for i, k in enumerate(ks):
                    last = mm3(o, weights(base, off + i * width, width), x_of(k), i == 0, i == len(ks) - 1)
                return last

            def raw_chunk(n):
                pe.wait_ge(raw_full[n % NRAW], 16 * (n // NRAW + 1))
                return raw[:, n % NRAW, :]

            def mod_tile(g):
                o = open_tile("mod", g)
                for c in range(2):
                    k = 2 * g + c
                    n = RAW0["mod_a"] + k if g < 4 else RAW0["mod_b"] + k - 8
                    w = raw_chunk(n)
                    for m in range(2):
                        for kk in range(KD):
                            last = mm(o[:, 4 * c + 2 * m:4 * c + 2 * m + 2],
                                      w[:, (m * KD + kk) * B:(m * KD + kk + 1) * B],
                                      csil[:, 2 * kk:2 * kk + 2], start=kk == 0, stop=kk == KD - 1)
                done(last)

            pe.wait_ge(ones_done, 1)
            pe.wait_ge(sq_done, 1)
            for name, n, src, w in (("ssq_x", 1, sq_x0, T), ("ssq_ctx", 2, sq_c0, TC)):
                o = open_tile(name)
                pe.wait_ge(sq_done, n)
                for k in range(KD):
                    last = mm(o[:, 0:w], ones[:], src[:, k, :], start=k == 0, stop=k == KD - 1)
                done(last)
            pe.wait_ge(silu_done, 1)
            for g in range(4):
                mod_tile(g)

            s1 = SPLIT0["s1"]
            hx = lambda k: (h_hi[:, k, :], h_lo[:, k, :])
            hcx = lambda k: (hc_hi[:, k, :], hc_lo[:, k, :])
            ks = range(KD)
            pe.wait_ge(lo_done, SPLITS["h", KD - 1] + 1)
            for j in range(QL):
                o = open_tile("cq", j)
                done(project(o, s1, S1_QKV + j * 8 * B, B, ks, hx))
            pe.wait_ge(lo_done, SPLITS["hc", KD - 1] + 1)
            for j in range(KL):
                for s in range(2):
                    o = open_tile("ckv", j, s)
                    done(project(o if s == 0 else o[:, 0:TC], s1, S1_QKV + (QL + j) * 8 * B, B, ks, hcx if s else hx))
            for s in range(2):
                o = open_tile("kpe", s)
                done(project(o[0:ROPE, 0:TC if s else T], s1, S1_KPE, ROPE, ks, hcx if s else hx))

            def fourier_in(g):
                done(project(open_tile("f", g), s1, S1_F + g * 8 * B, B, ks, hx))

            fourier_in(0)
            fourier_in(1)
            o = open_tile("ssq_cq")
            pe.wait_ge(sq_done, 2 + QL)
            for j in range(QL):
                last = mm(o, ones[:], sq_q[:, j, :], start=j == 0, stop=j == QL - 1)
            done(last)
            for s in range(2):
                o = open_tile("ssq_ckv", s)
                pe.wait_ge(sq_done, 2 + QL + 2 * KL)
                w = slice(0, T) if s == 0 else slice(T, TK)
                for j in range(KL):
                    last = mm(o[:, 0:TC if s else T], ones[:], sq_kv[:, j, w], start=j == 0, stop=j == KL - 1)
                done(last)
            fourier_in(2)
            fourier_in(3)
            o = open_tile("rot_k")
            pe.wait_ge(freed_dve, PLAN.freed_count(TILE["kpe", 1]))
            done(mm(o[0:QK, :], rotm[NOPE:QK, :], kraw[NOPE:QK, 0:T], start=True, stop=True))
            for g in range(NF + 1):
                if g < NF:
                    pe.wait_ge(lo_done, SPLITS["f", 3] + 1)
                    for half in range(2):
                        o = open_tile("f_ch", g, half)
                        for t in range(2):
                            tok = slice((2 * half + t) * P, (2 * half + t + 1) * P)
                            last = mm3(o[:, t * 256:(t + 1) * 256], (f_hi[:, g, tok], f_lo[:, g, tok]),
                                       (dftc_hi[:], dftc_lo[:]), True, True)
                        done(last)
                if g >= 1:
                    o = open_tile("four", g - 1)
                    pe.wait_ge(lo_done, SPLITS["f_ch", g - 1, 1] + 1)
                    for part in range(2):
                        for t in range(TT):
                            i = part * TT + t
                            x = weights(s1, S1_DFT + i * 4 * B, T)
                            a = slice(part * P, part * P + P)
                            last = mm3(o, (fc_hi[:, (g - 1) % 2, t // 2, t % 2, a], fc_lo[:, (g - 1) % 2, t // 2, t % 2, a]),
                                       x, i == 0, i == 2 * TT - 1)
                    done(last)
            for j in range(KD):
                done(project(open_tile("ga", j), s1, S1_GA + j * 8 * B, B, ks, hx))
            for j in range(KD):
                done(project(open_tile("gb", j), s1, S1_GB + j * 12 * B, B, ks, hx))
                o = open_tile("four_o", j)
                pe.wait_ge(lo_done, SPLITS["four", NF - 1] + 1)
                done(project(o, s1, S1_GB + j * 12 * B + 8 * B, B, range(NF), lambda k: (f_hi[:, k, :], f_lo[:, k, :])))
            for t in range(KT):
                o = open_tile("v", t)
                for k in range(KL):
                    tok = slice(t * P, t * P + P)
                    last = mm3(o, (ckv_hi[:, k, tok], ckv_lo[:, k, tok]), weights(s1, S1_V + k * T, T),
                               k == 0, k == KL - 1)
                done(last)

            def head_w(h):
                return S1_HEADS + (h // 4) * CH + (h % 4) * HEAD_W

            def prep_a(h):
                o = open_tile("uq", h)
                done(project(o[0:QK, :], s1, head_w(h), QK, range(QL), lambda k: (cq_hi[:, k, :], cq_lo[:, k, :])))
                for s in range(2):
                    o = open_tile("uk", h, s)
                    w = slice(0, T) if s == 0 else slice(T, TK)
                    done(project(o[0:NOPE, 0:TC if s else T], s1, head_w(h) + QL * QK, NOPE, range(KL),
                                 lambda k: (ckv_hi[:, k, w], ckv_lo[:, k, w])))

            def prep_b(h):
                o = open_tile("ssq_q", h)
                pe.wait_ge(qk_raw, 1 + 2 * h)
                done(mm(o[0:QK, :], ones[0:QK, 0:QK], sqq[:], start=True, stop=True))
                for s in range(2):
                    o = open_tile("ssq_k", h, s)
                    pe.wait_ge(qk_raw, 2 + 2 * h)
                    w = slice(0, T) if s == 0 else slice(T, TK)
                    done(mm(o[0:QK, 0:TC if s else T], ones[0:QK, 0:QK], sqk[:, w], start=True, stop=True))
                o = open_tile("rot_q", h)
                done(mm(o[0:QK, :], rotm[NOPE:QK, :], qg[NOPE:QK, :], start=True, stop=True))

            prep_a(0)
            prep_b(0)
            KH = TK // 2
            for h in range(H):
                pe.wait_ge(lo_done, SPLITS["k", h] + 1)
                for q in range(TT):
                    for s in range(2):
                        o = open_tile("mx", h, q, s)
                        done(mm(o[:, 0:KH], q_hi[0:QK, q * P:(q + 1) * P], k_hi[0:QK, s * KH:(s + 1) * KH],
                                start=True, stop=True))
                if h + 1 < H:
                    prep_a(h + 1)
                o = open_tile("mx_row", h)
                pe.wait_ge(mx_done, h + 1)
                for q in range(TT):
                    last = nc.tensor.transpose(o[0:1, q * P:(q + 1) * P], mxq[:, q:q + 1], ident[:])
                done(last)

                def pv(k):
                    if k == 0 and h >= 2:
                        pe.wait_ge(o_freed, h - 1)
                    pe.wait_ge(freed_act, PLAN.freed_count(TILE["sT", h, k]))
                    va = v[:, k, h // 2, h % 2:h % 2 + 2, :].rearrange("p a b -> p (a b)")
                    return mm(psum[:, 6 + h % 2, :], va, probs[:, k % 3, :], start=k == 0, stop=k == KT - 1)

                if h == 0:
                    pe.wait_ge(v_done, 2)
                for k in range(KT):
                    o = open_tile("sT", h, k)
                    if k == 0:
                        pe.wait_ge(freed_act, PLAN.freed_count(TILE["mx_row", h]))
                    tok = slice(k * P, k * P + P)
                    done(mm3(o, (k_hi[:, tok], k_lo[:, tok]), (q_hi[:], q_lo[:]), True, True))
                    if k >= 2:
                        pv(k - 2)
                pv(KT - 2)
                pv(KT - 1).then_inc(o_full, 1)
                if h + 1 < H:
                    prep_b(h + 1)
                mod_tile(4 + h)

            pe.wait_ge(lo_done, SPLITS["attn", 3] + 1)
            for j in range(KD):
                done(project(open_tile("attn_o", j), SPLIT0["wo"], j * 4 * B, B, range(4),
                             lambda k: (att_hi[:, k, :], att_lo[:, k, :])))
            sums = [0]

            def sum_squares(j, buf, first, last_one):
                sums[0] += 1
                pe.wait_ge(sq_done, SQ0 + sums[0])
                ins = mm(psum[:, 7, :], ones[:], buf[:, j % 2, :], start=first, stop=last_one)
                ins.then_inc(sq_summed, 1)

            SQ0 = 2 + QL + 2 * KL
            for j in range(KD):
                o = open_tile("merged", j)
                pe.wait_ge(lo_done, SPLITS["m", KD - 1] + 1)
                done(project(o, SPLIT0["w_out"], j * 8 * B, B, ks, lambda k: (m_hi[:, k, :], m_lo[:, k, :])))
                if j >= 1:
                    sum_squares(j - 1, sq, j == 1, False)
            sum_squares(KD - 1, sq, False, True)

            o = open_tile("logits")
            pe.wait_ge(h2_done, KD)
            for t in range(TT):
                for k in range(KD):
                    last = mm(o[:, t * NE:(t + 1) * NE], h2[:, k, t * P:(t + 1) * P], router[:, k, :],
                              start=k == 0, stop=k == KD - 1)
            done(last)
            o = open_tile("aff_t")
            pe.wait_ge(aff_done, 1)
            for t in range(TT):
                last = nc.tensor.transpose(o[0:NE, t * P:(t + 1) * P], aff[:, t, :], ident[:])
            done(last)
            for t in range(TT):
                for half in range(2):
                    o = open_tile("h2_tok", t, half)
                    for k in range(4):
                        last = nc.tensor.transpose(o[:, k * P:(k + 1) * P], h2[:, half * 4 + k, t * P:(t + 1) * P],
                                                   ident[:])
                    done(last)
            o = open_tile("slots_tok")
            pe.wait_ge(slots_done, 1)
            for t in range(TT):
                last = nc.tensor.transpose(o[:, t * NE:(t + 1) * NE], slots[:, t * P:(t + 1) * P], ident[0:NE, 0:NE])
            done(last)
            o = open_tile("gates")
            pe.wait_ge(picks_done, TT)
            for i in range(PAIRS):
                for t in range(TT):
                    last = mm(o[:, i * NE:(i + 1) * NE], pick_tok[:, t, i * P:(i + 1) * P].bitcast(F32), aff[:, t, :],
                              start=t == 0, stop=t == TT - 1)
            done(last)
            pe.wait_ge(lo_done, SPLITS["h2_tok", TT - 1, 1] + 1)
            for k in range(KD):
                for half in range(2):
                    o = open_tile("xe", k, half)
                    for t in range(TT):
                        x = pick_tok[:, t, half * T:(half + 1) * T]
                        ch = slice(k * P, k * P + P)
                        mm(o, h2t_hi[:, t, ch], x, start=t == 0, stop=False)
                        last = mm(o, h2t_lo[:, t, ch], x, start=False, stop=t == TT - 1)
                    done(last)
            pe.wait_ge(pick_in, 16)
            for i in range(PAIRS):
                o = open_tile("onehot", i)
                done(mm(o, pick[:, i * P:(i + 1) * P], slots[:], start=True, stop=True))

            def raw_wait(n, i):
                pe.wait_ge(raw_full[n % NRAW], i * (16 * 12 // NRAW) + 16 * (n // NRAW + 1))
                return raw[:, n % NRAW, :]

            def gate_up(e, n, i, b):
                for part in range(2):
                    for f in range(FE):
                        if f % 2 == 0:
                            w = raw_wait(n + 2 * part + f // 2, i)
                        for k in range(KD):
                            last = mm(psum[:, b, part * 256 + f * CAP:part * 256 + (f + 1) * CAP],
                                      w[:, ((f % 2) * KD + k) * B:((f % 2) * KD + k + 1) * B],
                                      xe[:, k, bass.ds(i * (2 * CAP) + e * CAP, CAP)], start=k == 0, stop=k == KD - 1)
                done(last)

            def down(e, n, i, bs):
                rows = slice((e % 2) * CAP, (e % 2 + 1) * CAP)
                pe.wait_ge(act_done, i * 2 + e + 1)
                for half in range(2):
                    pe.wait_ge(lo_done, i * 4 + ye0 + 2 * e - 3 + half)
                    w = raw_wait(n + half, i)
                    for k in range(FE):
                        last = mm(psum[rows, bs[half], :], act_e[:, e % 2, k * CAP:(k + 1) * CAP],
                                  w[:, k * T:(k + 1) * T], start=k == 0, stop=k == FE - 1)
                    done(last)

            n0 = RAW0["experts"]
            ye0 = SPLITS["ye", 0, 0]
            pe.wait_ge(freed_act, PLAN.freed_count(TILE["xe", KD - 1, 1]))
            pe.wait_ge(freed_dve, PLAN.freed_count(TILE["onehot", PAIRS - 1]))
            gate_up(0, n0, 0, 0)

            def pair(i, last_pair):
                gate_up(1, n0 + 4, i, 1)
                down(0, n0 + 8, i, (2, 3))
                if last_pair:
                    down(1, n0 + 10, i, (4, 5))
                else:
                    gate_up(2, n0 + 10, i, 4)
                    down(1, n0 + 14, i, (5, 0))

            with pe.Fori(0, PAIRS - 1) as i:
                pair(i, False)
            pair(PAIRS - 1, True)

            pe.wait_ge(lo_done, SPLITS["ye", NE - 1, 1] + 1)
            for j in range(KD):
                o = open_tile("combine", j)
                ch = slice(j * P, j * P + P)
                for i in range(PAIRS):
                    mm(o, ye_hi[:, i, ch], place[:, i, :], start=i == 0, stop=False)
                    last = mm(o, ye_lo[:, i, ch], place[:, i, :], start=False, stop=i == PAIRS - 1)
                done(last)
                if j >= 1:
                    sum_squares(j - 1, sq, j == 1, False)
            sum_squares(KD - 1, sq, False, True)

            w2 = SPLIT0["w_in_2"]

            def gates(j):
                for g, name in enumerate(("lru_r", "lru_i")):
                    o = open_tile(name, j)
                    if g == 0:
                        pe.wait_ge(conv_done, j + 1)
                    done(mm(o, wab[:, g, j, :], conv_u[:, j % 2, :], start=True, stop=True))

            pe.wait_ge(lo_done, SPLITS["g", KD - 1] + 1)
            pe.wait_ge(wab_in, 16)
            for j in range(LRU):
                done(project(open_tile("lru_x", j), w2, j * 8 * B, B, ks, hx))
                if j >= 1:
                    gates(j - 1)
            for j in range(SC):
                for i, name in enumerate(("sc_c", "sc_x", "sc_b")):
                    done(project(open_tile(name, j), w2, (LRU + 3 * j + i) * 8 * B, B, ks, hx))
                    if i == 0 and j == 0:
                        gates(LRU - 1)
            for j in range(LRU):
                done(project(open_tile("lru_gate", j), w2, (LRU + 3 * SC + j) * 8 * B, B, ks, hx))
            for j in range(KD):
                o = open_tile("mix_o", j)
                if j == 0:
                    pe.wait_ge(lo_done, SPLITS["y_sc", SC - 1] + 1)
                    pe.wait_ge(lo_done, SPLITS["y_lru", LRU - 1] + 1)
                done(project(o, SPLIT0["w_out_2"], j * 12 * B, B, range(12),
                             lambda k: (ysc_hi[:, k, :], ysc_lo[:, k, :]) if k < SC
                             else (ylru_hi[:, k - SC, :], ylru_lo[:, k - SC, :])))
                if j >= 1:
                    sum_squares(j - 1, sq, j == 1, False)
            sum_squares(KD - 1, sq, False, True)

            pe.wait_ge(lo_done, SPLITS["g2", KD - 1] + 1)
            ffc = SPLIT0["ffn"]

            def bank_free(q, t):
                t -= 5
                if t < 0:
                    pe.wait_ge(resid_done, q * KD + 3 * KD + t + KD + 1)
                elif t < 2 * FQ:
                    pe.wait_ge((accg_done, accu_done)[t % 2], q * FQ + t // 2 + 1)
                else:
                    pe.wait_ge(resid_done, q * KD + 4 * KD + t - 2 * FQ + 1)

            def quarter(q):
                got = [0]

                def ww(off):
                    c, o = off // CH, off % CH
                    if c + 1 > got[0]:
                        pe.wait_ge(w_lo_done, q * FFN_CHUNKS + ffc + c + 1)
                        got[0] = c + 1
                    return w_hi[:, (ffc + c) % NHL, o:o + B], w_lo[:, (ffc + c) % NHL, o:o + B]

                for t in range(FFN_TILES):
                    bank_free(q, t)
                    o = psum[:, t % 5, :]
                    if t < 2 * FQ:
                        for k in range(KD):
                            last = mm3(o, ww((t * KD + k) * B), hx(k), k == 0, k == KD - 1)
                    else:
                        j = t - 2 * FQ
                        if j == 0:
                            pe.wait_ge(lo_done, q * FQ + SPLITS["ff", 0, FQ - 1] + 1)
                        for k in range(FQ):
                            last = mm3(o, ww((2 * FQ * KD + j * FQ + k) * B), (ff_hi[:, k, :], ff_lo[:, k, :]),
                                       k == 0, k == FQ - 1)
                    done(last)

            with pe.Fori(0, QUARTERS - 1) as q:
                quarter(q)
            quarter(QUARTERS - 1)
            for j in range(KD):
                sum_squares(j, sq_last, j == 0, j == KD - 1)

        @block.scalar
        def _(act):
            A = nc.scalar.activation
            chain = [0]

            nsplit = [0]

            def split_weights(t):
                while nsplit[0] < NSPLIT and SPLIT_DUE[nsplit[0]] <= t:
                    c = nsplit[0]
                    n = RAW_OF_SPLIT[c]
                    if SPLIT_DUE[c]:
                        act.wait_ge(tile_full, SPLIT_DUE[c])
                    act.wait_ge(raw_full[n % NRAW], 16 * (n // NRAW + 1))
                    A(w_hi[:, c % NHL, :], raw[:, n % NRAW, :], ACT.Copy).then_inc(w_hi_done, 1)
                    nsplit[0] += 1

            def take(*name):
                split_weights(TILE[name])
                full(act, *name)
                return bank(*name)

            def hi(dst, src, **kw):
                A(dst, src, ACT.Identity if "bias" in kw else ACT.Copy, **kw).then_inc(hi_done, 1)

            pres = [0]

            def hi_of_pre(dst, src, **kw):
                pres[0] += 1
                act.wait_ge(pre_done, pres[0])
                hi(dst, src, **kw)

            act.wait_ge(consts_in, 16 * 7)
            A(csil, col("cond", 0, 16), ACT.Silu).then_inc(silu_done, 1)
            act.wait_ge(x_in, 32)
            A(sq_x0[:], x0[:], ACT.Square).then_inc(sq_done, 1)
            A(sq_c0[:], c0[:], ACT.Square).then_inc(sq_done, 1)
            act.wait_ge(z_done, 1)
            A(rstd_x0[:], take("ssq_x"), ACT.Sqrt, bias=eps, scale=1.0 / D).then_inc(freed_act, 1)
            A(rstd_c0[:], take("ssq_ctx")[:, 0:TC], ACT.Sqrt, bias=eps, scale=1.0 / D).then_inc(freed_act, 1)
            A(dftc_hi[:], dftc[:], ACT.Copy).then_inc(act_seq, 1)
            for g in range(4):
                split_weights(TILE["mod", g])
            for j in range(KD):
                hi_of_pre(h_hi[:, j, :], pre[:, j % 2, :], bias=mod[:, j, 0:1])
            for j in range(KD):
                hi_of_pre(hc_hi[:, j, :], pre[:, j % 2, 0:TC], bias=mod[:, j, 1:2])

            def square(dst, src):
                A(dst, src, ACT.Square).then_inc(sq_done, 1)

            for j in range(QL):
                square(sq_q[:, j, :], take("cq", j))
            for j in range(KL):
                square(sq_kv[:, j, 0:T], take("ckv", j, 0))
                square(sq_kv[:, j, T:TK], take("ckv", j, 1)[:, 0:TC])
            A(sqk[NOPE:QK, 0:T], take("kpe", 0)[0:ROPE, :], ACT.Square).then_inc(act_seq, 1)
            A(sqk[NOPE:QK, T:TK], take("kpe", 1)[0:ROPE, 0:TC], ACT.Square).then_inc(act_seq, 1)
            hi(f_hi[:, 0, :], take("f", 0))
            hi(f_hi[:, 1, :], take("f", 1))
            A(rstd_cq[:], take("ssq_cq"), ACT.Sqrt, bias=eps, scale=1.0 / (QL * P)).then_inc(freed_act, 1)
            A(rstd_ckv[:, 0:T], take("ssq_ckv", 0), ACT.Sqrt, bias=eps, scale=1.0 / (KL * P)).then_inc(freed_act, 1)
            A(rstd_ckv[:, T:TK], take("ssq_ckv", 1)[:, 0:TC], ACT.Sqrt, bias=eps,
              scale=1.0 / (KL * P)).then_inc(freed_act, 1)
            for j in range(QL):
                hi_of_pre(cq_hi[:, j, :], cqg[:, j, :])
            for j in range(KL):
                hi_of_pre(ckv_hi[:, j, :], ckvg[:, j, :])
            hi(f_hi[:, 2, :], take("f", 2))
            hi(f_hi[:, 3, :], take("f", 3))
            for g in range(NF + 1):
                if g < NF:
                    for half in range(2):
                        o = take("f_ch", g, half)
                        if g == 0:
                            act.wait_ge(lo_done, SPLITS["ckv", KL - 1] + 1)
                        if g >= 2:
                            full(act, "four", g - 2)
                        hi(fc_hi[:, g % 2, half, :, :], o.rearrange("p (t c) -> p t c", t=2))
                if g >= 1:
                    hi(f_hi[:, g - 1, :], take("four", g - 1))
            full(act, "four", NF - 1)
            for j in range(KD):
                A(ga[:, j, :], take("ga", j), ACT.Sigmoid).then_inc(freed_act, 1)
            for j in range(KD):
                o = take("gb", j)
                if j >= 2:
                    act.wait_ge(resid_done, j - 1)
                A(sg[j % 2][:], o, ACT.Sigmoid).then_inc(freed_act, 1)
                split_weights(TILE["four_o", j])
            for t in range(KT):
                A(v[:, t, :, 0:3:2, :], take("v", t).rearrange("p (g s d) -> p g s d", g=H // 2, s=2), ACT.Copy).then_inc(freed_act, 1)

            def prep_a(h):
                o = take("uq", h)
                if h >= 1:
                    act.wait_ge(pre_done, PRE_Q + 2 * h)
                    full(act, "rot_q", h - 1)
                A(sqq[:], o[0:QK, :], ACT.Square)
                A(qg[:], o[0:QK, :], ACT.Copy, scale=cols[0:QK, COLS["q_norm_g"]:COLS["q_norm_g"] + 1]).then_inc(qk_raw, 1)
                for s in range(2):
                    o = take("uk", h, s)[0:NOPE, 0:TC if s else T]
                    w = slice(0, T) if s == 0 else slice(T, TK)
                    A(sqk[0:NOPE, w], o, ACT.Square)
                    last = A(kraw[0:NOPE, w], o, ACT.Copy, scale=cols[0:NOPE, COLS["k_norm_g"]:COLS["k_norm_g"] + 1])
                last.then_inc(qk_raw, 1)

            def prep_b(h):
                o = take("ssq_q", h)
                if h >= 1:
                    act.wait_ge(lo_done, SPLITS["k", h - 1] + 1)
                A(rq[:], o[0:QK, :], ACT.Sqrt, bias=eps[0:QK, :], scale=1.0 / QK).then_inc(freed_act, 1)
                for s in range(2):
                    o = take("ssq_k", h, s)[0:QK, 0:TC if s else T]
                    w = slice(0, T) if s == 0 else slice(T, TK)
                    A(rk[:, w], o, ACT.Sqrt, bias=eps[0:QK, :], scale=1.0 / QK).then_inc(freed_act, 1)
                split_weights(TILE["rot_q", h])
                if h >= 1:
                    full(act, "sT", h - 1, KT - 1)
                hi_of_pre(q_hi[0:QK, :], rq[:])
                hi_of_pre(k_hi[0:QK, :], rk[:])

            act.wait_ge(resid_done, KD)
            prep_a(0)
            prep_b(0)
            for h in range(H):
                if h + 1 < H:
                    prep_a(h + 1)
                A(q_hi[QK:QK + 1, :], take("mx_row", h)[0:1, :], ACT.Copy, scale=-1.0).then_inc(freed_act, 1)
                for k in range(KT):
                    A(probs[:, k % 3, :], take("sT", h, k), ACT.Exp, scale=QK ** -0.5).then_inc(freed_act, 1)
                if h + 1 < H:
                    prep_b(h + 1)
                split_weights(TILE["mod", 4 + h])

            act.wait_ge(o_full, H)
            act.dma_start(x1[:], x_d).then_inc(x_again, 16)
            for j in range(4):
                act.wait_ge(o_freed, min(2 * j + 2, H))
                hi(att_hi[:, j, :], att[:, j, :])
            for j in range(KD):
                split_weights(TILE["attn_o", j])
                if j >= 1:
                    hi_of_pre(m_hi[:, j - 1, :], m_tmp[:, (j - 1) % 2, :])
            hi_of_pre(m_hi[:, KD - 1, :], m_tmp[:, (KD - 1) % 2, :])

            nsq = [0]

            def residual_squares(names, buf, base):
                for j in range(KD):
                    if names is not None:
                        split_weights(TILE[names, j])
                    act.wait_ge(resid_done, base + j + 1)
                    if nsq[0] >= 2:
                        act.wait_ge(sq_summed, nsq[0] - 1)
                    nsq[0] += 1
                    A(buf[:, j % 2, :], x1[:, j, :], ACT.Square).then_inc(sq_done, 1)
                if names is not None:
                    split_weights(TILE[names, KD - 1] + 1)
                act.wait_ge(sq_summed, nsq[0])
                A(rstd[:], psum[:, 7, :], ACT.Sqrt, bias=eps, scale=1.0 / D).then_inc(std_done, 1)

            residual_squares("merged", sq, KD)

            full(act, "logits")
            act.wait_ge(logit_max, 1)
            A(aff[:], aff[:], ACT.Exp).then_inc(aff_exp, 1)
            act.wait_ge(slots_done, 1)
            act.dma_start(pick[:], pick_d).then_inc(pick_in, 16)
            for t in range(TT):
                for half in range(2):
                    hi(h2t_hi[:, t, half * T:(half + 1) * T], take("h2_tok", t, half))
            for k in range(KD):
                for half in range(2):
                    A(xe[:, k, half * T:(half + 1) * T], take("xe", k, half), ACT.Copy).then_inc(freed_act, 1)
            g0 = TILE["gu", 0]

            def ye_round(e, i, tile):
                rows = slice((e % 2) * CAP, (e % 2 + 1) * CAP)
                for half in range(2):
                    act.wait_ge(tile_full, i * 6 + tile + half + 1)
                    dst = ye_hi[rows, i, half * T:(half + 1) * T] if isinstance(i, int) else \
                        ye_hi[rows, bass.ds(i, 1), half * T:(half + 1) * T].rearrange("p a c -> p (a c)")
                    hi(dst, psum[rows, (tile + half - g0) % 6, :],
                       scale=gcol[rows, i:i + 1] if isinstance(i, int) else gcol[rows, bass.ds(i, 1)])

            nc.scalar.preload_act_table(ACT.Silu)
            act.wait_ge(freed_dve, PLAN.freed_count(TILE["gates"]))
            full(act, "gu", 0)
            A(gate_s[:, 0, :], psum[:, 0, 0:256], ACT.Silu).then_inc(silu_e, 1)

            def pair(i, last_pair):
                act.wait_ge(tile_full, i * 6 + g0 + 2)
                A(gate_s[:, 1, :], psum[:, 1, 0:256], ACT.Silu).then_inc(silu_e, 1)
                ye_round(0, i, g0 + 2)
                if not last_pair:
                    act.wait_ge(tile_full, i * 6 + g0 + 5)
                    A(gate_s[:, 0, :], psum[:, 4, 0:256], ACT.Silu).then_inc(silu_e, 1)
                    ye_round(1, i, g0 + 5)
                else:
                    ye_round(1, i, g0 + 4)

            with act.Fori(0, PAIRS - 1) as i:
                pair(i, False)
            pair(PAIRS - 1, True)
            residual_squares("combine", sq, 2 * KD)
            act.dma_start(wab[:], wab_d).then_inc(wab_in, 16)

            for j in range(KD):
                hi_of_pre(h_hi[:, j, :], g_pre[:, j % 2, :])

            def lru_gates(j):
                o = take("lru_r", j)
                if j >= 1:
                    act.wait_ge(v_ready, j)
                A(e_r[:], o, ACT.Exp, bias=nba[:, j:j + 1], scale=-1.0).then_inc(freed_act, 1)
                A(e_i[:], take("lru_i", j), ACT.Exp, bias=nbx[:, j:j + 1], scale=-1.0).then_inc(freed_act, 1)
                act.wait_ge(ri_done, j + 1)
                A(lru_a[:, j, :], e_r[:], ACT.Exp, scale=nc8[:, j:j + 1]).then_inc(act_seq, 1)
                A(a_th[:], e_r[:], ACT.Tanh, scale=c8[:, j:j + 1])
                act.wait_ge(act_seq, 4 + j + 1)
                A(a_sq[:], lru_a[:, j, :], ACT.Square).then_inc(av_done, 1)

            act.wait_ge(sp_done, 1)
            A(sp_z, sp_z, ACT.Exp, scale=-1.0).then_inc(act_seq, 1)
            for j in range(LRU):
                split_weights(TILE["lru_x", j])
                if j >= 1:
                    lru_gates(j - 1)
            for j in range(SC):
                o = take("sc_c", j)
                if j >= 1:
                    full(act, "sc_x", j - 1)
                    act.wait_ge(freed_dve, PLAN.freed_count(TILE["sc_x", j - 1]))
                else:
                    full(act, "lru_i", LRU - 1)
                A(sc_c[:], o, ACT.Copy).then_inc(freed_act, 1)
                if j == 0:
                    lru_gates(LRU - 1)
                split_weights(TILE["sc_x", j])
                split_weights(TILE["sc_b", j])
                act.wait_ge(pre_done, PRE_SC + j + 1)
                hi(ysc_hi[:, j, :], sc_y[:])
                if j == 0:
                    act.wait_ge(v_ready, LRU)
                    for i in range(LRU):
                        A(lru_v[:, i, :], lru_v[:, i, :], ACT.Sqrt).then_inc(mult_done, 1)
            for j in range(LRU):
                o = take("lru_gate", j)
                if j >= 2:
                    act.wait_ge(pre_done, PRE_SC + SC + j - 1)
                else:
                    act.wait_ge(lo_done, SPLITS["y_sc", SC - 1] + 1)
                A(gl[:, j % 2, :], o, ACT.Gelu_apprx_tanh).then_inc(freed_act, 1)
                if j >= 1:
                    act.wait_ge(pre_done, PRE_SC + SC + j)
                    hi(ylru_hi[:, j - 1, :], y_pre[:, (j - 1) % 2, :])
            act.wait_ge(pre_done, PRE_SC + SC + LRU)
            hi(ylru_hi[:, LRU - 1, :], y_pre[:, (LRU - 1) % 2, :])
            pres[0] = PRE_SC + SC + LRU
            residual_squares("mix_o", sq, 3 * KD)

            for j in range(KD):
                hi_of_pre(h_hi[:, j, :], ff_pre[:, j % 2, :])
            nc.scalar.preload_act_table(ACT.Gelu_apprx_tanh)
            cw = COLS["ffn_conv_w_2"]
            pf = PRE_FF
            assert pres[0] == pf
            for q in range(QUARTERS):
                for i in range(FQ):
                    g = q * FQ + i
                    for half, name, acc in ((0, "ff_g", acc_g), (1, "ff_u", acc_u)):
                        o = take(name, q, i)
                        wcol = cols[:, cw + half * 3 * FF + 2 * FF + g:cw + half * 3 * FF + 2 * FF + g + 1]
                        if g >= 2:
                            act.wait_ge(pre_done, pf + g - 1)
                        A(acc[:, g % 2, :], o, ACT.Copy, scale=wcol).then_inc(acc_done, 1)
                    act.wait_ge(accg_done, g + 1)
                    A(ff_gl[:, g % 2, :], acc_g[:, g % 2, :], ACT.Gelu_apprx_tanh).then_inc(glu_done, 1)
                    act.wait_ge(pre_done, pf + g + 1)
                    if i == 0 and q >= 1:
                        full(act, "ff_o", q - 1, KD - 1)
                    hi(ff_hi[:, i, :], ff_pre[:, g % 2, :])
                for j in range(KD):
                    split_weights(TILE["ff_o", q, j])
            residual_squares(None, sq_last, 7 * KD)
            for j in range(KD):
                act.wait_ge(y_done, 1 + j)
                act.dma_start(out[:, j, :], y_out[:, j, :]).then_inc(out_done, 16)

        @block.vector
        def _(dve):
            V = nc.vector
            n = [0]

            def link(ins):
                n[0] += 1
                ins.then_inc(dve_seq, 1)
                dve.wait_ge(dve_seq, n[0])

            def pre_(ins):
                ins.then_inc(pre_done, 1)

            def lo(dst, src, hi_part, *name):
                dve.wait_ge(hi_done, SPLITS[name] + 1)
                return V.tensor_tensor(dst, src, hi_part.bitcast(F32), ALU.subtract)

            def take(*name):
                full(dve, *name)
                return bank(*name)

            def free(ins):
                ins.then_inc(freed_dve, 1)

            V.memset(eps, EPS).then_inc(z_done, 1)
            dve.wait_ge(consts_in, 16 * 7)
            dve.wait_ge(x_in, 32)

            def mod_evac(g):
                b = cols[:, COLS["b_mod"] + 4 * g:COLS["b_mod"] + 4 * g + 4].unsqueeze(2).to_broadcast([P, 4, 2])
                free(V.tensor_tensor(mod[:, 4 * g:4 * g + 4, :], take("mod", g)[:, 0:8].rearrange("p (m c) -> p m c", c=2),
                                     b, ALU.add))
                dve.wait_ge(freed_dve, PLAN.freed_count(TILE["mod", g]))

            dve.wait_ge(freed_act, 2)
            link(V.reciprocal(rstd_x0[:], rstd_x0[:]))
            link(V.reciprocal(rstd_c0[:], rstd_c0[:]))
            dve.wait_ge(act_seq, 1)
            link(V.tensor_tensor(dftc_lo[:], dftc[:], dftc_hi[:].bitcast(F32), ALU.subtract))
            for g in range(4):
                mod_evac(g)
            for i, a in ((0, a1), (1, a1c)):
                link(V.scalar_tensor_tensor(out=a, in0=mod[:, KD:2 * KD, i], scalar=1.0, in1=col("norm1_g", 0, KD),
                                            op0=ALU.add, op1=ALU.mult))

            def norm(count, pre_of, mk_pre, mk_lo):
                for j in range(count + 1):
                    if j < count:
                        pre_(mk_pre(j))
                    if j >= 1:
                        mk_lo(j - 1).then_inc(lo_done, 1)

            def mk0(src, a, r, w):
                def f(j):
                    if j >= 2:
                        dve.wait_ge(lo_done, SPLITS[w, j - 2] + 1)
                    elif w == "hc":
                        dve.wait_ge(lo_done, SPLITS["h", KD - 2 + j] + 1)
                    return V.scalar_tensor_tensor(out=pre[:, j % 2, 0:src.shape[2]], in0=src[:, j, :], scalar=a[:, j:j + 1],
                                                  in1=r[:], op0=ALU.mult, op1=ALU.mult)
                return f

            def lo0(dst, hi_t, i, w, width):
                def f(j):
                    dve.wait_ge(hi_done, SPLITS[w, j] + 1)
                    return V.scalar_tensor_tensor(out=dst[:, j, :], in0=pre[:, j % 2, 0:width], scalar=mod[:, j, i:i + 1],
                                                  in1=hi_t[:, j, :].bitcast(F32), op0=ALU.add, op1=ALU.subtract)
                return f

            norm(KD, None, mk0(x0, a1, rstd_x0, "h"), lo0(h_lo, h_hi, 0, "h", T))
            norm(KD, None, mk0(c0, a1c, rstd_c0, "hc"), lo0(hc_lo, hc_hi, 1, "hc", TC))

            nsq = 2
            for j in range(QL):
                o = take("cq", j)
                nsq += 1
                dve.wait_ge(sq_done, nsq)
                free(V.tensor_scalar(cqg[:, j, :], o, col("q_a_norm_g", j), None, ALU.mult))
            for j in range(KL):
                for s in range(2):
                    o = take("ckv", j, s)
                    nsq += 1
                    dve.wait_ge(sq_done, nsq)
                    w = slice(0, T) if s == 0 else slice(T, TK)
                    free(V.tensor_scalar(ckvg[:, j, w], o[:, 0:TC if s else T], col("kv_a_norm_g", j), None, ALU.mult))
            for s in range(2):
                o = take("kpe", s)
                dve.wait_ge(act_seq, 2 + s)
                w = slice(0, T) if s == 0 else slice(T, TK)
                free(V.tensor_scalar(kraw[NOPE:QK, w], o[0:ROPE, 0:TC if s else T],
                                     cols[NOPE:QK, COLS["k_norm_g"]:COLS["k_norm_g"] + 1], None, ALU.mult))
            dve.wait_ge(freed_dve, PLAN.freed_count(TILE["kpe", 1]))

            def evac_lo(dst, hi_part, *name):
                o = take(*name)
                dve.wait_ge(hi_done, SPLITS[name] + 1)
                V.tensor_tensor(dst, o, hi_part.bitcast(F32), ALU.subtract).then_inc(lo_done, 1)

            evac_lo(f_lo[:, 0, :], f_hi[:, 0, :], "f", 0)
            evac_lo(f_lo[:, 1, :], f_hi[:, 1, :], "f", 1)
            dve.wait_ge(freed_act, PLAN.freed_count(TILE["ssq_ckv", 1]))
            link(V.reciprocal(rstd_cq[:], rstd_cq[:]))
            link(V.reciprocal(rstd_ckv[:], rstd_ckv[:]))
            for src, dst, hi_t, r, name, cnt in ((cqg, cq_lo, cq_hi, rstd_cq, "cq", QL),
                                                 (ckvg, ckv_lo, ckv_hi, rstd_ckv, "ckv", KL)):
                norm(cnt, None, lambda j: V.tensor_tensor(src[:, j, :], src[:, j, :], r[:], ALU.mult),
                     lambda j: lo(dst[:, j, :], src[:, j, :], hi_t[:, j, :], name, j))
            evac_lo(f_lo[:, 2, :], f_hi[:, 2, :], "f", 2)
            evac_lo(f_lo[:, 3, :], f_hi[:, 3, :], "f", 3)
            o = take("rot_k")
            link(V.tensor_tensor(rk[NOPE:QK, 0:T], o[NOPE:QK, :], rope_cs[NOPE:QK, 1, :], ALU.mult))
            link(V.tensor_tensor(kraw[NOPE:QK, 0:T], kraw[NOPE:QK, 0:T], rope_cs[NOPE:QK, 0, :], ALU.mult))
            free(V.tensor_tensor(kraw[NOPE:QK, 0:T], kraw[NOPE:QK, 0:T], rk[NOPE:QK, 0:T], ALU.add))
            for g in range(NF + 1):
                if g < NF:
                    for half in range(2):
                        o = take("f_ch", g, half)
                        dve.wait_ge(hi_done, SPLITS["f_ch", g, half] + 1)
                        V.tensor_tensor(fc_lo[:, g % 2, half, :, :], o.rearrange("p (t c) -> p t c", t=2),
                                        fc_hi[:, g % 2, half, :, :].bitcast(F32), ALU.subtract).then_inc(lo_done, 1)
                if g >= 1:
                    evac_lo(f_lo[:, g - 1, :], f_hi[:, g - 1, :], "four", g - 1)
            for j in range(KD):
                o = take("four_o", j)
                dve.wait_ge(freed_act, PLAN.freed_count(TILE["gb", j]))
                V.tensor_tensor(gbf[:, j, :], o, sg[j % 2][:], ALU.mult).then_inc(resid_done, 1)
            full(dve, "four_o", KD - 1)
            V.memset(v[:, :, :, 1, :], 1.0).then_inc(v_done, 1)
            V.memset(k_hi[QK:QK + 1, :].bitcast(F32), 1.0)
            V.memset(k_lo[QK:QK + 1, :].bitcast(F32), 0.0)
            V.memset(q_lo[QK:QK + 1, :].bitcast(F32), 0.0).then_inc(v_done, 1)

            def final(h):
                dve.wait_ge(freed_act, PLAN.freed_count(TILE["ssq_k", h, 1]))
                link(V.reciprocal(rq[:], rq[:]))
                link(V.reciprocal(rk[:], rk[:]))
                o = take("rot_q", h)
                free(V.tensor_tensor(tmp_a[NOPE:QK, :], o[NOPE:QK, :], rope_cs[NOPE:QK, 1, :], ALU.mult))
                link(V.tensor_tensor(qg[NOPE:QK, :], qg[NOPE:QK, :], rope_cs[NOPE:QK, 0, :], ALU.mult))
                dve.wait_ge(freed_dve, PLAN.freed_count(TILE["rot_q", h]))
                link(V.tensor_tensor(qg[NOPE:QK, :], qg[NOPE:QK, :], tmp_a[NOPE:QK, :], ALU.add))
                pre_(V.tensor_tensor(rq[:], qg[:], rq[:], ALU.mult))
                pre_(V.tensor_tensor(rk[:], kraw[:], rk[:], ALU.mult))
                lo(q_lo[0:QK, :], rq[:], q_hi[0:QK, :], "q", h).then_inc(lo_done, 1)
                lo(k_lo[0:QK, :], rk[:], k_hi[0:QK, :], "k", h).then_inc(lo_done, 1)

            final(0)
            KH = TK // 2
            for h in range(H):
                for q in range(TT):
                    for s in range(2):
                        o = take("mx", h, q, s)
                        free(V.tensor_reduce(mx2[:, 2 * q + s:2 * q + s + 1], o[:, 0:KH], AX.X, ALU.max))
                dve.wait_ge(freed_dve, PLAN.freed_count(TILE["mx", h, TT - 1, 1]))
                V.tensor_reduce(mxq, mx2.rearrange("p (q s) -> p q s", s=2), AX.X, ALU.max).then_inc(mx_done, 1)
                if h + 1 < H:
                    final(h + 1)
                dve.wait_ge(o_full, h + 1)
                o = psum[:, 6 + h % 2, :]
                r0 = (h % 2) * VD
                link(V.reciprocal(rs[r0:r0 + VD, :], o[VD - r0:2 * VD - r0, :]))
                V.tensor_tensor(att[r0:r0 + VD, h // 2, :], o[r0:r0 + VD, :], rs[r0:r0 + VD, :], ALU.mult)\
                    .then_inc(o_freed, 1)
                mod_evac(4 + h)

            for j in range(4):
                lo(att_lo[:, j, :], att[:, j, :], att_hi[:, j, :], "attn", j).then_inc(lo_done, 1)
            link(V.scalar_tensor_tensor(out=a2, in0=mod[:, 4 * KD:5 * KD, 0], scalar=1.0, in1=col("norm2_g", 0, KD),
                                        op0=ALU.add, op1=ALU.mult))
            for j in range(KD + 1):
                if j < KD:
                    o = take("attn_o", j)
                    if j >= 2:
                        dve.wait_ge(lo_done, SPLITS["m", j - 2] + 1)
                    free(V.tensor_tensor(m_tmp[:, j % 2, :], o, ga[:, j, :], ALU.mult))
                    dve.wait_ge(freed_dve, PLAN.freed_count(TILE["attn_o", j]))
                    pre_(V.tensor_tensor(m_tmp[:, j % 2, :], m_tmp[:, j % 2, :], gbf[:, j, :], ALU.add))
                if j >= 1:
                    lo(m_lo[:, j - 1, :], m_tmp[:, (j - 1) % 2, :], m_hi[:, j - 1, :], "m", j - 1).then_inc(lo_done, 1)

            def residual(j, name, base, scale=None):
                o = take(*name)
                if scale is None:
                    ins = V.tensor_tensor(x1[:, j, :], o, x1[:, j, :], ALU.add)
                else:
                    ins = V.scalar_tensor_tensor(out=x1[:, j, :], in0=o, scalar=scale, in1=x1[:, j, :],
                                                 op0=ALU.mult, op1=ALU.add)
                ins.then_inc(resid_done, 1)

            stds = [0]

            def inverse():
                stds[0] += 1
                dve.wait_ge(std_done, stds[0])
                link(V.reciprocal(rstd[:], rstd[:]))

            dve.wait_ge(x_again, 16)
            for j in range(KD):
                residual(j, ("merged", j), KD, mod[:, 2 * KD + j, 0:1])
            inverse()

            for j in range(KD):
                link(V.scalar_tensor_tensor(out=h2[:, j, :], in0=x1[:, j, :], scalar=a2[:, j:j + 1], in1=rstd[:],
                                            op0=ALU.mult, op1=ALU.mult))
                V.tensor_scalar(h2[:, j, :], h2[:, j, :], mod[:, 3 * KD + j, 0:1], None, ALU.add).then_inc(h2_done, 1)
            lg = take("logits")[:, 0:TT * NE].rearrange("p (t e) -> p t e", t=TT)
            link(V.tensor_reduce(aff_m[:], lg, AX.X, ALU.max))
            V.tensor_tensor(aff[:], lg, aff_m[:].unsqueeze(2).to_broadcast([P, TT, NE]), ALU.subtract).then_inc(logit_max, 1)
            dve.wait_ge(aff_exp, 1)
            link(V.tensor_reduce(aff_s[:], aff[:], AX.X, ALU.add))
            link(V.reciprocal(aff_s[:], aff_s[:]))
            V.tensor_tensor(aff[:], aff[:], aff_s[:].unsqueeze(2).to_broadcast([P, TT, NE]), ALU.mult).then_inc(aff_done, 1)
            o = take("aff_t")
            link(V.tensor_copy(aff_t[:], o[0:NE, :]))
            free(V.tensor_copy(work[:], o[0:NE, :]))
            dve.wait_ge(freed_dve, PLAN.freed_count(TILE["aff_t"]))
            for r in range(CAP // 8):
                link(V.max(top8[:], work[:]))
                link(V.match_replace(out=work[:], in_to_replace=top8[:], in_values=work[:], imm_value=-1.0))
            link(V.tensor_scalar(chosen[:], work[:], 0.0, None, ALU.is_lt))
            link(V.memset(ones_row[:], 1.0))
            link(V.tensor_tensor_scan(slots[:], ones_row[:], chosen[:], 0.0, ALU.mult, ALU.add))
            link(V.tensor_tensor(slots[:], slots[:], chosen[:], ALU.mult))
            V.tensor_scalar(slots[:], slots[:], -1.0, None, ALU.add).then_inc(slots_done, 1)
            for t in range(TT):
                for half in range(2):
                    evac_lo(h2t_lo[:, t, half * T:(half + 1) * T], h2t_hi[:, t, half * T:(half + 1) * T], "h2_tok", t, half)
            free(V.tensor_copy(slots_tok[:], take("slots_tok")[:, 0:TT * NE].rearrange("p (t e) -> p t e", t=TT)))
            dve.wait_ge(freed_dve, PLAN.freed_count(TILE["slots_tok"]))
            for t in range(TT):
                V.tensor_tensor(pick_tok[:, t, :].rearrange("p (e c) -> p e c", e=NE),
                                slots_tok[:, t, :].unsqueeze(2).to_broadcast([P, NE, CAP]),
                                iota[:].unsqueeze(1).to_broadcast([P, NE, CAP]), ALU.is_equal).then_inc(picks_done, 1)
            o = take("gates")
            link(V.tensor_copy(gcol[0:CAP, :], o[0:CAP, 0:PAIRS * NE:NE + 2]))
            free(V.tensor_copy(gcol[CAP:P, :], o[CAP:P, 1:PAIRS * NE:NE + 2]))
            dve.wait_ge(freed_dve, PLAN.freed_count(TILE["gates"]))
            for i in range(PAIRS):
                free(V.tensor_scalar(place[:, i, :], take("onehot", i), col("slot"), None, ALU.is_equal))
            g0 = TILE["gu", 0]
            sp0 = SPLITS["ye", 0, 0]

            def expert_act(e, i, b, tile, silus):
                dve.wait_ge(tile_full, i * 6 + tile + 1)
                dve.wait_ge(silu_e, i * 2 + silus)
                V.tensor_tensor(act_e[:, e % 2, :], psum[:, b, 256:512], gate_s[:, e % 2, :], ALU.mult).then_inc(act_done, 1)

            def ye_lo_part(e, i, bs, splits):
                rows = slice((e % 2) * CAP, (e % 2 + 1) * CAP)
                for half in range(2):
                    dve.wait_ge(hi_done, i * 4 + splits + half + 1)
                    if isinstance(i, int):
                        hi_t, dst = (z[rows, i, half * T:(half + 1) * T] for z in (ye_hi, ye_lo))
                        g = gcol[rows, i:i + 1]
                    else:
                        hi_t, dst = (z[rows, bass.ds(i, 1), half * T:(half + 1) * T].rearrange("p a c -> p (a c)")
                                     for z in (ye_hi, ye_lo))
                        g = gcol[rows, bass.ds(i, 1)]
                    V.scalar_tensor_tensor(out=dst, in0=psum[rows, bs[half], :], scalar=g, in1=hi_t.bitcast(F32),
                                           op0=ALU.mult, op1=ALU.subtract).then_inc(lo_done, 1)

            expert_act(0, 0, 0, g0, 1)

            def pair(i, last_pair):
                expert_act(1, i, 1, g0 + 1, 2)
                ye_lo_part(0, i, (2, 3), sp0)
                if last_pair:
                    ye_lo_part(1, i, (4, 5), sp0 + 2)
                else:
                    expert_act(2, i, 4, g0 + 4, 3)
                    ye_lo_part(1, i, (5, 0), sp0 + 2)

            with dve.Fori(0, PAIRS - 1) as i:
                pair(i, False)
            pair(PAIRS - 1, True)
            for j in range(KD):
                residual(j, ("combine", j), 2 * KD, mod[:, 5 * KD + j, 0:1])

            lam = col("lru_lambda_2", 0, LRU)
            link(V.tensor_scalar(sp_s, lam, -1.0, None, ALU.mult))
            V.tensor_tensor(sp_z, lam, sp_s, ALU.max).then_inc(sp_done, 1)
            link(V.tensor_scalar(nba, col("lru_ba_2", 0, LRU), -1.0, None, ALU.mult))
            link(V.tensor_scalar(nbx, col("lru_bx_2", 0, LRU), -1.0, None, ALU.mult))

            inverse()

            def gain(src, dst, g, name):
                def f(j):
                    if j >= 2:
                        dve.wait_ge(lo_done, SPLITS[name, j - 2] + 1)
                    return V.scalar_tensor_tensor(out=dst[:, j % 2, :], in0=src[:, j, :], scalar=col(g, j), in1=rstd[:],
                                                  op0=ALU.mult, op1=ALU.mult)
                return f

            norm(KD, None, gain(x1, g_pre, "norm1_g_2", "g"),
                 lambda j: lo(h_lo[:, j, :], g_pre[:, j % 2, :], h_hi[:, j, :], "g", j))

            dve.wait_ge(act_seq, 4)
            link(V.tensor_scalar(sp_s2, sp_z, 2.0, None, ALU.add))
            link(V.reciprocal(sp_s2, sp_s2))
            link(V.tensor_tensor(sp_z, sp_z, sp_s2, ALU.mult))
            link(V.tensor_tensor(sp_s2, sp_z, sp_z, ALU.mult))
            link(V.memset(sp_p, 1.0 / 19))
            for k in range(17, 0, -2):
                link(V.tensor_tensor(sp_p, sp_p, sp_s2, ALU.mult))
                link(V.tensor_scalar(sp_p, sp_p, 1.0 / k, None, ALU.add))
            link(V.tensor_tensor(sp_p, sp_p, sp_z, ALU.mult))
            link(V.tensor_scalar(sp_s, sp_s, 0.0, None, ALU.max))
            link(V.scalar_tensor_tensor(out=sp_p, in0=sp_p, scalar=2.0, in1=sp_s, op0=ALU.mult, op1=ALU.add))
            link(V.tensor_scalar(c8, sp_p, 8.0, None, ALU.mult))
            link(V.tensor_scalar(nc8, sp_p, -8.0, None, ALU.mult))

            def lru_conv(j):
                o = take("lru_x", j)
                if j >= 2:
                    full(dve, "lru_i", j - 2)
                u = conv_u[:, j % 2, :]
                tap = lambda k: col("lru_conv_w_2", k * LRU + j)
                link(V.tensor_scalar(u, o, tap(3), col("lru_conv_b_2", j), ALU.mult, ALU.add))
                for k in (2, 1):
                    s = 3 - k
                    link(V.scalar_tensor_tensor(out=u[:, s:T], in0=o[:, 0:T - s], scalar=tap(k), in1=u[:, s:T],
                                                op0=ALU.mult, op1=ALU.add))
                V.scalar_tensor_tensor(out=u[:, 3:T], in0=o[:, 0:T - 3], scalar=tap(0), in1=u[:, 3:T],
                                       op0=ALU.mult, op1=ALU.add).then_inc(conv_done, 1)

            def lru_gates(j):
                dve.wait_ge(freed_act, PLAN.freed_count(TILE["lru_i", j]))
                link(V.tensor_scalar(e_r[:], e_r[:], 1.0, None, ALU.add))
                V.reciprocal(e_r[:], e_r[:]).then_inc(ri_done, 1)
                link(V.tensor_scalar(e_i[:], e_i[:], 1.0, None, ALU.add))
                link(V.reciprocal(e_i[:], e_i[:]))
                link(V.tensor_tensor(lru_b[:, j, :], e_i[:], conv_u[:, j % 2, :], ALU.mult))
                dve.wait_ge(av_done, j + 1)
                V.scalar_tensor_tensor(out=lru_v[:, j, :], in0=a_sq[:], scalar=1.0, in1=a_th[:],
                                       op0=ALU.add, op1=ALU.mult).then_inc(v_ready, 1)

            for j in range(LRU):
                lru_conv(j)
                if j >= 1:
                    lru_gates(j - 1)
            for j in range(SC):
                if j == 0:
                    lru_gates(LRU - 1)
                o = take("sc_x", j)
                dve.wait_ge(freed_act, PLAN.freed_count(TILE["sc_c", j]))
                free(V.tensor_tensor(sc_cx[:], o, sc_c[:], ALU.mult))
                dve.wait_ge(freed_dve, PLAN.freed_count(TILE["sc_x", j]))
                tap = lambda k: col("sc_conv_w_2", k * SC + j)
                link(V.tensor_scalar(sc_acc[:], sc_cx[:], tap(2), None, ALU.mult))
                for k in (1, 0):
                    s = 2 - k
                    link(V.scalar_tensor_tensor(out=sc_acc[:, s:T], in0=sc_cx[:, 0:T - s], scalar=tap(k),
                                                in1=sc_acc[:, s:T], op0=ALU.mult, op1=ALU.add))
                o = take("sc_b", j)
                pre_(V.tensor_tensor(sc_y[:], o, sc_acc[:], ALU.mult))
                lo(ysc_lo[:, j, :], sc_y[:], ysc_hi[:, j, :], "y_sc", j).then_inc(lo_done, 1)
                dve.wait_ge(lo_done, SPLITS["y_sc", j] + 1)
            for j in range(LRU):
                dve.wait_ge(mult_done, j + 1)
                link(V.tensor_tensor(lru_b[:, j, :], lru_b[:, j, :], lru_v[:, j, :], ALU.mult))
                link(V.tensor_tensor_scan(lru_v[:, j, :], lru_a[:, j, :], lru_b[:, j, :], 0.0, ALU.mult, ALU.add))
            for j in range(LRU + 1):
                if j < LRU:
                    dve.wait_ge(freed_act, PLAN.freed_count(TILE["lru_gate", j]))
                    if j >= 2:
                        dve.wait_ge(lo_done, SPLITS["y_lru", j - 2] + 1)
                    pre_(V.tensor_tensor(y_pre[:, j % 2, :], lru_v[:, j, :], gl[:, j % 2, :], ALU.mult))
                if j >= 1:
                    lo(ylru_lo[:, j - 1, :], y_pre[:, (j - 1) % 2, :], ylru_hi[:, j - 1, :], "y_lru", j - 1)\
                        .then_inc(lo_done, 1)
            for j in range(KD):
                residual(j, ("mix_o", j), 3 * KD)
            inverse()
            norm(KD, None, gain(x1, ff_pre, "norm2_g_2", "g2"),
                 lambda j: lo(h_lo[:, j, :], ff_pre[:, j % 2, :], h_hi[:, j, :], "g2", j))

            cw = COLS["ffn_conv_w_2"]
            for q in range(QUARTERS):
                for i in range(FQ + 1):
                    if i < FQ:
                        g = q * FQ + i
                        for half, name, acc in ((0, "ff_g", acc_g), (1, "ff_u", acc_u)):
                            tap = lambda k: cols[:, cw + half * 3 * FF + k * FF + g:cw + half * 3 * FF + k * FF + g + 1]
                            o = take(name, q, i)
                            dve.wait_ge(acc_done, 2 * g + half + 1)
                            a = acc[:, g % 2, :]
                            link(V.scalar_tensor_tensor(out=a[:, 1:T], in0=o[:, 0:T - 1], scalar=tap(1), in1=a[:, 1:T],
                                                        op0=ALU.mult, op1=ALU.add))
                            done_sem = (accg_done, accu_done)[half]
                            V.scalar_tensor_tensor(out=a[:, 2:T], in0=o[:, 0:T - 2], scalar=tap(0), in1=a[:, 2:T],
                                                   op0=ALU.mult, op1=ALU.add).then_inc(done_sem, 1)
                        dve.wait_ge(accu_done, g + 1)
                        dve.wait_ge(glu_done, g + 1)
                        if g >= 2:
                            p = SPLITS["ff", (g - 2) // FQ, (g - 2) % FQ]
                            dve.wait_ge(lo_done, p + 1)
                        pre_(V.tensor_tensor(ff_pre[:, g % 2, :], acc_u[:, g % 2, :], ff_gl[:, g % 2, :], ALU.mult))
                    if i >= 1:
                        g = q * FQ + i - 1
                        lo(ff_lo[:, i - 1, :], ff_pre[:, g % 2, :], ff_hi[:, i - 1, :], "ff", q, i - 1).then_inc(lo_done, 1)
                for j in range(KD):
                    residual(j, ("ff_o", q, j), (4 + q) * KD)
            inverse()
            for j in range(KD):
                V.scalar_tensor_tensor(out=y_out[:, j, :], in0=x1[:, j, :], scalar=col("final_g_2", j), in1=rstd[:],
                                       op0=ALU.mult, op1=ALU.mult).then_inc(y_done, 1)


def kernel(**inputs):
    import numpy as np
    import concourse.bacc as bacc
    from concourse.bass_utils import run_bass_kernel_spmd as run

    a = {k: np.ascontiguousarray(v) for k, v in inputs.items()}
    f = np.float32

    def tiles(w, m=B):
        k, n = w.shape
        return w.reshape(k // P, P, n // m, m).transpose(1, 2, 0, 3).reshape(P, -1)

    def rows(w):
        return w.reshape(-1, P, w.shape[1]).transpose(1, 0, 2).reshape(P, -1)

    def pad(parts, total):
        out = np.zeros((P, total), f)
        for off, p in parts:
            out[:, off:off + p.shape[1]] = p
        return out

    tt = np.arange(T)
    ang = 2 * np.pi * ((tt[:, None] * tt[None, :]) % T) / T
    norm = 1.0 / np.sqrt(T * P)
    dft = np.concatenate([rows(np.cos(ang).astype(f)), rows((-np.sin(ang)).astype(f))], axis=1)
    cc = np.arange(P)
    angc = 2 * np.pi * ((cc[:, None] * cc[None, :]) % P) / P
    dftc = np.concatenate([np.cos(angc) * norm, np.sin(angc) * norm], axis=1).astype(f)
    nfreq = ROPE // 4
    inv = (1.0 / (f(10000.0) ** (np.arange(nfreq, dtype=f) / f(nfreq)))).astype(f)
    rope = np.zeros((ROPE, 2, T), f)
    for axis, pos in enumerate((tt // 64, tt % 64)):
        an = (pos.astype(f)[:, None] * inv[None, :]).astype(f)
        an = np.concatenate([an, an], axis=1).T
        rope[axis * 16:axis * 16 + 16, 0] = np.cos(an)
        rope[axis * 16:axis * 16 + 16, 1] = np.sin(an)
    rot = np.zeros((QK, QK), f)
    for b0 in (NOPE, NOPE + 16):
        for i in range(8):
            rot[b0 + 8 + i, b0 + i] = -1.0
            rot[b0 + i, b0 + 8 + i] = 1.0
    pick = np.zeros((NE, PAIRS * P), f)
    for e in range(NE):
        pick[e, (e // 2) * P + (e % 2) * CAP:(e // 2) * P + (e % 2 + 1) * CAP] = 1.0
    iota = np.broadcast_to(np.arange(CAP, dtype=f), (P, CAP))

    w_mod = a["w_mod"][0]
    mod = tiles(w_mod)
    w_in = a["w_in"][0]
    offs = np.cumsum([0, 384, 256, 32, 512, 1024, 1024])
    wq, wkv, wkpe, wf, wga, wgb = (w_in[:, offs[i]:offs[i + 1]] for i in range(6))
    wqu, wkvu = a["w_q_up"][0], a["w_kv_up"][0].reshape(256, H, NOPE + VD)
    gb, wfo = tiles(wgb).reshape(P, KD, 8 * B), tiles(a["w_fourier"][0]).reshape(P, KD, 4 * B)
    parts = [(S1_QKV, tiles(wq)), (S1_QKV + QL * 8 * B, tiles(wkv)), (S1_KPE, rows(wkpe)), (S1_F, tiles(wf)),
             (S1_DFT, dft), (S1_GA, tiles(wga)), (S1_GB, np.concatenate([gb, wfo], axis=2).reshape(P, -1)),
             (S1_V, rows(wkvu[:, :, NOPE:].reshape(256, H * VD)))]
    for h in range(H):
        o = S1_HEADS + (h // 4) * CH + (h % 4) * HEAD_W
        parts.append((o, rows(wqu[:, h * QK:(h + 1) * QK])))
        parts.append((o + QL * QK, rows(wkvu[:, h, :NOPE])))
    s1 = pad(parts, 20 * CH)
    wg, wu, wd = a["w_e_gate"][0], a["w_e_up"][0], a["w_e_down"][0]

    def gate_up(e):
        return [tiles(wg[e]), tiles(wu[e])]

    def down(e):
        return [rows(wd[e][:, :T]), rows(wd[e][:, T:])]

    ex = gate_up(0)
    for e in range(NE):
        if e + 1 < NE:
            ex += gate_up(e + 1)
        ex += down(e)
    w2 = a["w_in_2"][0]
    cols2 = [w2[:, :1024]]
    for j in range(SC):
        cols2 += [w2[:, 2560 + j * P:2560 + (j + 1) * P], w2[:, 3072 + j * P:3072 + (j + 1) * P],
                  w2[:, 2048 + j * P:2048 + (j + 1) * P]]
    cols2.append(w2[:, 1024:2048])
    w2s = tiles(np.concatenate(cols2, axis=1))
    wo2 = a["w_out_2"][0]
    wo2 = tiles(np.concatenate([wo2[1024:], wo2[:1024]], axis=0))
    wup, wdn = a["w_up_2"][0], a["w_down_2"][0]
    up_g, up_u = (tiles(w).reshape(P, FF, 8 * B) for w in (wup[:, :3072], wup[:, 3072:]))
    ff = []
    for q in range(QUARTERS):
        for i in range(FQ):
            ff += [up_g[:, q * FQ + i], up_u[:, q * FQ + i]]
        ff.append(tiles(wdn[q * FQ * P:(q + 1) * FQ * P]))
    stream = np.concatenate([mod[:, :8 * CH], s1, mod[:, 8 * CH:], tiles(a["w_o_attn"][0]), tiles(a["w_out"][0])]
                            + ex + [w2s, wo2] + ff, axis=1)
    stream = np.ascontiguousarray(stream.reshape(P, -1, CH).transpose(1, 0, 2))
    assert stream.shape[0] == len(CHUNKS), (stream.shape, len(CHUNKS))

    cols = np.zeros((P, NCOLS), f)

    def put(name, vec):
        v2 = vec.reshape(-1, P).T
        cols[:, COLS[name]:COLS[name] + v2.shape[1]] = v2

    for name in ("norm1_g", "b_mod", "q_a_norm_g", "kv_a_norm_g", "norm2_g", "norm1_g_2", "lru_conv_w_2",
                 "lru_conv_b_2", "lru_ba_2", "lru_bx_2", "lru_lambda_2", "sc_conv_w_2", "norm2_g_2", "final_g_2"):
        put(name, a[name])
    put("ffn_conv_w_2", a["ffn_conv_w_2"][0].reshape(3, 2, 3072).transpose(1, 0, 2))
    cols[:QK, COLS["q_norm_g"]] = a["q_norm_g"][0]
    cols[:QK, COLS["k_norm_g"]] = a["k_norm_g"][0]
    cond = np.stack([a["c"][0].reshape(KD, P), a["c_ctx"].reshape(KD, P)], axis=1)
    cols[:, COLS["cond"]:COLS["cond"] + 16] = cond.reshape(16, P).T
    cols[:, COLS["slot"]] = np.arange(P) % CAP
    wab = np.zeros((P, 2, LRU, P), f)
    for g, name in enumerate(("lru_wa_2", "lru_wx_2")):
        w = a[name][0].reshape(LRU, 2, 64, 64)
        for s in range(2):
            wab[s * 64:(s + 1) * 64, g, :, s * 64:(s + 1) * 64] = w[:, s].transpose(1, 0, 2)

    def chan(x):
        return np.ascontiguousarray(x.T.reshape(KD, P, -1).transpose(1, 0, 2))

    arrays = {"stream": stream, "cols": cols, "x": chan(a["x"][0]), "ctx": chan(a["ctx"][0]),
              "router": np.ascontiguousarray(a["w_router"][0].reshape(KD, P, NE).transpose(1, 0, 2)), "wab": wab,
              "rope": rope, "rot": rot, "dftc": dftc, "ident": np.eye(P, dtype=f),
              "iota": np.ascontiguousarray(iota), "pick": pick}
    nc = bacc.Bacc("TRN2", target_bir_lowering=False, num_devices=1)
    aps = [nc.dram_tensor(f"in_{k}", v.shape, F32, kind="ExternalInput").ap() for k, v in arrays.items()]
    out = nc.dram_tensor("out", (P, KD, T), F32, kind="ExternalOutput").ap()
    build(nc, *aps, out)
    r = run(nc, [{f"in_{k}": v for k, v in arrays.items()}], core_ids=[0])
    y = r.results[0]["out"]
    return y.transpose(2, 1, 0).reshape(1, T, D)
```

```python
import concourse.bass as bass
from concourse import mybir
from contextlib import ExitStack

F32 = mybir.dt.float32
F32R = mybir.dt.float32r
I32 = mybir.dt.int32
ALU = mybir.AluOpType
ACT = mybir.ActivationFunctionType
AX = mybir.AxisListType

P = 128
T = 512
TC = 256
TK = T + TC
D = 1024
KD = D // P
EPS = 1e-6
H = 8
QK = 96
NOPE = 64
ROPE = 32
VD = 64
QL = 384 // P
KL = 256 // P
NF = 512 // P
TT = T // P
KT = TK // P
NE = 16
CAP = 2 * T // NE
FE = 512 // P
PAIRS = NE // 2
LRU = 8
SC = 4
FF = 3072 // P
QUARTERS = 4
FQ = FF // QUARTERS

CH = 2048
NRAW = 4
NHL = 3
SECTIONS = [("mod_a", 8, False), ("s1", 20, True), ("mod_b", 16, False), ("wo", 2, True), ("w_out", 4, True),
            ("experts", 96, False), ("w_in_2", 14, True), ("w_out_2", 6, True), ("ffn", 36, True)]
B = 128
S1_QKV, S1_KPE, S1_F, S1_DFT = 0, 40 * B, 44 * B, 80 * B
S1_GA, S1_GB, S1_V, S1_HEADS = 112 * B, 176 * B, 17 * CH, 18 * CH
HEAD_W = QL * QK + KL * NOPE
assert 4 * HEAD_W <= CH

COLS = {}
_n = 0
for _name, _w in [("norm1_g", 8), ("b_mod", 48), ("q_a_norm_g", QL), ("kv_a_norm_g", KL), ("q_norm_g", 1),
                  ("k_norm_g", 1), ("norm2_g", 8), ("cond", 16), ("norm1_g_2", 8), ("lru_conv_w_2", 32),
                  ("lru_conv_b_2", 8), ("lru_ba_2", 8), ("lru_bx_2", 8), ("lru_lambda_2", 8),
                  ("sc_conv_w_2", 12), ("norm2_g_2", 8), ("ffn_conv_w_2", 144), ("final_g_2", 8), ("slot", 1)]:
    COLS[_name] = _n
    _n += _w
NCOLS = _n


class Order:

    def __init__(self):
        self.at = {}

    def add(self, *name):
        assert name not in self.at, name
        self.at[name] = len(self.at)

    def __getitem__(self, name):
        return self.at[name if isinstance(name, tuple) else (name,)]

    def __len__(self):
        return len(self.at)


class Plan:

    def __init__(self):
        self.tiles = Order()
        self.bank, self.freed, self.prev = [], [], []
        self.counts = {"act": 0, "dve": 0}
        self.last_user = {}
        self.owner = {}
        self.nb = 6
        self.start = 0

    def phase(self, nb):
        self.nb, self.start = nb, len(self.tiles)

    def add(self, *name, by="dve", raw=(), split=(), bank=None):
        t = len(self.tiles)
        self.tiles.add(*name)
        b = (t - self.start) % self.nb if bank is None else bank
        self.bank.append(b)
        if isinstance(by, str):
            self.counts[by] += 1
            by = (by, self.counts[by])
        self.freed.append(by)
        self.prev.append(self.owner.get(b))
        self.owner[b] = t
        for c in raw:
            self.last_user["raw", c] = t
        for c in split:
            self.last_user["split", c] = t

    def freed_count(self, t):
        return self.freed[t][1]


def section_start(name, split_only):
    n = 0
    for s, k, split in SECTIONS:
        if s == name:
            return n
        if split or not split_only:
            n += k


def raw_chunks():
    out, ns, nr = [], 0, 0
    for _, k, split in SECTIONS:
        for _ in range(k):
            out.append((split, ns if split else nr))
            ns, nr = ns + split, nr + (not split)
    return out


CHUNKS = raw_chunks()
RAW_OF_SPLIT = [n for n, (s, _) in enumerate(CHUNKS) if s]
SPLIT0 = {s: section_start(s, True) for s, _, sp in SECTIONS if sp}
RAW_N = {s: sum(k for _, k, _ in SECTIONS[:i]) for i, (s, _, _) in enumerate(SECTIONS)}
RAW0 = {s: section_start(s, False) for s, _, sp in SECTIONS}


def blocks(base, first, count, width=B):
    return range(base + first // CH, base + (first + count * width - 1) // CH + 1)


def split_steps():
    o = Order()
    for j in range(KD):
        o.add("h", j)
    for j in range(KD):
        o.add("hc", j)
    o.add("f", 0)
    o.add("f", 1)
    for j in range(QL):
        o.add("cq", j)
    for j in range(KL):
        o.add("ckv", j)
    o.add("f", 2)
    o.add("f", 3)
    for g in range(NF + 1):
        if g < NF:
            o.add("f_ch", g, 0)
            o.add("f_ch", g, 1)
        if g >= 1:
            o.add("four", g - 1)
    for h in range(H):
        o.add("q", h)
        o.add("k", h)
    for j in range(4):
        o.add("attn", j)
    for j in range(KD):
        o.add("m", j)
    for e in range(NE):
        o.add("ye", e, 0)
        o.add("ye", e, 1)
    for j in range(KD):
        o.add("g", j)
    for j in range(SC):
        o.add("y_sc", j)
    for j in range(LRU):
        o.add("y_lru", j)
    for j in range(KD):
        o.add("g2", j)
    for q in range(QUARTERS):
        for i in range(FQ):
            o.add("ff", q, i)
    return o


SPLITS = split_steps()

PRE_Q = 2 * KD + QL + KL
PRE_SC = PRE_Q + 2 * H + 2 * KD
PRE_FF = PRE_SC + SC + LRU + KD


def make_plan():
    p = Plan()
    s1 = SPLIT0["s1"]
    for g in range(4):
        if g == 3:
            p.add("ssq_xc")
        p.add("mod", g, raw=(2 * g, 2 * g + 1))
    p.add("bc_x", by=("pre_done", KD))
    p.add("bc_c", by=("pre_done", 2 * KD))
    for j in range(QL):
        p.add("cq", j, split=blocks(s1, S1_QKV + j * 8 * B, 8))
    for j in range(KL):
        p.add("ckv", j, 0)
        p.add("ckv", j, 1, split=blocks(s1, S1_QKV + (QL + j) * 8 * B, 8))
    p.add("kpe", 0)
    p.add("kpe", 1, split=blocks(s1, S1_KPE, 2))
    p.add("f", 0, by=("lo_done", SPLITS["f", 0] + 1), split=blocks(s1, S1_F, 8))
    p.add("ssq_c")
    p.add("f", 1, by=("lo_done", SPLITS["f", 1] + 1), split=blocks(s1, S1_F + 8 * B, 8))
    p.add("bc_cq", by=("pre_done", 2 * KD + QL))
    p.add("bc_ckv", 0, by=("pre_done", PRE_Q))
    p.add("bc_ckv", 1, by=("pre_done", PRE_Q))
    p.add("rot_k")
    p.add("f", 2, by=("lo_done", SPLITS["f", 2] + 1), split=blocks(s1, S1_F + 16 * B, 8))
    p.add("f", 3, by=("lo_done", SPLITS["f", 3] + 1), split=blocks(s1, S1_F + 24 * B, 12))
    for g in range(NF + 1):
        if g < NF:
            p.add("f_ch", g, 0, by=("lo_done", SPLITS["f_ch", g, 0] + 1))
            p.add("f_ch", g, 1, by=("lo_done", SPLITS["f_ch", g, 1] + 1))
        if g >= 1:
            p.add("four", g - 1, by=("lo_done", SPLITS["four", g - 1] + 1), split=blocks(s1, S1_DFT, 32))
    for j in range(KD):
        p.add("ga", j, by="act", split=blocks(s1, S1_GA + j * 8 * B, 8))
    for j in range(KD):
        p.add("gb", j, by="act", split=blocks(s1, S1_GB + j * 12 * B, 8))
        p.add("four_o", j, by=("resid_done", j + 1), split=blocks(s1, S1_GB + j * 12 * B + 8 * B, 4))
    for t in range(KT):
        p.add("v", t, by="act", split=blocks(s1, S1_V, 8))

    def prep_a(h):
        c = (s1 + (S1_HEADS + (h // 4) * CH) // CH,)
        p.add("uq", h, by=("qk_raw", 2 * h + 1), split=c)
        p.add("uk", h, 0, by=("qk_raw", 2 * h + 2), split=c)
        p.add("uk", h, 1, by=("qk_raw", 2 * h + 2), split=c)

    def prep_b(h):
        p.add("rot_q", h)
        p.add("bc_q", h, by=("pre_done", PRE_Q + 2 * h + 1))
        p.add("bc_k", h, 0, by=("pre_done", PRE_Q + 2 * h + 2))
        p.add("bc_k", h, 1, by=("pre_done", PRE_Q + 2 * h + 2))

    prep_a(0)
    p.add("ssq_h", 0)
    prep_b(0)
    for h in range(H):
        for q in range(TT):
            for s in range(2):
                p.add("mx", h, q, s)
        if h + 1 < H:
            prep_a(h + 1)
        p.add("mod_b", 2 * h, by=("modb_done", 2 * h + 1), raw=(8 + 2 * h,))
        p.add("mx_row", h, by="act")
        for k in range(KT):
            p.add("sT", h, k, by="act")
            if k == 1 and h + 1 < H:
                p.add("ssq_h", h + 1)
            if k == 3 and h + 1 < H:
                prep_b(h + 1)
        p.add("mod_b", 2 * h + 1, by=("modb_done", 2 * h + 2), raw=(9 + 2 * h,))
    for j in range(KD):
        p.add("attn_o", j, split=blocks(SPLIT0["wo"], j * 4 * B, 4))
    for j in range(KD):
        p.add("merged", j, by=("resid_done", KD + j + 1), split=blocks(SPLIT0["w_out"], j * 8 * B, 8))
    p.add("logits", by=("logit_max", 1))
    p.add("aff_t")
    for t in range(TT):
        p.add("h2_tok", t, 0, by="act")
        p.add("h2_tok", t, 1, by="act")
    p.add("slots_tok")
    for i in range(KD):
        p.add("xe", i, 0, by="act")
        p.add("xe", i, 1, by="act")
    p.add("gates")
    for i in range(PAIRS):
        p.add("onehot", i)
    e0 = 8 + 16
    p.phase(6)
    def gate_up(e, at):
        p.add("gate_e", e, by=("silu_e", e + 1), raw=(at, at + 1), bank=e % 2)
        if e >= 1:
            p.add("act_t", e - 1, by=("act_t_done", e), bank=6)
        p.add("up_e", e, by=("act_done", e + 1), raw=(at + 2, at + 3), bank=2 + e % 2)
        return at + 4

    at = gate_up(0, e0)
    for e in range(NE):
        if e + 1 < NE:
            at = gate_up(e + 1, at)
        else:
            p.add("act_t", e, by=("act_t_done", e + 1), bank=6)
        for half in range(2):
            p.add("ye", e, half, by=("lo_done", SPLITS["ye", e, half] + 1), raw=(at + half,), bank=4 + half)
        at += 2
    for j in range(KD):
        p.add("combine", j, by=("resid_done", 2 * KD + j + 1))
    w = SPLIT0["w_in_2"]
    for j in range(LRU):
        p.add("lru_x", j, by=("conv_done", j + 1), split=blocks(w, j * 8 * B, 8))
        if j >= 2:
            p.add("lru_r", j - 2, by="act")
            p.add("lru_i", j - 2, by="act")
    for j in range(SC):
        p.add("sc_c", j, by="act", split=blocks(w, (LRU + 3 * j) * 8 * B, 8))
        if j == 0:
            for i in (LRU - 2, LRU - 1):
                p.add("lru_r", i, by="act")
                p.add("lru_i", i, by="act")
        p.add("sc_x", j, split=blocks(w, (LRU + 3 * j + 1) * 8 * B, 8))
        p.add("sc_b", j, by=("pre_done", PRE_SC + j + 1), split=blocks(w, (LRU + 3 * j + 2) * 8 * B, 8))
    for j in range(LRU):
        p.add("lru_gate", j, by="act", split=blocks(w, (LRU + 3 * SC + j) * 8 * B, 8))
    for j in range(KD):
        p.add("mix_o", j, by=("resid_done", 3 * KD + j + 1), split=blocks(SPLIT0["w_out_2"], j * 12 * B, 12))
    w = SPLIT0["ffn"]
    p.phase(5)
    for q in range(QUARTERS):
        for i in range(FQ):
            p.add("ff_g", q, i, by=("accg_done", q * FQ + i + 1), split=blocks(w, (q * 144 + i * 16) * B, 8))
            p.add("ff_u", q, i, by=("accu_done", q * FQ + i + 1), split=blocks(w, (q * 144 + i * 16 + 8) * B, 8))
        for j in range(KD):
            p.add("ff_o", q, j, by=("resid_done", (4 + q) * KD + j + 1), split=blocks(w, (q * 144 + 96 + j * 6) * B, 6))
    return p


PLAN = make_plan()
TILE = PLAN.tiles
LAST = PLAN.last_user


NSPLIT = len(RAW_OF_SPLIT)


def split_due(c):
    n = RAW_OF_SPLIT[c] - NRAW
    due = [LAST["split", c - NHL] + 1] if c >= NHL else [0]
    due += [LAST["raw", k] + 1 for sp, k in CHUNKS[:max(n + 1, 0)] if not sp]
    if c >= SPLIT0["w_in_2"]:
        due.append(TILE["combine", KD - 1] + 1)
    if SPLIT0["wo"] <= c < SPLIT0["w_in_2"]:
        due.append(TILE["sT", H - 1, 3 if c == SPLIT0["wo"] else 5])
    return max(due)


SPLIT_DUE = [split_due(c) for c in range(NSPLIT)]
FFN0 = TILE["ff_g", 0, 0]
FFN_TILES = 2 * FQ + KD
FFN_CHUNKS = 9


def build(nc, stream, cols_d, x_d, ctx_d, router_d, wab_d, rope_d, rot_d, dftc_d, ident_d, iota_d, pick_d, out):
    with ExitStack() as ctx:
        base = 16512

        def at(name, kb, shape, dt=F32):
            return nc.alloc_sbuf_tensor_at(name, shape, dt, offset=base + int(kb * 1024))

        def sem(name):
            return ctx.enter_context(nc.semaphore(name))

        raw = at("raw", 0, [P, NRAW, CH])
        w_hi = at("w_hi", 32, [P, NHL, CH], F32R)
        w_lo = at("w_lo", 56, [P, NHL, CH], F32R)
        R = 80
        x1 = at("x1", R + 96, [P, KD, T])
        cols = at("cols", R + 122.75, [P, NCOLS])
        mod = at("mod", R + 124.25, [P, 48, 2])
        ones = at("ones", R + 124.75, [P, P])
        ident = at("ident", R + 125.25, [P, P])
        router = at("router", R + 125.75, [P, KD, NE])
        iota = at("iota", R + 126.25, [P, CAP])
        small = at("small", R + 126.5, [P, 256])
        assert base + (R + 127.5) * 1024 <= 229368 and NCOLS * 4 <= 1536

        def part(off, n):
            return small[:, off:off + n]
        a1, a1c, a2 = part(0, 8), part(8, 8), part(16, 8)
        eps, csil = part(24, 1), part(32, 16)
        nc8, c8 = part(64, 8), part(72, 8)
        sp_z, sp_s, sp_s2, sp_p = part(80, 8), part(88, 8), part(96, 8), part(104, 8)
        mx2, mxq, gcol = part(112, 8), part(120, 4), part(128, 8)
        nv, ny, nt, rcol = part(136, 10), part(146, 10), part(156, 10), part(166, 10)
        h_hi = at("h_hi", R + 0, [P, KD, T], F32R)
        h_lo = at("h_lo", R + 16, [P, KD, T], F32R)
        hc_hi = at("hc_hi", R + 32, [P, KD, TC], F32R)
        hc_lo = at("hc_lo", R + 40, [P, KD, TC], F32R)
        x0 = at("x0", R + 48, [P, KD, T])
        c0 = at("c0", R + 64, [P, KD, TC])
        sq_x0 = at("sq_x0", R + 72, [P, KD, T])
        sq_c0 = at("sq_c0", R + 88, [P, KD, TC])
        pre = at("pre", R + 96, [P, 2, T])
        sum_x = at("sum_x", R + 96, [P, T])
        sum_c = at("sum_c", R + 98, [P, TC])
        macc_x = at("macc_x", R + 0, [P, 8, B])
        macc_c = at("macc_c", R + 32, [P, 8, B])
        mprod = at("mprod", R + 36, [P, 1, KD, B])
        cqg = at("cqg", R + 48, [P, QL, T])
        ckvg = at("ckvg", R + 54, [P, KL, TK])
        sq_q = at("sq_cq", R + 60, [P, QL, T])
        sq_kv = at("sq_ckv", R + 66, [P, KL, TK])
        cq_hi = at("cq_hi", R + 80, [P, QL, T], F32R)
        cq_lo = at("cq_lo", R + 86, [P, QL, T], F32R)
        ckv_hi = at("ckv_hi", R + 92, [P, KL, TK], F32R)
        ckv_lo = at("ckv_lo", R + 98, [P, KL, TK], F32R)
        f_hi = at("f_hi", R + 32, [P, NF, T], F32R)
        f_lo = at("f_lo", R + 40, [P, NF, T], F32R)
        fc_hi = at("fc_hi", R + 48, [P, 2, 2, 2, 256], F32R)
        fc_lo = at("fc_lo", R + 56, [P, 2, 2, 2, 256], F32R)
        ga = at("ga", R + 48, [P, KD, T])
        gbf = at("gbf", R + 64, [P, KD, T])
        kraw = at("kraw", R + 104, [QK, TK])
        sqk = at("sqk", R + 107, [QK, TK])
        sqq = at("sqq", R + 110, [QK, T])
        rk = at("rk", R + 112, [QK, TK])
        rope_cs = at("rope_cs", R + 115, [QK, 2, T])
        dftc = at("dftc", R + 119, [P, 256])
        dftc_hi = at("dftc_hi", R + 120, [P, 256], F32R)
        dftc_lo = at("dftc_lo", R + 121, [P, 256], F32R)
        rotm = at("rotm", R + 122, [QK, QK])
        sg = [at("sg0", R + 110, [P, T]), at("sg1", R + 112, [P, T])]
        macc = at("macc", R + 121, [P, 2, B])
        v = at("v", R + 0, [P, KT, H // 2, 3, VD])
        q_hi = at("q_hi", R + 18, [QK + 1, T], F32R)
        q_lo = at("q_lo", R + 20, [QK + 1, T], F32R)
        k_hi = at("k_hi", R + 22, [QK + 1, TK], F32R)
        k_lo = at("k_lo", R + 25, [QK + 1, TK], F32R)
        probs = at("probs", R + 28, [P, 3, T])
        att = at("att", R + 34, [P, 4, T])
        tmp_a = at("tmp_a", R + 42, [P, T])
        rs = at("rs", R + 44, [P, T])
        qg = at("qg", R + 46, [QK, T])
        rq = at("rq", R + 119, [QK, T])
        att_hi = at("att_hi", R + 80, [P, 4, T], F32R)
        att_lo = at("att_lo", R + 88, [P, 4, T], F32R)
        m_hi = at("m_hi", R + 0, [P, KD, T], F32R)
        m_lo = at("m_lo", R + 16, [P, KD, T], F32R)
        m_tmp = at("m_tmp", R + 42, [P, 2, T])
        sq = at("sq", R + 48, [P, 2, T])
        h2 = at("h2", R + 80, [P, KD, T])
        h2t_hi = at("h2t_hi", R + 0, [P, TT, D], F32R)
        h2t_lo = at("h2t_lo", R + 16, [P, TT, D], F32R)
        h2t = at("h2t", 64, [P, TT, D])
        pick_tok = at("pick_tok", R + 32, [P, TT, NE * CAP], F32R)
        xe = at("xe", R + 48, [P, KD, NE * CAP])
        place = at("place", R + 80, [P, PAIRS, T], F32R)
        aff_t = at("aff_t", R + 112, [NE, T])
        work = at("work", R + 114, [NE, T])
        chosen = at("chosen", R + 116, [NE, T])
        slots = at("slots", R + 118, [NE, T])
        pick = at("pick", R + 112, [NE, PAIRS * P])
        aff = at("aff", R + 120, [P, TT, NE])
        aff_m = at("aff_m", R + 120.25, [P, TT])
        aff_s = at("aff_s", R + 120.5, [P, TT])
        slots_tok = at("slots_tok", R + 120.75, [P, TT, NE])
        top8 = at("top8", R + 121, [NE, 8])
        ones_row = at("ones_row", R + 40, [NE, T])
        gate_s = at("gate_s", R + 112, [CAP, T])
        act_r = at("act_r", R + 116, [CAP, T])
        act_e = at("act_e", R + 114, [P, 2, FE * CAP])
        ye_hi = at("ye_hi", R + 0, [P, PAIRS, D], F32R)
        ye_lo = at("ye_lo", 32, [P, PAIRS, D], F32R)
        lru_a = at("lru_a", R + 32, [P, LRU, T])
        lru_v = at("lru_v", R + 48, [P, LRU, T])
        lru_b = at("lru_b", R + 64, [P, LRU, T])
        g_pre = at("g_pre", R + 80, [P, 2, T])
        conv_u = at("conv_u", R + 84, [P, 3, T])
        e_i = at("e_i", R + 90, [P, T])
        a_sq = at("a_sq", R + 118, [P, 2, T])
        wab = at("wab", R + 112, [P, 2, LRU, P])
        ysc_hi = at("ysc_hi", R + 80, [P, SC, T], F32R)
        ysc_lo = at("ysc_lo", R + 88, [P, SC, T], F32R)
        sc_c = at("sc_c", R + 112, [P, T])
        sc_cx = at("sc_cx", R + 114, [P, T])
        sc_acc = at("sc_acc", R + 116, [P, T])
        sc_y = at("sc_y", R + 94, [P, T])
        gl = at("gl", R + 112, [P, 2, T])
        y_pre = at("y_pre", R + 116, [P, 2, T])
        ylru_hi = at("ylru_hi", R + 32, [P, LRU, T], F32R)
        ylru_lo = at("ylru_lo", R + 64, [P, LRU, T], F32R)
        ff_hi = at("ff_hi", R + 32, [P, FQ, T], F32R)
        ff_lo = at("ff_lo", R + 44, [P, FQ, T], F32R)
        acc_g = at("acc_g", R + 56, [P, 2, T])
        acc_u = at("acc_u", R + 60, [P, 2, T])
        ff_gl = at("ff_gl", R + 64, [P, 2, T])
        ff_pre = at("ff_pre", R + 68, [P, 2, T])
        sq_last = at("sq_last", R + 72, [P, 2, T])
        y_out = at("y_out", R + 0, [P, KD, T])

        psum = nc.alloc_psum_tensor("psum", [P, 8, T], F32)

        raw_full = [sem(f"raw_full{i}") for i in range(NRAW)]
        w_hi_done = sem("w_hi_done")
        w_lo_done = sem("w_lo_done")
        tile_full = sem("tile_full")
        freed_act = sem("freed_act")
        freed_dve = sem("freed_dve")
        hi_done = sem("hi_done")
        lo_done = sem("lo_done")
        cols_in = sem("cols_in")
        consts_in = sem("consts_in")
        macc_x_done = sem("macc_x_done")
        macc_c_done = sem("macc_c_done")
        macc_done = sem("macc_done")
        modb_done = sem("modb_done")
        pool_seq = sem("pool_seq")
        sum_done = sem("sum_done")
        x_in = sem("x_in")
        x_again = sem("x_again")
        wab_in = sem("wab_in")
        pick_in = sem("pick_in")
        silu_done = sem("silu_done")
        sq_done = sem("sq_done")
        sq_summed = sem("sq_summed")
        pre_done = sem("pre_done")
        act_seq = sem("act_seq")
        dve_seq = sem("dve_seq")
        ones_done = sem("ones_done")
        qk_raw = sem("qk_raw")
        mx_done = sem("mx_done")
        o_full = sem("o_full")
        v_done = sem("v_done")
        resid_done = sem("resid_done")
        h2_done = sem("h2_done")
        h2_pre = sem("h2_pre")
        raw_used = sem("raw_used")
        rcol_done = sem("rcol_done")
        bc_full = sem("bc_full")
        tok_done = sem("tok_done")
        tok_lo = sem("tok_lo")
        o_raw = sem("o_raw")
        att_done = sem("att_done")
        logit_max = sem("logit_max")
        aff_exp = sem("aff_exp")
        aff_done = sem("aff_done")
        slots_done = sem("slots_done")
        picks_done = sem("picks_done")
        silu_e = sem("silu_e")
        act_done = sem("act_done")
        act_t_done = sem("act_t_done")
        conv_done = sem("conv_done")
        a_sq_done = sem("a_sq_done")
        lru_b_done = sem("lru_b_done")
        av_done = sem("av_done")
        v_ready = sem("v_ready")
        mult_done = sem("mult_done")
        glu_done = sem("glu_done")
        acc_done = sem("acc_done")
        accg_done = sem("accg_done")
        accu_done = sem("accu_done")
        sp_done = sem("sp_done")
        y_done = sem("y_done")
        out_done = sem("out_done")
        z_done = sem("z_done")

        freeing = {"act": freed_act, "dve": freed_dve, "lo_done": lo_done, "resid_done": resid_done,
                   "qk_raw": qk_raw, "logit_max": logit_max, "act_done": act_done, "conv_done": conv_done,
                   "pre_done": pre_done, "accg_done": accg_done, "accu_done": accu_done,
                   "modb_done": modb_done, "silu_e": silu_e, "act_t_done": act_t_done}

        block = ctx.enter_context(nc.Block())

        def col(name, j=0, n=1):
            return cols[:, COLS[name] + j:COLS[name] + j + n]

        def bank(*name):
            return psum[:, PLAN.bank[TILE[name]], :]

        def full(eng, *name):
            eng.wait_ge(tile_full, TILE[name] + 1)

        @block.sync
        def _(sp):
            sp.dma_start(cols[:], cols_d).then_inc(cols_in, 16)

            def load(n, slot):
                sp.dma_start(raw[:, slot, :], stream[bass.ds(n, 1), :, :].rearrange("a p c -> p (a c)")
                             if not isinstance(n, int) else stream[n, :, :]).then_inc(raw_full[slot], 16)

            for n in range(NRAW):
                load(n, n)
            sp.dma_start(x0[:], x_d).then_inc(x_in, 16)
            sp.dma_start(c0[:], ctx_d).then_inc(x_in, 16)
            sp.dma_start(ident[:], ident_d).then_inc(consts_in, 16)
            sp.dma_start(dftc[:], dftc_d).then_inc(consts_in, 16)
            sp.dma_start(iota[:], iota_d).then_inc(consts_in, 16)
            sp.dma_start(router[:], router_d).then_inc(consts_in, 16)
            sp.dma_start(rotm[:], rot_d).then_inc(consts_in, 16)
            sp.dma_start(rope_cs[NOPE:QK, :, :], rope_d).then_inc(consts_in, 16)
            n = NRAW
            while n < len(CHUNKS):
                split, k = CHUNKS[n - NRAW]
                run = n
                while run < len(CHUNKS) and CHUNKS[run - NRAW][0] == split:
                    run += 1
                experts = RAW0["experts"] <= n - NRAW < RAW0["w_in_2"]
                if not split and not experts:
                    run = min(run, RAW0["experts"] + NRAW)
                e = RAW0["experts"]
                loops = (run - n) // NRAW if split or experts else 0
                if loops >= 2:
                    with sp.Fori(0, loops) as i:
                        for s in range(NRAW):
                            if split:
                                sp.wait_ge(w_lo_done, i * NRAW + k + s + 1)
                            else:
                                sp.wait_ge(raw_used, i * NRAW + (n - NRAW - e) + s + 1)
                            load(i * NRAW + (n + s), (n + s) % NRAW)
                    n += loops * NRAW
                    continue
                for m in range(n, run):
                    _, k = CHUNKS[m - NRAW]
                    if split:
                        sp.wait_ge(w_lo_done, k + 1)
                    elif m - NRAW >= e:
                        sp.wait_ge(raw_used, m - NRAW - e + 1)
                    else:
                        sp.wait_ge(tile_full, LAST["raw", k] + 1)
                    load(m, m % NRAW)
                n = run
            sp.wait_ge(out_done, 16 * KD)

        @block.gpsimd
        def _(pool):
            nc.gpsimd.memset(ones[:], 1.0).then_inc(ones_done, 1)

            def lo(c, slot, raw_slot):
                pool.wait_ge(w_hi_done, c + 1)
                nc.gpsimd.tensor_tensor(w_lo[:, slot, :], raw[:, raw_slot, :], w_hi[:, slot, :].bitcast(F32),
                                        ALU.subtract).then_inc(w_lo_done, 1)

            def token_lo():
                for t in range(TT):
                    for half in range(2):
                        pool.wait_ge(tok_done, 2 * t + half + 1)
                        w = slice(half * T, half * T + T)
                        nc.gpsimd.tensor_tensor(h2t_lo[:, t, w], h2t[:, t, w], h2t_hi[:, t, w].bitcast(F32),
                                                ALU.subtract).then_inc(tok_lo, 1)

            def tiles_sum(prod, dst, wait, finished):
                half = KD // 2
                while half >= 1:
                    wait()
                    last = half == 1
                    out_ = dst if last else prod[:, :, 0:half, :]
                    nc.gpsimd.tensor_tensor(out_, prod[:, :, 0:half, :], prod[:, :, half:2 * half, :], ALU.add)\
                        .then_inc(finished if last else pool_seq, 1)
                    half //= 2

            steps = [0]

            def next_step():
                steps[0] += 1
                pool.wait_ge(pool_seq, steps[0])

            pool.wait_ge(silu_done, 1)
            for c in range(8):
                pool.wait_ge(raw_full[c % NRAW], 16 * (c // NRAW + 1))
                if c >= 1:
                    pool.wait_ge(macc_c_done, c)
                w = raw[:, c % NRAW, KD * B:2 * KD * B].rearrange("p (k c) -> p k c", k=KD)
                nc.gpsimd.tensor_tensor(mprod[:, 0, :, :], w, csil[:, 1:16:2].unsqueeze(2).to_broadcast([P, KD, B]),
                                        ALU.mult).then_inc(pool_seq, 1)
                tiles_sum(mprod, macc_c[:, c:c + 1, :].unsqueeze(2), next_step, macc_c_done)

            def modulation_b():
                n = RAW_N["mod_b"]
                base, per = steps[0], 3
                x_cond = csil[:, 0:16:2].unsqueeze(2).to_broadcast([P, KD, B])

                def chunk(i, c):
                    slot = (n + c) % NRAW
                    pool.wait_ge(raw_full[slot], i * 16 + 16 * ((n + c) // NRAW + 1))
                    for m in range(2):
                        w = raw[:, slot, m * KD * B:(m + 1) * KD * B].rearrange("p (k c) -> p k c", k=KD)
                        ins = nc.gpsimd.tensor_tensor(w, w, x_cond, ALU.mult)
                    ins.then_inc(pool_seq, 1)
                    step = [0]

                    def wait():
                        step[0] += 1
                        pool.wait_ge(pool_seq, i * (NRAW * per) + (base + c * per + step[0]))
                        if step[0] == per and not (isinstance(i, int) and c == 0):
                            pool.wait_ge(modb_done, i * NRAW + c)
                    tiles_sum(raw[:, slot, :].rearrange("p (m k c) -> p m k c", m=2, k=KD), macc[:].unsqueeze(2), wait,
                              macc_done)
                for c in range(NRAW):
                    chunk(0, c)
                with pool.Fori(1, 16 // NRAW) as i:
                    for c in range(NRAW):
                        chunk(i, c)

            PERIOD = NRAW * NHL
            c = 0
            while c < NSPLIT:
                if c == SPLIT0["wo"]:
                    modulation_b()
                run = c
                while run < NSPLIT and RAW_OF_SPLIT[run] - run == RAW_OF_SPLIT[c] - c:
                    run += 1
                loops = (run - c) // PERIOD
                if loops >= 2:
                    if c == SPLIT0["w_in_2"]:
                        token_lo()
                    with pool.Fori(0, loops) as i:
                        for s in range(PERIOD):
                            lo(i * PERIOD + (c + s), (c + s) % NHL, RAW_OF_SPLIT[c + s] % NRAW)
                    c += loops * PERIOD
                for s in range(c, run):
                    if s == SPLIT0["w_in_2"]:
                        token_lo()
                    lo(s, s % NHL, RAW_OF_SPLIT[s] % NRAW)
                c = run

        @block.tensor
        def _(pe):
            mm = nc.tensor.matmul
            seen = [0]

            def open_tile(*name):
                t = TILE[name]
                prev = PLAN.prev[t]
                if prev is not None:
                    pe.wait_ge(freeing[PLAN.freed[prev][0]], PLAN.freed_count(prev))
                return psum[:, PLAN.bank[t], :]

            def weights(base, off, width):
                c, o = base + off // CH, off % CH
                assert o + width <= CH
                if c + 1 > seen[0]:
                    pe.wait_ge(w_lo_done, c + 1)
                    seen[0] = c + 1
                return w_hi[:, c % NHL, o:o + width], w_lo[:, c % NHL, o:o + width]

            def mm3(o, w, x, start, stop):
                mm(o, w[0], x[0], start=start, stop=False)
                mm(o, w[0], x[1], start=False, stop=False)
                return mm(o, w[1], x[0], start=False, stop=stop)

            def done(ins):
                ins.then_inc(tile_full, 1)

            def project(o, base, off, width, ks, x_of):
                for i, k in enumerate(ks):
                    last = mm3(o, weights(base, off + i * width, width), x_of(k), i == 0, i == len(ks) - 1)
                return last

            def raw_chunk(n):
                pe.wait_ge(raw_full[n % NRAW], 16 * (n // NRAW + 1))
                return raw[:, n % NRAW, :]

            def mod_tile(g):
                o = open_tile("mod", g)
                for c in range(2):
                    w = raw_chunk(2 * g + c)
                    for k in range(KD):
                        mm(o[:, 4 * c:4 * c + 2], w[:, k * B:(k + 1) * B], csil[:, 2 * k:2 * k + 2],
                           start=k == 0 and c == 0, stop=k == KD - 1, skip_group_check=True)
                for c in range(2):
                    for i, (acc, ready) in enumerate(((macc_x, macc_x_done), (macc_c, macc_c_done))):
                        pe.wait_ge(ready, 2 * g + c + 1)
                        last = mm(o[:, 4 * c + 2 + i:4 * c + 3 + i], acc[:, 2 * g + c, :], one, start=False, stop=True,
                                  skip_group_check=True)
                done(last)

            def mod_b_tile(k):
                o = open_tile("mod_b", k)
                pe.wait_ge(macc_done, k + 1)
                for m in range(2):
                    last = mm(o[:, m:m + 1], macc[:, m, :], one, start=True, stop=True)
                done(last)

            pe.wait_ge(ones_done, 1)
            one = ones[:, 0:1]

            def columns(o, at, src, tiles, rows=P, start=True, stop=True):
                for t in range(tiles):
                    last = mm(o[:, at + t:at + t + 1], src[:, t * P:(t + 1) * P], one[0:rows, :],
                              start=start and t == 0, stop=stop, skip_group_check=True)
                return last

            def broadcast(o, at, tiles, rows=P):
                for t in range(tiles):
                    last = mm(o[0:rows, t * P:(t + 1) * P], rcol[:, at + t:at + t + 1].to_broadcast([P, rows]), ident[:],
                              start=True, stop=True)
                return last

            rcols = [0]

            def wait_rcol():
                rcols[0] += 1
                pe.wait_ge(rcol_done, rcols[0])

            pe.wait_ge(silu_done, 1)
            for g in range(4):
                if g == 3:
                    o = open_tile("ssq_xc")
                    pe.wait_ge(sum_done, 1)
                    columns(o, 0, sum_x, TT)
                    pe.wait_ge(sum_done, 2)
                    done(columns(o, TT, sum_c, 2, start=False))
                mod_tile(g)
            pe.wait_ge(consts_in, 16 * 6)
            o, o2 = open_tile("bc_x"), open_tile("bc_c")
            wait_rcol()
            done(broadcast(o, 0, TT))
            done(broadcast(o2, TT, 2))

            s1 = SPLIT0["s1"]
            hx = lambda k: (h_hi[:, k, :], h_lo[:, k, :])
            hcx = lambda k: (hc_hi[:, k, :], hc_lo[:, k, :])

            def project_two(o2, w_of, x_of, splits, tiles=KD):
                for k in range(tiles):
                    pe.wait_ge(lo_done, (splits + k if isinstance(splits, int) else splits[k]) + 1)
                    for i in range(2):
                        last = mm3(o2[i], w_of(i, k), x_of(k), k == 0, k == tiles - 1)
                        if k == tiles - 1:
                            done(last)

            ks = range(KD)
            project_two((open_tile("cq", 0), open_tile("cq", 1)),
                        lambda i, k: weights(s1, S1_QKV + (i * KD + k) * B, B), hx, SPLITS["h", 0])
            for j in range(2, QL):
                o = open_tile("cq", j)
                done(project(o, s1, S1_QKV + j * 8 * B, B, ks, hx))
            pe.wait_ge(lo_done, SPLITS["hc", KD - 1] + 1)
            for j in range(KL):
                for s in range(2):
                    o = open_tile("ckv", j, s)
                    done(project(o if s == 0 else o[:, 0:TC], s1, S1_QKV + (QL + j) * 8 * B, B, ks, hcx if s else hx))
            for s in range(2):
                o = open_tile("kpe", s)
                done(project(o[0:ROPE, 0:TC if s else T], s1, S1_KPE, ROPE, ks, hcx if s else hx))

            def fourier_in(g):
                done(project(open_tile("f", g), s1, S1_F + g * 8 * B, B, ks, hx))

            fourier_in(0)
            o = open_tile("ssq_c")
            pe.wait_ge(sq_done, 2 + QL)
            for j in range(QL):
                columns(o, 0, sq_q[:, j, :], TT, start=j == 0, stop=j == QL - 1)
            pe.wait_ge(sq_done, 2 + QL + 2 * KL)
            for j in range(KL):
                last = columns(o, TT, sq_kv[:, j, :], KT, start=False, stop=j == KL - 1)
            done(last)
            fourier_in(1)
            o3 = open_tile("bc_cq"), open_tile("bc_ckv", 0), open_tile("bc_ckv", 1)
            wait_rcol()
            done(broadcast(o3[0], 0, TT))
            done(broadcast(o3[1], TT, TT))
            done(broadcast(o3[2], 2 * TT, 2))
            o = open_tile("rot_k")
            pe.wait_ge(freed_dve, PLAN.freed_count(TILE["kpe", 1]))
            done(mm(o[0:QK, :], rotm[NOPE:QK, :], kraw[NOPE:QK, 0:T], start=True, stop=True))
            fourier_in(2)
            fourier_in(3)
            for g in range(NF + 1):
                if g < NF:
                    pe.wait_ge(lo_done, SPLITS["f", 3] + 1)
                    for half in range(2):
                        o = open_tile("f_ch", g, half)
                        for t in range(2):
                            tok = slice((2 * half + t) * P, (2 * half + t + 1) * P)
                            last = mm3(o[:, t * 256:(t + 1) * 256], (f_hi[:, g, tok], f_lo[:, g, tok]),
                                       (dftc_hi[:], dftc_lo[:]), True, True)
                        done(last)
                if g >= 1:
                    o = open_tile("four", g - 1)
                    pe.wait_ge(lo_done, SPLITS["f_ch", g - 1, 1] + 1)
                    for part in range(2):
                        for t in range(TT):
                            i = part * TT + t
                            x = weights(s1, S1_DFT + i * 4 * B, T)
                            a = slice(part * P, part * P + P)
                            last = mm3(o, (fc_hi[:, (g - 1) % 2, t // 2, t % 2, a], fc_lo[:, (g - 1) % 2, t // 2, t % 2, a]),
                                       x, i == 0, i == 2 * TT - 1)
                    done(last)
            for j in range(KD):
                done(project(open_tile("ga", j), s1, S1_GA + j * 8 * B, B, ks, hx))
            for j in range(KD):
                done(project(open_tile("gb", j), s1, S1_GB + j * 12 * B, B, ks, hx))
                o = open_tile("four_o", j)
                pe.wait_ge(lo_done, SPLITS["four", NF - 1] + 1)
                done(project(o, s1, S1_GB + j * 12 * B + 8 * B, B, range(NF), lambda k: (f_hi[:, k, :], f_lo[:, k, :])))
            for t in range(KT):
                o = open_tile("v", t)
                for k in range(KL):
                    tok = slice(t * P, t * P + P)
                    last = mm3(o, (ckv_hi[:, k, tok], ckv_lo[:, k, tok]), weights(s1, S1_V + k * T, T),
                               k == 0, k == KL - 1)
                done(last)

            def head_w(h):
                return S1_HEADS + (h // 4) * CH + (h % 4) * HEAD_W

            def prep_a(h):
                o = open_tile("uq", h)
                done(project(o[0:QK, :], s1, head_w(h), QK, range(QL), lambda k: (cq_hi[:, k, :], cq_lo[:, k, :])))
                for s in range(2):
                    o = open_tile("uk", h, s)
                    w = slice(0, T) if s == 0 else slice(T, TK)
                    done(project(o[0:NOPE, 0:TC if s else T], s1, head_w(h) + QL * QK, NOPE, range(KL),
                                 lambda k: (ckv_hi[:, k, w], ckv_lo[:, k, w])))

            def sums(h):
                o = open_tile("ssq_h", h)
                pe.wait_ge(qk_raw, 1 + 2 * h)
                columns(o, 0, sqq, TT, QK)
                pe.wait_ge(qk_raw, 2 + 2 * h)
                done(columns(o, TT, sqk, KT, QK, start=False))

            def prep_b(h):
                o = open_tile("rot_q", h)
                pe.wait_ge(qk_raw, 1 + 2 * h)
                done(mm(o[0:QK, :], rotm[NOPE:QK, :], qg[NOPE:QK, :], start=True, stop=True))
                o3 = open_tile("bc_q", h), open_tile("bc_k", h, 0), open_tile("bc_k", h, 1)
                wait_rcol()
                done(broadcast(o3[0], 0, TT, QK))
                done(broadcast(o3[1], TT, TT, QK))
                done(broadcast(o3[2], 2 * TT, 2, QK))

            prep_a(0)
            sums(0)
            prep_b(0)
            KH = TK // 2
            for h in range(H):
                pe.wait_ge(hi_done, SPLITS["k", h] + 1)
                for q in range(TT):
                    for s in range(2):
                        o = open_tile("mx", h, q, s)
                        done(mm(o[:, 0:KH], q_hi[0:QK, q * P:(q + 1) * P], k_hi[0:QK, s * KH:(s + 1) * KH],
                                start=True, stop=True))
                if h + 1 < H:
                    prep_a(h + 1)
                mod_b_tile(2 * h)
                o = open_tile("mx_row", h)
                pe.wait_ge(mx_done, h + 1)
                for q in range(TT):
                    last = nc.tensor.transpose(o[0:1, q * P:(q + 1) * P], mxq[:, q:q + 1], ident[:])
                done(last)

                def pv(k):
                    if k == 0 and h >= 2:
                        pe.wait_ge(o_raw, h - 1)
                    pe.wait_ge(freed_act, PLAN.freed_count(TILE["sT", h, k]))
                    va = v[:, k, h // 2, h % 2:h % 2 + 2, :].rearrange("p a b -> p (a b)")
                    return mm(psum[:, 6 + h % 2, :], va, probs[:, k % 3, :], start=k == 0, stop=k == KT - 1)

                if h == 0:
                    pe.wait_ge(v_done, 2)
                for k in range(KT):
                    o = open_tile("sT", h, k)
                    if k == 0:
                        pe.wait_ge(lo_done, SPLITS["k", h] + 1)
                        pe.wait_ge(freed_act, PLAN.freed_count(TILE["mx_row", h]))
                    tok = slice(k * P, k * P + P)
                    done(mm3(o, (k_hi[:, tok], k_lo[:, tok]), (q_hi[:], q_lo[:]), True, True))
                    if k == 1 and h + 1 < H:
                        sums(h + 1)
                    if k >= 2:
                        pv(k - 2)
                    if k == 3 and h + 1 < H:
                        prep_b(h + 1)
                mod_b_tile(2 * h + 1)
                pv(KT - 2)
                pv(KT - 1).then_inc(o_full, 1)

            att_x = lambda k: (att_hi[:, k, :], att_lo[:, k, :])
            project_two((open_tile("attn_o", 0), open_tile("attn_o", 1)),
                        lambda i, k: weights(SPLIT0["wo"], (i * 4 + k) * B, B), att_x, SPLITS["attn", 0], 4)
            for j in range(2, KD):
                done(project(open_tile("attn_o", j), SPLIT0["wo"], j * 4 * B, B, range(4), att_x))
            nsums = [0]

            def sum_squares(j, buf, first, last_one):
                nsums[0] += 1
                pe.wait_ge(sq_done, SQ0 + nsums[0])
                columns(psum[:, 7, :], 0, buf[:, j % 2, :], TT, start=first, stop=last_one).then_inc(sq_summed, 1)
                if last_one:
                    wait_rcol()
                    broadcast(psum[:, 6, :], 0, TT).then_inc(bc_full, 1)

            SQ0 = 2 + QL + 2 * KL
            merged_x = lambda k: (m_hi[:, k, :], m_lo[:, k, :])
            project_two((open_tile("merged", 0), open_tile("merged", 1)),
                        lambda i, k: weights(SPLIT0["w_out"], (i * 8 + k) * B, B), merged_x, SPLITS["m", 0])
            for j in range(1, KD):
                if j >= 2:
                    done(project(open_tile("merged", j), SPLIT0["w_out"], j * 8 * B, B, ks, merged_x))
                sum_squares(j - 1, sq, j == 1, False)
            sum_squares(KD - 1, sq, False, True)

            o = open_tile("logits")
            for k in range(KD):
                pe.wait_ge(h2_done, k + 1)
                for t in range(TT):
                    last = mm(o[:, t * NE:(t + 1) * NE], h2[:, k, t * P:(t + 1) * P], router[:, k, :],
                              start=k == 0 and t == 0, stop=k == KD - 1, skip_group_check=True)
            done(last)
            o = open_tile("aff_t")
            pe.wait_ge(aff_done, 1)
            for t in range(TT):
                last = nc.tensor.transpose(o[0:NE, t * P:(t + 1) * P], aff[:, t, :], ident[:])
            done(last)
            for t in range(TT):
                for half in range(2):
                    o = open_tile("h2_tok", t, half)
                    for k in range(4):
                        last = nc.tensor.transpose(o[:, k * P:(k + 1) * P], h2[:, half * 4 + k, t * P:(t + 1) * P],
                                                   ident[:])
                    done(last)
            o = open_tile("slots_tok")
            pe.wait_ge(slots_done, 1)
            for t in range(TT):
                last = nc.tensor.transpose(o[:, t * NE:(t + 1) * NE], slots[:, t * P:(t + 1) * P], ident[0:NE, 0:NE])
            done(last)
            pe.wait_ge(picks_done, TT)
            pe.wait_ge(tok_lo, 2 * TT)
            for k in range(KD):
                for half in range(2):
                    o = open_tile("xe", k, half)
                    for t in range(TT):
                        x = pick_tok[:, t, half * T:(half + 1) * T]
                        ch = slice(k * P, k * P + P)
                        mm(o, h2t_hi[:, t, ch], x, start=t == 0, stop=False)
                        last = mm(o, h2t_lo[:, t, ch], x, start=False, stop=t == TT - 1)
                    done(last)
            o = open_tile("gates")
            for i in range(PAIRS):
                for t in range(TT):
                    last = mm(o[:, i * NE:(i + 1) * NE], pick_tok[:, t, i * P:(i + 1) * P].bitcast(F32), aff[:, t, :],
                              start=t == 0, stop=t == TT - 1)
            done(last)
            pe.wait_ge(pick_in, 16)
            for i in range(PAIRS):
                o = open_tile("onehot", i)
                done(mm(o, pick[:, i * P:(i + 1) * P], slots[:], start=True, stop=True))

            def raw_wait(n, i):
                pe.wait_ge(raw_full[n % NRAW], i * (16 * 12 // NRAW) + 16 * (n // NRAW + 1))
                return raw[:, n % NRAW, :]

            def project_e(e, n, i, b, first=False):
                for k in range(KD):
                    if k % 4 == 0:
                        w = raw_wait(n + k // 4, i)
                    x = xe[:, k, (2 * i + e) * CAP:(2 * i + e + 1) * CAP]
                    last = mm(psum[0:CAP, b, :], x, w[:, (k % 4) * T:(k % 4 + 1) * T], start=k == 0, stop=k == KD - 1)
                    if k == 0 and not first or k == 4:
                        last.then_inc(raw_used, 1)
                done(last)

            def transposes(i, e):
                pe.wait_ge(act_done, 2 * i + e + 1)
                if 2 * i + e >= 1:
                    pe.wait_ge(act_t_done, 2 * i + e)
                for k in range(FE):
                    last = nc.tensor.transpose(psum[:, 6, k * CAP:(k + 1) * CAP], act_r[:, k * P:(k + 1) * P],
                                               ident[0:CAP, 0:CAP])
                done(last)

            def down(e, n, i):
                rows = slice((e % 2) * CAP, (e % 2 + 1) * CAP)
                pe.wait_ge(act_t_done, i * 2 + e + 1)
                for half in range(2):
                    if 2 * i + e >= 1:
                        pe.wait_ge(lo_done, i * 4 + ye0 + 2 * e - 1 + half)
                    w = raw_wait(n + half, i)
                    for k in range(FE):
                        last = mm(psum[rows, 4 + half, :], act_e[:, e % 2, k * CAP:(k + 1) * CAP],
                                  w[:, k * T:(k + 1) * T], start=k == 0, stop=k == FE - 1)
                        if k == 0:
                            last.then_inc(raw_used, 1)
                    done(last)

            n0 = RAW0["experts"]
            ye0 = SPLITS["ye", 0, 0]
            pe.wait_ge(freed_act, PLAN.freed_count(TILE["xe", KD - 1, 1]))
            pe.wait_ge(freed_dve, PLAN.freed_count(TILE["onehot", PAIRS - 1]))
            project_e(0, n0, 0, 0, first=True)
            project_e(0, n0 + 2, 0, 2)
            for i in range(PAIRS):
                project_e(1, n0 + 4, i, 1)
                transposes(i, 0)
                project_e(1, n0 + 6, i, 3)
                down(0, n0 + 8, i)
                if i < PAIRS - 1:
                    project_e(2, n0 + 10, i, 0)
                    transposes(i, 1)
                    project_e(2, n0 + 12, i, 2)
                    down(1, n0 + 14, i)
                else:
                    transposes(i, 1)
                    down(1, n0 + 10, i)

            for j in range(KD):
                o = open_tile("combine", j)
                ch = slice(j * P, j * P + P)
                for i in range(PAIRS):
                    if j == 0 and i == 0:
                        pe.wait_ge(lo_done, SPLITS["ye", NE - 3, 1] + 1)
                    if j == 0 and i == PAIRS - 1:
                        pe.wait_ge(lo_done, SPLITS["ye", NE - 1, 1] + 1)
                    ins = mm(o, ye_hi[:, i, ch], place[:, i, :], start=i == 0, stop=False)
                    if j == 0 and i == 0:
                        ins.then_inc(raw_used, 1)
                    last = mm(o, ye_lo[:, i, ch], place[:, i, :], start=False, stop=i == PAIRS - 1)
                done(last)
                if j >= 1:
                    sum_squares(j - 1, sq, j == 1, False)
            sum_squares(KD - 1, sq, False, True)

            w2 = SPLIT0["w_in_2"]

            def gates(j):
                for g, name in enumerate(("lru_r", "lru_i")):
                    o = open_tile(name, j)
                    if g == 0:
                        pe.wait_ge(conv_done, j + 1)
                    done(mm(o, wab[:, g, j, :], conv_u[:, j % 3, :], start=True, stop=True))

            project_two((open_tile("lru_x", 0), open_tile("lru_x", 1)),
                        lambda i, k: weights(w2, (i * KD + k) * B, B), hx, SPLITS["g", 0])
            for j in range(2, LRU):
                done(project(open_tile("lru_x", j), w2, j * 8 * B, B, ks, hx))
                if j == 2:
                    pe.wait_ge(wab_in, 16)
                gates(j - 2)
            for j in range(SC):
                for i, name in enumerate(("sc_c", "sc_x", "sc_b")):
                    done(project(open_tile(name, j), w2, (LRU + 3 * j + i) * 8 * B, B, ks, hx))
                    if i == 0 and j == 0:
                        gates(LRU - 2)
                        gates(LRU - 1)
            for j in range(LRU):
                done(project(open_tile("lru_gate", j), w2, (LRU + 3 * SC + j) * 8 * B, B, ks, hx))
            mix_x = lambda k: (ysc_hi[:, k, :], ysc_lo[:, k, :]) if k < SC else \
                (ylru_hi[:, k - SC, :], ylru_lo[:, k - SC, :])
            project_two((open_tile("mix_o", 0), open_tile("mix_o", 1)),
                        lambda i, k: weights(SPLIT0["w_out_2"], (i * 12 + k) * B, B), mix_x,
                        [SPLITS["y_sc", k] if k < SC else SPLITS["y_lru", k - SC] for k in range(SC + LRU)], SC + LRU)
            for j in range(1, KD):
                if j >= 2:
                    done(project(open_tile("mix_o", j), SPLIT0["w_out_2"], j * 12 * B, B, range(12), mix_x))
                sum_squares(j - 1, sq, j == 1, False)
            sum_squares(KD - 1, sq, False, True)

            ffc = SPLIT0["ffn"]

            def bank_free(q, t):
                t -= 5
                if t < 0:
                    pe.wait_ge(resid_done, q * KD + 3 * KD + t + KD + 1)
                elif t < 2 * FQ:
                    pe.wait_ge((accg_done, accu_done)[t % 2], q * FQ + t // 2 + 1)
                else:
                    pe.wait_ge(resid_done, q * KD + 4 * KD + t - 2 * FQ + 1)

            def quarter(q):
                got = [0]

                def ww(off):
                    c, o = off // CH, off % CH
                    if c + 1 > got[0]:
                        pe.wait_ge(w_lo_done, q * FFN_CHUNKS + ffc + c + 1)
                        got[0] = c + 1
                    return w_hi[:, (ffc + c) % NHL, o:o + B], w_lo[:, (ffc + c) % NHL, o:o + B]

                bank_free(q, 0)
                bank_free(q, 1)
                project_two((psum[:, 0, :], psum[:, 1, :]), lambda i, k: ww((i * KD + k) * B), hx, SPLITS["g2", 0])
                for t in range(2, FFN_TILES):
                    if t == 2 * FQ:
                        bank_free(q, t)
                        bank_free(q, t + 1)
                        for k in range(FQ):
                            pe.wait_ge(lo_done, q * FQ + SPLITS["ff", 0, k] + 1)
                            for i in range(2):
                                last = mm3(psum[:, (t + i) % 5, :], ww((2 * FQ * KD + i * FQ + k) * B),
                                           (ff_hi[:, k, :], ff_lo[:, k, :]), k == 0, k == FQ - 1)
                                if k == FQ - 1:
                                    done(last)
                        continue
                    if t == 2 * FQ + 1:
                        continue
                    bank_free(q, t)
                    o = psum[:, t % 5, :]
                    if t < 2 * FQ:
                        for k in range(KD):
                            last = mm3(o, ww((t * KD + k) * B), hx(k), k == 0, k == KD - 1)
                    else:
                        j = t - 2 * FQ
                        for k in range(FQ):
                            last = mm3(o, ww((2 * FQ * KD + j * FQ + k) * B), (ff_hi[:, k, :], ff_lo[:, k, :]),
                                       k == 0, k == FQ - 1)
                    done(last)

            with pe.Fori(0, QUARTERS - 1) as q:
                quarter(q)
            quarter(QUARTERS - 1)
            for j in range(KD):
                sum_squares(j, sq_last, j == 0, j == KD - 1)

        @block.scalar
        def _(act):
            A = nc.scalar.activation

            nsplit = [0]

            def split_weights(t):
                while nsplit[0] < NSPLIT and SPLIT_DUE[nsplit[0]] <= t:
                    c = nsplit[0]
                    n = RAW_OF_SPLIT[c]
                    if SPLIT_DUE[c]:
                        act.wait_ge(tile_full, SPLIT_DUE[c])
                    act.wait_ge(raw_full[n % NRAW], 16 * (n // NRAW + 1))
                    A(w_hi[:, c % NHL, :], raw[:, n % NRAW, :], ACT.Copy).then_inc(w_hi_done, 1)
                    nsplit[0] += 1

            def take(*name):
                split_weights(TILE[name])
                full(act, *name)
                return bank(*name)

            def hi(dst, src, **kw):
                A(dst, src, ACT.Identity if "bias" in kw else ACT.Copy, **kw).then_inc(hi_done, 1)

            pres = [0]

            def hi_of_pre(dst, src, **kw):
                pres[0] += 1
                act.wait_ge(pre_done, pres[0])
                hi(dst, src, **kw)

            act.wait_ge(cols_in, 16)
            A(csil, col("cond", 0, 16), ACT.Silu).then_inc(silu_done, 1)
            act.wait_ge(x_in, 32)
            A(sq_x0[:], x0[:], ACT.Square).then_inc(sq_done, 1)
            A(sq_c0[:], c0[:], ACT.Square).then_inc(sq_done, 1)
            act.wait_ge(consts_in, 16 * 6)
            A(dftc_hi[:], dftc[:], ACT.Copy).then_inc(act_seq, 1)
            for g in range(4):
                split_weights(TILE["mod", g])
            for j in range(KD):
                hi_of_pre(h_hi[:, j, :], pre[:, j % 2, :], bias=mod[:, j, 0:1])
            for j in range(KD):
                hi_of_pre(hc_hi[:, j, :], pre[:, j % 2, 0:TC], bias=mod[:, j, 1:2])

            def square(dst, src):
                A(dst, src, ACT.Square).then_inc(sq_done, 1)

            for j in range(QL):
                square(sq_q[:, j, :], take("cq", j))
            for j in range(KL):
                square(sq_kv[:, j, 0:T], take("ckv", j, 0))
                square(sq_kv[:, j, T:TK], take("ckv", j, 1)[:, 0:TC])
            A(sqk[NOPE:QK, 0:T], take("kpe", 0)[0:ROPE, :], ACT.Square).then_inc(act_seq, 1)
            A(sqk[NOPE:QK, T:TK], take("kpe", 1)[0:ROPE, 0:TC], ACT.Square).then_inc(act_seq, 1)
            hi(f_hi[:, 0, :], take("f", 0))
            hi(f_hi[:, 1, :], take("f", 1))
            for j in range(QL):
                hi_of_pre(cq_hi[:, j, :], cqg[:, j, :])
            for j in range(KL):
                hi_of_pre(ckv_hi[:, j, :], ckvg[:, j, :])
            hi(f_hi[:, 2, :], take("f", 2))
            hi(f_hi[:, 3, :], take("f", 3))
            for g in range(NF + 1):
                if g < NF:
                    for half in range(2):
                        o = take("f_ch", g, half)
                        if g == 0:
                            act.wait_ge(lo_done, SPLITS["ckv", KL - 1] + 1)
                        if g >= 2:
                            full(act, "four", g - 2)
                        hi(fc_hi[:, g % 2, half, :, :], o.rearrange("p (t c) -> p t c", t=2))
                if g >= 1:
                    hi(f_hi[:, g - 1, :], take("four", g - 1))
            full(act, "four", NF - 1)
            for j in range(KD):
                A(ga[:, j, :], take("ga", j), ACT.Sigmoid).then_inc(freed_act, 1)
            for j in range(KD):
                o = take("gb", j)
                if j >= 2:
                    act.wait_ge(resid_done, j - 1)
                A(sg[j % 2][:], o, ACT.Sigmoid).then_inc(freed_act, 1)
                split_weights(TILE["four_o", j])
            for t in range(KT):
                A(v[:, t, :, 0:3:2, :], take("v", t).rearrange("p (g s d) -> p g s d", g=H // 2, s=2), ACT.Copy).then_inc(freed_act, 1)

            def prep_a(h):
                o = take("uq", h)
                if h >= 1:
                    act.wait_ge(pre_done, PRE_Q + 2 * h)
                    full(act, "bc_k", h - 1, 1)
                A(sqq[:], o[0:QK, :], ACT.Square)
                A(qg[:], o[0:QK, :], ACT.Copy, scale=cols[0:QK, COLS["q_norm_g"]:COLS["q_norm_g"] + 1]).then_inc(qk_raw, 1)
                for s in range(2):
                    o = take("uk", h, s)[0:NOPE, 0:TC if s else T]
                    w = slice(0, T) if s == 0 else slice(T, TK)
                    A(sqk[0:NOPE, w], o, ACT.Square)
                    last = A(kraw[0:NOPE, w], o, ACT.Copy, scale=cols[0:NOPE, COLS["k_norm_g"]:COLS["k_norm_g"] + 1])
                last.then_inc(qk_raw, 1)

            def round_qk(h):
                split_weights(TILE["bc_k", h, 1])
                if h >= 1:
                    full(act, "sT", h - 1, KT - 1)
                hi_of_pre(q_hi[0:QK, :], rq[:])
                hi_of_pre(k_hi[0:QK, :], rk[:])

            def output(h):
                act.wait_ge(o_full, h + 1)
                r0 = (h % 2) * VD
                A(att[r0:r0 + VD, h // 2, :], psum[r0:r0 + VD, 6 + h % 2, :], ACT.Copy)
                if h >= 2:
                    act.wait_ge(att_done, h // 2)
                A(rs[r0:r0 + VD, :], psum[VD - r0:2 * VD - r0, 6 + h % 2, :], ACT.Copy).then_inc(o_raw, 1)

            act.wait_ge(resid_done, KD)
            prep_a(0)
            round_qk(0)
            for h in range(H):
                if h + 1 < H:
                    prep_a(h + 1)
                split_weights(TILE["mod_b", 2 * h])
                A(q_hi[QK:QK + 1, :], take("mx_row", h)[0:1, :], ACT.Copy, scale=-1.0).then_inc(freed_act, 1)
                for k in range(KT):
                    A(probs[:, k % 3, :], take("sT", h, k), ACT.Exp, scale=QK ** -0.5).then_inc(freed_act, 1)
                    if k == 1 and h >= 1:
                        output(h - 1)
                if h + 1 < H:
                    round_qk(h + 1)
            for j in range(3):
                act.wait_ge(att_done, j + 1)
                hi(att_hi[:, j, :], att[:, j, :])
            output(H - 1)

            act.dma_start(x1[:], x_d).then_inc(x_again, 16)
            act.wait_ge(att_done, 4)
            hi(att_hi[:, 3, :], att[:, 3, :])
            for j in range(KD):
                split_weights(TILE["attn_o", j])
                if j >= 1:
                    hi_of_pre(m_hi[:, j - 1, :], m_tmp[:, (j - 1) % 2, :])
            hi_of_pre(m_hi[:, KD - 1, :], m_tmp[:, (KD - 1) % 2, :])

            nsq = [0]

            def residual_squares(names, buf, base):
                for j in range(KD):
                    if names is not None:
                        split_weights(TILE[names, j])
                    act.wait_ge(resid_done, base + j + 1)
                    if nsq[0] >= 2:
                        act.wait_ge(sq_summed, nsq[0] - 1)
                    nsq[0] += 1
                    A(buf[:, j % 2, :], x1[:, j, :], ACT.Square).then_inc(sq_done, 1)
                if names is not None:
                    split_weights(TILE[names, KD - 1] + 1)

            residual_squares("merged", sq, KD)

            for j in range(KD):
                act.wait_ge(h2_pre, j + 1)
                A(h2[:, j, :], h2[:, j, :], ACT.Identity, bias=mod[:, 3 * KD + j, 0:1]).then_inc(h2_done, 1)
            full(act, "logits")
            act.wait_ge(logit_max, 1)
            A(aff[:], aff[:], ACT.Exp).then_inc(aff_exp, 1)
            for t in range(TT):
                for half in range(2):
                    o = take("h2_tok", t, half)
                    w = slice(half * T, half * T + T)
                    A(h2t[:, t, w], o, ACT.Copy)
                    A(h2t_hi[:, t, w], o, ACT.Copy).then_inc(freed_act, 1)
                    act.wait_ge(freed_act, PLAN.freed_count(TILE["h2_tok", t, half]))
                    act.sem_inc(tok_done, 1)
            act.wait_ge(slots_done, 1)
            act.dma_start(pick[:], pick_d).then_inc(pick_in, 16)
            for k in range(KD):
                for half in range(2):
                    A(xe[:, k, half * T:(half + 1) * T], take("xe", k, half), ACT.Copy).then_inc(freed_act, 1)
            def ye_round(e, i):
                rows = slice((e % 2) * CAP, (e % 2 + 1) * CAP)
                for half in range(2):
                    act.wait_ge(tile_full, i * 10 + (TILE["ye", e, half] + 1) - last_shift(e, i))
                    dst = ye_hi[rows, i, half * T:(half + 1) * T] if isinstance(i, int) else \
                        ye_hi[rows, bass.ds(i, 1), half * T:(half + 1) * T].rearrange("p a c -> p (a c)")
                    hi(dst, psum[rows, 4 + half, :],
                       scale=gcol[rows, i:i + 1] if isinstance(i, int) else gcol[rows, bass.ds(i, 1)])

            def last_shift(e, i):
                return 2 if isinstance(i, int) and 2 * i + e == NE - 1 else 0

            def silu(e, i):
                act.wait_ge(tile_full, i * 10 + (TILE["gate_e", e] + 1))
                act.wait_ge(act_done, i * 2 + e)
                A(gate_s[:], psum[0:CAP, e % 2, :], ACT.Silu).then_inc(silu_e, 1)

            nc.scalar.preload_act_table(ACT.Silu)
            act.wait_ge(freed_dve, PLAN.freed_count(TILE["gates"]))
            full(act, "gate_e", 0)
            A(gate_s[:], psum[0:CAP, 0, :], ACT.Silu).then_inc(silu_e, 1)

            def pair(i, last_pair):
                silu(1, i)
                ye_round(0, i)
                if not last_pair:
                    silu(2, i)
                ye_round(1, i)

            with act.Fori(0, PAIRS - 1) as i:
                pair(i, False)
            pair(PAIRS - 1, True)
            act.dma_start(wab[:], wab_d).then_inc(wab_in, 16)
            residual_squares("combine", sq, 2 * KD)

            for j in range(KD):
                hi_of_pre(h_hi[:, j, :], g_pre[:, j % 2, :])

            def lru_gates(j):
                A(lru_a[:, j, :], take("lru_r", j), ACT.Sigmoid, bias=col("lru_ba_2", j)).then_inc(freed_act, 1)
                if j >= 1:
                    act.wait_ge(lru_b_done, j)
                A(e_i[:], take("lru_i", j), ACT.Sigmoid, bias=col("lru_bx_2", j)).then_inc(freed_act, 1)
                act.wait_ge(freed_act, PLAN.freed_count(TILE["lru_r", j]))
                A(lru_v[:, j, :], lru_a[:, j, :], ACT.Tanh, scale=c8[:, j:j + 1]).then_inc(av_done, 1)

            def lru_decay():
                for j in range(LRU):
                    A(lru_a[:, j, :], lru_a[:, j, :], ACT.Exp, scale=nc8[:, j:j + 1]).then_inc(act_seq, 1)
                    act.wait_ge(act_seq, 4 + j + 1)
                    if j >= 2:
                        act.wait_ge(v_ready, j - 1)
                    A(a_sq[:, j % 2, :], lru_a[:, j, :], ACT.Square).then_inc(a_sq_done, 1)
                act.wait_ge(v_ready, LRU)
                for j in range(LRU):
                    A(lru_v[:, j, :], lru_v[:, j, :], ACT.Sqrt).then_inc(mult_done, 1)

            act.wait_ge(sp_done, 1)
            A(sp_z, sp_z, ACT.Exp, scale=-1.0).then_inc(act_seq, 1)
            for j in range(LRU):
                split_weights(TILE["lru_x", j])
                if j >= 2:
                    lru_gates(j - 2)
            for j in range(SC):
                o = take("sc_c", j)
                if j >= 1:
                    full(act, "sc_x", j - 1)
                    act.wait_ge(freed_dve, PLAN.freed_count(TILE["sc_x", j - 1]))
                else:
                    full(act, "lru_i", LRU - 1)
                A(sc_c[:], o, ACT.Copy).then_inc(freed_act, 1)
                if j == 0:
                    lru_gates(LRU - 2)
                    lru_gates(LRU - 1)
                split_weights(TILE["sc_x", j])
                split_weights(TILE["sc_b", j])
                act.wait_ge(pre_done, PRE_SC + j + 1)
                hi(ysc_hi[:, j, :], sc_y[:])
                if j == 0:
                    lru_decay()
            for j in range(LRU):
                o = take("lru_gate", j)
                if j >= 2:
                    act.wait_ge(pre_done, PRE_SC + SC + j - 1)
                else:
                    act.wait_ge(lo_done, SPLITS["y_sc", SC - 1] + 1)
                A(gl[:, j % 2, :], o, ACT.Gelu_apprx_tanh).then_inc(freed_act, 1)
                if j >= 1:
                    act.wait_ge(pre_done, PRE_SC + SC + j)
                    hi(ylru_hi[:, j - 1, :], y_pre[:, (j - 1) % 2, :])
            act.wait_ge(pre_done, PRE_SC + SC + LRU)
            hi(ylru_hi[:, LRU - 1, :], y_pre[:, (LRU - 1) % 2, :])
            pres[0] = PRE_SC + SC + LRU
            residual_squares("mix_o", sq, 3 * KD)

            for j in range(KD):
                hi_of_pre(h_hi[:, j, :], ff_pre[:, j % 2, :])
            nc.scalar.preload_act_table(ACT.Gelu_apprx_tanh)
            cw = COLS["ffn_conv_w_2"]
            pf = PRE_FF
            assert pres[0] == pf
            for q in range(QUARTERS):
                for i in range(FQ):
                    g = q * FQ + i
                    for half, name, acc in ((0, "ff_g", acc_g), (1, "ff_u", acc_u)):
                        o = take(name, q, i)
                        wcol = cols[:, cw + half * 3 * FF + 2 * FF + g:cw + half * 3 * FF + 2 * FF + g + 1]
                        if g >= 2:
                            act.wait_ge(pre_done, pf + g - 1)
                        A(acc[:, g % 2, :], o, ACT.Copy, scale=wcol).then_inc(acc_done, 1)
                    act.wait_ge(accg_done, g + 1)
                    A(ff_gl[:, g % 2, :], acc_g[:, g % 2, :], ACT.Gelu_apprx_tanh).then_inc(glu_done, 1)
                    act.wait_ge(pre_done, pf + g + 1)
                    if i == 0 and q >= 1:
                        full(act, "ff_o", q - 1, KD - 1)
                    hi(ff_hi[:, i, :], ff_pre[:, g % 2, :])
                for j in range(KD):
                    split_weights(TILE["ff_o", q, j])
            residual_squares(None, sq_last, 7 * KD)
            for j in range(KD):
                act.wait_ge(y_done, 1 + j)
                act.dma_start(out[:, j, :], y_out[:, j, :]).then_inc(out_done, 16)

        @block.vector
        def _(dve):
            V = nc.vector
            n = [0]

            def link(ins):
                n[0] += 1
                ins.then_inc(dve_seq, 1)
                dve.wait_ge(dve_seq, n[0])

            def pre_(ins):
                ins.then_inc(pre_done, 1)

            def lo(dst, src, hi_part, *name):
                dve.wait_ge(hi_done, SPLITS[name] + 1)
                return V.tensor_tensor(dst, src, hi_part.bitcast(F32), ALU.subtract)

            def take(*name):
                full(dve, *name)
                return bank(*name)

            def free(ins):
                ins.then_inc(freed_dve, 1)

            V.memset(eps, EPS).then_inc(z_done, 1)

            def mod_evac(g):
                b = cols[:, COLS["b_mod"] + 4 * g:COLS["b_mod"] + 4 * g + 4].unsqueeze(2).to_broadcast([P, 4, 2])
                free(V.tensor_tensor(mod[:, 4 * g:4 * g + 4, :], take("mod", g)[:, 0:8].rearrange("p (m c) -> p m c", c=2),
                                     b, ALU.add))
                dve.wait_ge(freed_dve, PLAN.freed_count(TILE["mod", g]))

            def mod_b_evac(k):
                m = 16 + 2 * k
                V.tensor_tensor(mod[:, m:m + 2, 0], take("mod_b", k)[:, 0:2], col("b_mod", m, 2), ALU.add)\
                    .then_inc(modb_done, 1)

            def inverse_norms(src, n, groups, sem_):
                for a, m, scale in groups:
                    ins = V.tensor_scalar(nv[:, a:a + m], src[:, a:a + m], scale, EPS, ALU.mult, ALU.add)
                    if (a, m, scale) == groups[-1]:
                        if sem_ is None:
                            link(ins)
                        else:
                            free(ins)
                            dve.wait_ge(freed_dve, sem_)
                v_, y, t = nv[:, 0:n], ny[:, 0:n], nt[:, 0:n]
                link(V.tensor_scalar(y.bitcast(I32), v_.bitcast(I32), 1, None, ALU.logical_shift_right))
                link(V.tensor_scalar(y.bitcast(I32), y.bitcast(I32), -1.0, float(0x5F3759DF), ALU.mult, ALU.add))
                for i in range(3):
                    link(V.tensor_tensor(t, y, y, ALU.mult))
                    link(V.scalar_tensor_tensor(out=t, in0=t, scalar=-0.5, in1=v_, op0=ALU.mult, op1=ALU.mult))
                    if i < 2:
                        link(V.scalar_tensor_tensor(out=y, in0=t, scalar=1.5, in1=y, op0=ALU.add, op1=ALU.mult))
                V.scalar_tensor_tensor(out=rcol[:, 0:n], in0=t, scalar=1.5, in1=y, op0=ALU.add, op1=ALU.mult)\
                    .then_inc(rcol_done, 1)

            def modulation_x(c):
                dve.wait_ge(raw_full[c % NRAW], 16 * (c // NRAW + 1))
                for k in range(KD):
                    w, s = raw[:, c % NRAW, (KD + k) * B:(KD + k + 1) * B], csil[:, 2 * k:2 * k + 1]
                    if k == 0:
                        ins = V.tensor_scalar(macc_x[:, c, :], w, s, None, ALU.mult)
                    else:
                        ins = V.scalar_tensor_tensor(out=macc_x[:, c, :], in0=w, scalar=s, in1=macc_x[:, c, :],
                                                     op0=ALU.mult, op1=ALU.add)
                    if k < KD - 1:
                        link(ins)
                ins.then_inc(macc_x_done, 1)

            dve.wait_ge(silu_done, 1)
            for c in range(8):
                if c == 6:
                    for which, (src, dst) in enumerate(((sq_x0, sum_x), (sq_c0, sum_c))):
                        dve.wait_ge(sq_done, which + 1)
                        V.tensor_reduce(dst[:], src[:].rearrange("p k t -> p t k"), AX.X, ALU.add).then_inc(sum_done, 1)
                if c % 2 == 0 and c >= 2:
                    mod_evac(c // 2 - 1)
                modulation_x(c)
            inverse_norms(take("ssq_xc"), 6, [(0, 6, 1.0 / D)], PLAN.freed_count(TILE["ssq_xc"]))
            mod_evac(3)
            dve.wait_ge(act_seq, 1)
            link(V.tensor_tensor(dftc_lo[:], dftc[:], dftc_hi[:].bitcast(F32), ALU.subtract))
            for i, a in ((0, a1), (1, a1c)):
                link(V.scalar_tensor_tensor(out=a, in0=mod[:, KD:2 * KD, i], scalar=1.0, in1=col("norm1_g", 0, KD),
                                            op0=ALU.add, op1=ALU.mult))

            def norm(count, pre_of, mk_pre, mk_lo):
                for j in range(count + 1):
                    if j < count:
                        pre_(mk_pre(j))
                    if j >= 1:
                        mk_lo(j - 1).then_inc(lo_done, 1)

            def mk0(src, a, r, w):
                def f(j):
                    if j >= 2:
                        dve.wait_ge(lo_done, SPLITS[w, j - 2] + 1)
                    elif w == "hc":
                        dve.wait_ge(lo_done, SPLITS["h", KD - 2 + j] + 1)
                    return V.scalar_tensor_tensor(out=pre[:, j % 2, 0:src.shape[2]], in0=src[:, j, :], scalar=a[:, j:j + 1],
                                                  in1=r, op0=ALU.mult, op1=ALU.mult)
                return f

            def lo0(dst, hi_t, i, w, width):
                def f(j):
                    dve.wait_ge(hi_done, SPLITS[w, j] + 1)
                    return V.scalar_tensor_tensor(out=dst[:, j, :], in0=pre[:, j % 2, 0:width], scalar=mod[:, j, i:i + 1],
                                                  in1=hi_t[:, j, :].bitcast(F32), op0=ALU.add, op1=ALU.subtract)
                return f

            norm(KD, None, mk0(x0, a1, take("bc_x"), "h"), lo0(h_lo, h_hi, 0, "h", T))
            norm(KD, None, mk0(c0, a1c, take("bc_c")[:, 0:TC], "hc"), lo0(hc_lo, hc_hi, 1, "hc", TC))

            nsq = 2
            for j in range(QL):
                o = take("cq", j)
                nsq += 1
                dve.wait_ge(sq_done, nsq)
                free(V.tensor_scalar(cqg[:, j, :], o, col("q_a_norm_g", j), None, ALU.mult))
            for j in range(KL):
                for s in range(2):
                    o = take("ckv", j, s)
                    nsq += 1
                    dve.wait_ge(sq_done, nsq)
                    w = slice(0, T) if s == 0 else slice(T, TK)
                    free(V.tensor_scalar(ckvg[:, j, w], o[:, 0:TC if s else T], col("kv_a_norm_g", j), None, ALU.mult))
            for s in range(2):
                o = take("kpe", s)
                dve.wait_ge(act_seq, 2 + s)
                w = slice(0, T) if s == 0 else slice(T, TK)
                free(V.tensor_scalar(kraw[NOPE:QK, w], o[0:ROPE, 0:TC if s else T],
                                     cols[NOPE:QK, COLS["k_norm_g"]:COLS["k_norm_g"] + 1], None, ALU.mult))
            dve.wait_ge(freed_dve, PLAN.freed_count(TILE["kpe", 1]))

            def evac_lo(dst, hi_part, *name):
                o = take(*name)
                dve.wait_ge(hi_done, SPLITS[name] + 1)
                V.tensor_tensor(dst, o, hi_part.bitcast(F32), ALU.subtract).then_inc(lo_done, 1)

            evac_lo(f_lo[:, 0, :], f_hi[:, 0, :], "f", 0)
            inverse_norms(take("ssq_c"), 10, [(0, 4, 1.0 / (QL * P)), (4, 6, 1.0 / (KL * P))],
                          PLAN.freed_count(TILE["ssq_c"]))
            evac_lo(f_lo[:, 1, :], f_hi[:, 1, :], "f", 1)
            r = take("bc_cq")
            norm(QL, None, lambda j: V.tensor_tensor(cqg[:, j, :], cqg[:, j, :], r, ALU.mult),
                 lambda j: lo(cq_lo[:, j, :], cqg[:, j, :], cq_hi[:, j, :], "cq", j))
            r0, r1 = take("bc_ckv", 0), take("bc_ckv", 1)[:, 0:TC]

            def ckv_pre(j):
                V.tensor_tensor(ckvg[:, j, 0:T], ckvg[:, j, 0:T], r0, ALU.mult)
                return V.tensor_tensor(ckvg[:, j, T:TK], ckvg[:, j, T:TK], r1, ALU.mult)

            norm(KL, None, ckv_pre, lambda j: lo(ckv_lo[:, j, :], ckvg[:, j, :], ckv_hi[:, j, :], "ckv", j))
            o = take("rot_k")
            link(V.tensor_tensor(rk[NOPE:QK, 0:T], o[NOPE:QK, :], rope_cs[NOPE:QK, 1, :], ALU.mult))
            link(V.tensor_tensor(kraw[NOPE:QK, 0:T], kraw[NOPE:QK, 0:T], rope_cs[NOPE:QK, 0, :], ALU.mult))
            free(V.tensor_tensor(kraw[NOPE:QK, 0:T], kraw[NOPE:QK, 0:T], rk[NOPE:QK, 0:T], ALU.add))
            evac_lo(f_lo[:, 2, :], f_hi[:, 2, :], "f", 2)
            evac_lo(f_lo[:, 3, :], f_hi[:, 3, :], "f", 3)
            for g in range(NF + 1):
                if g < NF:
                    for half in range(2):
                        o = take("f_ch", g, half)
                        dve.wait_ge(hi_done, SPLITS["f_ch", g, half] + 1)
                        V.tensor_tensor(fc_lo[:, g % 2, half, :, :], o.rearrange("p (t c) -> p t c", t=2),
                                        fc_hi[:, g % 2, half, :, :].bitcast(F32), ALU.subtract).then_inc(lo_done, 1)
                if g >= 1:
                    evac_lo(f_lo[:, g - 1, :], f_hi[:, g - 1, :], "four", g - 1)
            for j in range(KD):
                o = take("four_o", j)
                dve.wait_ge(freed_act, PLAN.freed_count(TILE["gb", j]))
                V.tensor_tensor(gbf[:, j, :], o, sg[j % 2][:], ALU.mult).then_inc(resid_done, 1)
            full(dve, "four_o", KD - 1)
            V.memset(v[:, :, :, 1, :], 1.0).then_inc(v_done, 1)
            V.memset(k_hi[QK:QK + 1, :].bitcast(F32), 1.0)
            V.memset(k_lo[QK:QK + 1, :].bitcast(F32), 0.0)
            V.memset(q_lo[QK:QK + 1, :].bitcast(F32), 0.0).then_inc(v_done, 1)

            def final(h):
                o = take("rot_q", h)
                free(V.tensor_tensor(tmp_a[NOPE:QK, :], o[NOPE:QK, :], rope_cs[NOPE:QK, 1, :], ALU.mult))
                link(V.tensor_tensor(qg[NOPE:QK, :], qg[NOPE:QK, :], rope_cs[NOPE:QK, 0, :], ALU.mult))
                dve.wait_ge(freed_dve, PLAN.freed_count(TILE["rot_q", h]))
                link(V.tensor_tensor(qg[NOPE:QK, :], qg[NOPE:QK, :], tmp_a[NOPE:QK, :], ALU.add))
                pre_(V.tensor_tensor(rq[:], qg[:], take("bc_q", h)[0:QK, :], ALU.mult))
                V.tensor_tensor(rk[:, 0:T], kraw[:, 0:T], take("bc_k", h, 0)[0:QK, :], ALU.mult)
                pre_(V.tensor_tensor(rk[:, T:TK], kraw[:, T:TK], take("bc_k", h, 1)[0:QK, 0:TC], ALU.mult))
                lo(q_lo[0:QK, :], rq[:], q_hi[0:QK, :], "q", h).then_inc(lo_done, 1)
                lo(k_lo[0:QK, :], rk[:], k_hi[0:QK, :], "k", h).then_inc(lo_done, 1)

            def norms(h):
                inverse_norms(take("ssq_h", h), 10, [(0, 10, 1.0 / QK)], PLAN.freed_count(TILE["ssq_h", h]))

            def pair_output(j):
                dve.wait_ge(o_raw, 2 * j + 2)
                link(V.reciprocal(rs[:], rs[:]))
                V.tensor_tensor(att[:, j, :], att[:, j, :], rs[:], ALU.mult).then_inc(att_done, 1)

            norms(0)
            final(0)
            KH = TK // 2
            for h in range(H):
                for q in range(TT):
                    for s in range(2):
                        o = take("mx", h, q, s)
                        free(V.tensor_reduce(mx2[:, 2 * q + s:2 * q + s + 1], o[:, 0:KH], AX.X, ALU.max))
                dve.wait_ge(freed_dve, PLAN.freed_count(TILE["mx", h, TT - 1, 1]))
                V.tensor_reduce(mxq, mx2.rearrange("p (q s) -> p q s", s=2), AX.X, ALU.max).then_inc(mx_done, 1)
                mod_b_evac(2 * h)
                if h + 1 < H:
                    norms(h + 1)
                if h >= 2 and h % 2 == 0:
                    pair_output(h // 2 - 1)
                if h + 1 < H:
                    final(h + 1)
                mod_b_evac(2 * h + 1)
            for j in range(3):
                lo(att_lo[:, j, :], att[:, j, :], att_hi[:, j, :], "attn", j).then_inc(lo_done, 1)
            pair_output(H // 2 - 1)

            lo(att_lo[:, 3, :], att[:, 3, :], att_hi[:, 3, :], "attn", 3).then_inc(lo_done, 1)
            link(V.scalar_tensor_tensor(out=a2, in0=mod[:, 4 * KD:5 * KD, 0], scalar=1.0, in1=col("norm2_g", 0, KD),
                                        op0=ALU.add, op1=ALU.mult))
            for j in range(KD + 1):
                if j < KD:
                    o = take("attn_o", j)
                    if j >= 2:
                        dve.wait_ge(lo_done, SPLITS["m", j - 2] + 1)
                    free(V.tensor_tensor(m_tmp[:, j % 2, :], o, ga[:, j, :], ALU.mult))
                    dve.wait_ge(freed_dve, PLAN.freed_count(TILE["attn_o", j]))
                    pre_(V.tensor_tensor(m_tmp[:, j % 2, :], m_tmp[:, j % 2, :], gbf[:, j, :], ALU.add))
                if j >= 1:
                    lo(m_lo[:, j - 1, :], m_tmp[:, (j - 1) % 2, :], m_hi[:, j - 1, :], "m", j - 1).then_inc(lo_done, 1)

            def residual(j, name, base, scale=None):
                o = take(*name)
                if scale is None:
                    ins = V.tensor_tensor(x1[:, j, :], o, x1[:, j, :], ALU.add)
                else:
                    ins = V.scalar_tensor_tensor(out=x1[:, j, :], in0=o, scalar=scale, in1=x1[:, j, :],
                                                 op0=ALU.mult, op1=ALU.add)
                ins.then_inc(resid_done, 1)

            nrms = [0]

            def inverse():
                nrms[0] += 1
                dve.wait_ge(sq_summed, nrms[0] * KD)
                inverse_norms(psum[:, 7, :], TT, [(0, TT, 1.0 / D)], None)
                dve.wait_ge(bc_full, nrms[0])
                return psum[:, 6, :]

            dve.wait_ge(x_again, 16)
            for j in range(KD):
                residual(j, ("merged", j), KD, mod[:, 2 * KD + j, 0:1])
            rstd = inverse()

            for j in range(KD):
                V.scalar_tensor_tensor(out=h2[:, j, :], in0=x1[:, j, :], scalar=a2[:, j:j + 1], in1=rstd,
                                       op0=ALU.mult, op1=ALU.mult).then_inc(h2_pre, 1)
            lg = take("logits")[:, 0:TT * NE].rearrange("p (t e) -> p t e", t=TT)
            link(V.tensor_reduce(aff_m[:], lg, AX.X, ALU.max))
            V.tensor_tensor(aff[:], lg, aff_m[:].unsqueeze(2).to_broadcast([P, TT, NE]), ALU.subtract).then_inc(logit_max, 1)
            dve.wait_ge(aff_exp, 1)
            link(V.tensor_reduce(aff_s[:], aff[:], AX.X, ALU.add))
            link(V.reciprocal(aff_s[:], aff_s[:]))
            V.tensor_tensor(aff[:], aff[:], aff_s[:].unsqueeze(2).to_broadcast([P, TT, NE]), ALU.mult).then_inc(aff_done, 1)
            o = take("aff_t")
            link(V.tensor_copy(aff_t[:], o[0:NE, :]))
            free(V.tensor_copy(work[:], o[0:NE, :]))
            dve.wait_ge(freed_dve, PLAN.freed_count(TILE["aff_t"]))
            for r in range(CAP // 8):
                link(V.max(top8[:], work[:]))
                link(V.match_replace(out=work[:], in_to_replace=top8[:], in_values=work[:], imm_value=-1.0))
            link(V.tensor_scalar(chosen[:], work[:], 0.0, None, ALU.is_lt))
            link(V.memset(ones_row[:], 1.0))
            link(V.tensor_tensor_scan(slots[:], ones_row[:], chosen[:], 0.0, ALU.mult, ALU.add))
            link(V.tensor_tensor(slots[:], slots[:], chosen[:], ALU.mult))
            V.tensor_scalar(slots[:], slots[:], -1.0, None, ALU.add).then_inc(slots_done, 1)
            free(V.tensor_copy(slots_tok[:], take("slots_tok")[:, 0:TT * NE].rearrange("p (t e) -> p t e", t=TT)))
            dve.wait_ge(freed_dve, PLAN.freed_count(TILE["slots_tok"]))
            for t in range(TT):
                V.tensor_tensor(pick_tok[:, t, :].rearrange("p (e c) -> p e c", e=NE),
                                slots_tok[:, t, :].unsqueeze(2).to_broadcast([P, NE, CAP]),
                                iota[:].unsqueeze(1).to_broadcast([P, NE, CAP]), ALU.is_equal).then_inc(picks_done, 1)
            o = take("gates")
            link(V.tensor_copy(gcol[0:CAP, :], o[0:CAP, 0:PAIRS * NE:NE + 2]))
            free(V.tensor_copy(gcol[CAP:P, :], o[CAP:P, 1:PAIRS * NE:NE + 2]))
            dve.wait_ge(freed_dve, PLAN.freed_count(TILE["gates"]))
            for i in range(PAIRS):
                free(V.tensor_scalar(place[:, i, :], take("onehot", i), col("slot"), None, ALU.is_equal))
            sp0 = SPLITS["ye", 0, 0]

            def expert_act(e, i):
                dve.wait_ge(tile_full, i * 10 + (TILE["up_e", e] + 1))
                dve.wait_ge(silu_e, i * 2 + (e + 1))
                V.tensor_tensor(act_r[:], psum[0:CAP, 2 + e % 2, :], gate_s[:], ALU.mult).then_inc(act_done, 1)

            def copy_t(e, i):
                last = isinstance(i, int) and 2 * i + e == NE - 1
                dve.wait_ge(tile_full, i * 10 + (TILE["act_t", e] + 1) - (1 if last else 0))
                V.tensor_copy(act_e[:, e % 2, :], psum[:, 6, 0:FE * CAP]).then_inc(act_t_done, 1)

            def ye_lo_part(e, i):
                rows = slice((e % 2) * CAP, (e % 2 + 1) * CAP)
                for half in range(2):
                    dve.wait_ge(hi_done, i * 4 + (sp0 + 2 * e + half + 1))
                    if isinstance(i, int):
                        hi_t, dst = (z[rows, i, half * T:(half + 1) * T] for z in (ye_hi, ye_lo))
                        g = gcol[rows, i:i + 1]
                    else:
                        hi_t, dst = (z[rows, bass.ds(i, 1), half * T:(half + 1) * T].rearrange("p a c -> p (a c)")
                                     for z in (ye_hi, ye_lo))
                        g = gcol[rows, bass.ds(i, 1)]
                    V.scalar_tensor_tensor(out=dst, in0=psum[rows, 4 + half, :], scalar=g, in1=hi_t.bitcast(F32),
                                           op0=ALU.mult, op1=ALU.subtract).then_inc(lo_done, 1)

            expert_act(0, 0)

            def pair(i, last_pair):
                copy_t(0, i)
                expert_act(1, i)
                ye_lo_part(0, i)
                copy_t(1, i)
                if not last_pair:
                    expert_act(2, i)
                ye_lo_part(1, i)

            with dve.Fori(0, PAIRS - 1) as i:
                pair(i, False)
            pair(PAIRS - 1, True)
            for j in range(KD):
                residual(j, ("combine", j), 2 * KD, mod[:, 5 * KD + j, 0:1])

            lam = col("lru_lambda_2", 0, LRU)
            link(V.tensor_scalar(sp_s, lam, -1.0, None, ALU.mult))
            V.tensor_tensor(sp_z, lam, sp_s, ALU.max).then_inc(sp_done, 1)

            rstd = inverse()

            def gain(src, dst, g, name):
                def f(j):
                    if j >= 2:
                        dve.wait_ge(lo_done, SPLITS[name, j - 2] + 1)
                    return V.scalar_tensor_tensor(out=dst[:, j % 2, :], in0=src[:, j, :], scalar=col(g, j), in1=rstd,
                                                  op0=ALU.mult, op1=ALU.mult)
                return f

            norm(KD, None, gain(x1, g_pre, "norm1_g_2", "g"),
                 lambda j: lo(h_lo[:, j, :], g_pre[:, j % 2, :], h_hi[:, j, :], "g", j))

            dve.wait_ge(act_seq, 4)
            link(V.tensor_scalar(sp_s2, sp_z, 2.0, None, ALU.add))
            link(V.reciprocal(sp_s2, sp_s2))
            link(V.tensor_tensor(sp_z, sp_z, sp_s2, ALU.mult))
            link(V.tensor_tensor(sp_s2, sp_z, sp_z, ALU.mult))
            link(V.memset(sp_p, 1.0 / 19))
            for k in range(17, 0, -2):
                link(V.tensor_tensor(sp_p, sp_p, sp_s2, ALU.mult))
                link(V.tensor_scalar(sp_p, sp_p, 1.0 / k, None, ALU.add))
            link(V.tensor_tensor(sp_p, sp_p, sp_z, ALU.mult))
            link(V.tensor_scalar(sp_s, sp_s, 0.0, None, ALU.max))
            link(V.scalar_tensor_tensor(out=sp_p, in0=sp_p, scalar=2.0, in1=sp_s, op0=ALU.mult, op1=ALU.add))
            link(V.tensor_scalar(c8, sp_p, 8.0, None, ALU.mult))
            link(V.tensor_scalar(nc8, sp_p, -8.0, None, ALU.mult))

            def lru_conv(j):
                o = take("lru_x", j)
                if j >= 3:
                    full(dve, "lru_i", j - 3)
                    dve.wait_ge(lru_b_done, j - 2)
                u = conv_u[:, j % 3, :]
                tap = lambda k: col("lru_conv_w_2", k * LRU + j)
                link(V.tensor_scalar(u, o, tap(3), col("lru_conv_b_2", j), ALU.mult, ALU.add))
                for k in (2, 1):
                    s = 3 - k
                    link(V.scalar_tensor_tensor(out=u[:, s:T], in0=o[:, 0:T - s], scalar=tap(k), in1=u[:, s:T],
                                                op0=ALU.mult, op1=ALU.add))
                V.scalar_tensor_tensor(out=u[:, 3:T], in0=o[:, 0:T - 3], scalar=tap(0), in1=u[:, 3:T],
                                       op0=ALU.mult, op1=ALU.add).then_inc(conv_done, 1)

            def lru_gates(j):
                dve.wait_ge(freed_act, PLAN.freed_count(TILE["lru_i", j]))
                V.tensor_tensor(lru_b[:, j, :], e_i[:], conv_u[:, j % 3, :], ALU.mult).then_inc(lru_b_done, 1)

            def lru_decay(j):
                dve.wait_ge(a_sq_done, j + 1)
                V.scalar_tensor_tensor(out=lru_v[:, j, :], in0=a_sq[:, j % 2, :], scalar=1.0, in1=lru_v[:, j, :],
                                       op0=ALU.add, op1=ALU.mult).then_inc(v_ready, 1)

            for j in range(LRU):
                lru_conv(j)
                if j >= 2:
                    lru_gates(j - 2)
            for j in range(SC):
                if j == 0:
                    lru_gates(LRU - 2)
                    lru_gates(LRU - 1)
                o = take("sc_x", j)
                dve.wait_ge(freed_act, PLAN.freed_count(TILE["sc_c", j]))
                free(V.tensor_tensor(sc_cx[:], o, sc_c[:], ALU.mult))
                dve.wait_ge(freed_dve, PLAN.freed_count(TILE["sc_x", j]))
                tap = lambda k: col("sc_conv_w_2", k * SC + j)
                link(V.tensor_scalar(sc_acc[:], sc_cx[:], tap(2), None, ALU.mult))
                for k in (1, 0):
                    s = 2 - k
                    link(V.scalar_tensor_tensor(out=sc_acc[:, s:T], in0=sc_cx[:, 0:T - s], scalar=tap(k),
                                                in1=sc_acc[:, s:T], op0=ALU.mult, op1=ALU.add))
                o = take("sc_b", j)
                pre_(V.tensor_tensor(sc_y[:], o, sc_acc[:], ALU.mult))
                lo(ysc_lo[:, j, :], sc_y[:], ysc_hi[:, j, :], "y_sc", j).then_inc(lo_done, 1)
                dve.wait_ge(lo_done, SPLITS["y_sc", j] + 1)
                if j == 0:
                    for i in range(LRU):
                        lru_decay(i)
            for j in range(LRU):
                dve.wait_ge(mult_done, j + 1)
                link(V.tensor_tensor(lru_b[:, j, :], lru_b[:, j, :], lru_v[:, j, :], ALU.mult))
                link(V.tensor_tensor_scan(lru_v[:, j, :], lru_a[:, j, :], lru_b[:, j, :], 0.0, ALU.mult, ALU.add))
            for j in range(LRU + 1):
                if j < LRU:
                    dve.wait_ge(freed_act, PLAN.freed_count(TILE["lru_gate", j]))
                    if j >= 2:
                        dve.wait_ge(lo_done, SPLITS["y_lru", j - 2] + 1)
                    pre_(V.tensor_tensor(y_pre[:, j % 2, :], lru_v[:, j, :], gl[:, j % 2, :], ALU.mult))
                if j >= 1:
                    lo(ylru_lo[:, j - 1, :], y_pre[:, (j - 1) % 2, :], ylru_hi[:, j - 1, :], "y_lru", j - 1)\
                        .then_inc(lo_done, 1)
            for j in range(KD):
                residual(j, ("mix_o", j), 3 * KD)
            rstd = inverse()
            norm(KD, None, gain(x1, ff_pre, "norm2_g_2", "g2"),
                 lambda j: lo(h_lo[:, j, :], ff_pre[:, j % 2, :], h_hi[:, j, :], "g2", j))

            cw = COLS["ffn_conv_w_2"]
            for q in range(QUARTERS):
                for i in range(FQ + 1):
                    if i < FQ:
                        g = q * FQ + i
                        for half, name, acc in ((0, "ff_g", acc_g), (1, "ff_u", acc_u)):
                            tap = lambda k: cols[:, cw + half * 3 * FF + k * FF + g:cw + half * 3 * FF + k * FF + g + 1]
                            o = take(name, q, i)
                            dve.wait_ge(acc_done, 2 * g + half + 1)
                            a = acc[:, g % 2, :]
                            link(V.scalar_tensor_tensor(out=a[:, 1:T], in0=o[:, 0:T - 1], scalar=tap(1), in1=a[:, 1:T],
                                                        op0=ALU.mult, op1=ALU.add))
                            done_sem = (accg_done, accu_done)[half]
                            V.scalar_tensor_tensor(out=a[:, 2:T], in0=o[:, 0:T - 2], scalar=tap(0), in1=a[:, 2:T],
                                                   op0=ALU.mult, op1=ALU.add).then_inc(done_sem, 1)
                        dve.wait_ge(accu_done, g + 1)
                        dve.wait_ge(glu_done, g + 1)
                        if g >= 2:
                            p = SPLITS["ff", (g - 2) // FQ, (g - 2) % FQ]
                            dve.wait_ge(lo_done, p + 1)
                        pre_(V.tensor_tensor(ff_pre[:, g % 2, :], acc_u[:, g % 2, :], ff_gl[:, g % 2, :], ALU.mult))
                    if i >= 1:
                        g = q * FQ + i - 1
                        lo(ff_lo[:, i - 1, :], ff_pre[:, g % 2, :], ff_hi[:, i - 1, :], "ff", q, i - 1).then_inc(lo_done, 1)
                for j in range(KD):
                    residual(j, ("ff_o", q, j), (4 + q) * KD)
            rstd = inverse()
            for j in range(KD):
                V.scalar_tensor_tensor(out=y_out[:, j, :], in0=x1[:, j, :], scalar=col("final_g_2", j), in1=rstd,
                                       op0=ALU.mult, op1=ALU.mult).then_inc(y_done, 1)


def kernel(**inputs):
    import numpy as np
    import concourse.bacc as bacc
    from concourse.bass_utils import run_bass_kernel_spmd as run

    a = {k: np.ascontiguousarray(v) for k, v in inputs.items()}
    f = np.float32

    def tiles(w, m=B):
        k, n = w.shape
        return w.reshape(k // P, P, n // m, m).transpose(1, 2, 0, 3).reshape(P, -1)

    def rows(w):
        return w.reshape(-1, P, w.shape[1]).transpose(1, 0, 2).reshape(P, -1)

    def pad(parts, total):
        out = np.zeros((P, total), f)
        for off, p in parts:
            out[:, off:off + p.shape[1]] = p
        return out

    tt = np.arange(T)
    ang = 2 * np.pi * ((tt[:, None] * tt[None, :]) % T) / T
    norm = 1.0 / np.sqrt(T * P)
    dft = np.concatenate([rows(np.cos(ang).astype(f)), rows((-np.sin(ang)).astype(f))], axis=1)
    cc = np.arange(P)
    angc = 2 * np.pi * ((cc[:, None] * cc[None, :]) % P) / P
    dftc = np.concatenate([np.cos(angc) * norm, np.sin(angc) * norm], axis=1).astype(f)
    nfreq = ROPE // 4
    inv = (1.0 / (f(10000.0) ** (np.arange(nfreq, dtype=f) / f(nfreq)))).astype(f)
    rope = np.zeros((ROPE, 2, T), f)
    for axis, pos in enumerate((tt // 64, tt % 64)):
        an = (pos.astype(f)[:, None] * inv[None, :]).astype(f)
        an = np.concatenate([an, an], axis=1).T
        rope[axis * 16:axis * 16 + 16, 0] = np.cos(an)
        rope[axis * 16:axis * 16 + 16, 1] = np.sin(an)
    rot = np.zeros((QK, QK), f)
    for b0 in (NOPE, NOPE + 16):
        for i in range(8):
            rot[b0 + 8 + i, b0 + i] = -1.0
            rot[b0 + i, b0 + 8 + i] = 1.0
    pick = np.zeros((NE, PAIRS * P), f)
    for e in range(NE):
        pick[e, (e // 2) * P + (e % 2) * CAP:(e // 2) * P + (e % 2 + 1) * CAP] = 1.0
    iota = np.broadcast_to(np.arange(CAP, dtype=f), (P, CAP))

    w_mod = a["w_mod"][0]
    mod = tiles(w_mod)
    w_in = a["w_in"][0]
    offs = np.cumsum([0, 384, 256, 32, 512, 1024, 1024])
    wq, wkv, wkpe, wf, wga, wgb = (w_in[:, offs[i]:offs[i + 1]] for i in range(6))
    wqu, wkvu = a["w_q_up"][0], a["w_kv_up"][0].reshape(256, H, NOPE + VD)
    gb, wfo = tiles(wgb).reshape(P, KD, 8 * B), tiles(a["w_fourier"][0]).reshape(P, KD, 4 * B)
    parts = [(S1_QKV, tiles(wq)), (S1_QKV + QL * 8 * B, tiles(wkv)), (S1_KPE, rows(wkpe)), (S1_F, tiles(wf)),
             (S1_DFT, dft), (S1_GA, tiles(wga)), (S1_GB, np.concatenate([gb, wfo], axis=2).reshape(P, -1)),
             (S1_V, rows(wkvu[:, :, NOPE:].reshape(256, H * VD)))]
    for h in range(H):
        o = S1_HEADS + (h // 4) * CH + (h % 4) * HEAD_W
        parts.append((o, rows(wqu[:, h * QK:(h + 1) * QK])))
        parts.append((o + QL * QK, rows(wkvu[:, h, :NOPE])))
    s1 = pad(parts, 20 * CH)
    wg, wu, wd = a["w_e_gate"][0], a["w_e_up"][0], a["w_e_down"][0]

    def gate_up(e):
        return [rows(wg[e]), rows(wu[e])]

    def down(e):
        return [rows(wd[e][:, :T]), rows(wd[e][:, T:])]

    ex = gate_up(0)
    for e in range(NE):
        if e + 1 < NE:
            ex += gate_up(e + 1)
        ex += down(e)
    w2 = a["w_in_2"][0]
    cols2 = [w2[:, :1024]]
    for j in range(SC):
        cols2 += [w2[:, 2560 + j * P:2560 + (j + 1) * P], w2[:, 3072 + j * P:3072 + (j + 1) * P],
                  w2[:, 2048 + j * P:2048 + (j + 1) * P]]
    cols2.append(w2[:, 1024:2048])
    w2s = tiles(np.concatenate(cols2, axis=1))
    wo2 = a["w_out_2"][0]
    wo2 = tiles(np.concatenate([wo2[1024:], wo2[:1024]], axis=0))
    wup, wdn = a["w_up_2"][0], a["w_down_2"][0]
    up_g, up_u = (tiles(w).reshape(P, FF, 8 * B) for w in (wup[:, :3072], wup[:, 3072:]))
    ff = []
    for q in range(QUARTERS):
        for i in range(FQ):
            ff += [up_g[:, q * FQ + i], up_u[:, q * FQ + i]]
        ff.append(tiles(wdn[q * FQ * P:(q + 1) * FQ * P]))
    stream = np.concatenate([mod[:, :8 * CH], s1, mod[:, 8 * CH:], tiles(a["w_o_attn"][0]), tiles(a["w_out"][0])]
                            + ex + [w2s, wo2] + ff, axis=1)
    stream = np.ascontiguousarray(stream.reshape(P, -1, CH).transpose(1, 0, 2))
    assert stream.shape[0] == len(CHUNKS), (stream.shape, len(CHUNKS))

    cols = np.zeros((P, NCOLS), f)

    def put(name, vec):
        v2 = vec.reshape(-1, P).T
        cols[:, COLS[name]:COLS[name] + v2.shape[1]] = v2

    for name in ("norm1_g", "b_mod", "q_a_norm_g", "kv_a_norm_g", "norm2_g", "norm1_g_2", "lru_conv_w_2",
                 "lru_conv_b_2", "lru_ba_2", "lru_bx_2", "lru_lambda_2", "sc_conv_w_2", "norm2_g_2", "final_g_2"):
        put(name, a[name])
    put("ffn_conv_w_2", a["ffn_conv_w_2"][0].reshape(3, 2, 3072).transpose(1, 0, 2))
    cols[:QK, COLS["q_norm_g"]] = a["q_norm_g"][0]
    cols[:QK, COLS["k_norm_g"]] = a["k_norm_g"][0]
    cond = np.stack([a["c"][0].reshape(KD, P), a["c_ctx"].reshape(KD, P)], axis=1)
    cols[:, COLS["cond"]:COLS["cond"] + 16] = cond.reshape(16, P).T
    cols[:, COLS["slot"]] = np.arange(P) % CAP
    wab = np.zeros((P, 2, LRU, P), f)
    for g, name in enumerate(("lru_wa_2", "lru_wx_2")):
        w = a[name][0].reshape(LRU, 2, 64, 64)
        for s in range(2):
            wab[s * 64:(s + 1) * 64, g, :, s * 64:(s + 1) * 64] = w[:, s].transpose(1, 0, 2)

    def chan(x):
        return np.ascontiguousarray(x.T.reshape(KD, P, -1).transpose(1, 0, 2))

    arrays = {"stream": stream, "cols": cols, "x": chan(a["x"][0]), "ctx": chan(a["ctx"][0]),
              "router": np.ascontiguousarray(a["w_router"][0].reshape(KD, P, NE).transpose(1, 0, 2)), "wab": wab,
              "rope": rope, "rot": rot, "dftc": dftc, "ident": np.eye(P, dtype=f),
              "iota": np.ascontiguousarray(iota), "pick": pick}
    nc = bacc.Bacc("TRN2", target_bir_lowering=False, num_devices=1)
    aps = [nc.dram_tensor(f"in_{k}", v.shape, F32, kind="ExternalInput").ap() for k, v in arrays.items()]
    out = nc.dram_tensor("out", (P, KD, T), F32, kind="ExternalOutput").ap()
    build(nc, *aps, out)
    r = run(nc, [{f"in_{k}": v for k, v in arrays.items()}], core_ids=[0])
    y = r.results[0]["out"]
    return y.transpose(2, 1, 0).reshape(1, T, D)
```
